# Optimizing a Trainium2 kernel written in Bass

```python
import jax, jax.numpy as jnp
from jax import lax
import numpy as np

D_MODEL = 1024
BATCH = 1
SEQ = 512
DEPTH = 2

GRID_W = 64
CTX_LEN = 256
D_MIX = D_MODEL
N_GROUPS_MIX = 4
GROUP_W = D_MIX // N_GROUPS_MIX
D_FF = 4 * D_MODEL
NORM_EPS = 1e-6
GN_EPS = 1e-5
CONV_K = 31
CONV_NORM_GROUPS = 4
RW_HEAD = 64
RW_HEADS = GROUP_W // RW_HEAD
RW_DECAY_LORA = 64
RW_A_LORA = 64
RW_GATE_LORA = 128
RW_LNX_EPS = 64e-5
POOL_WINDOWS = (2, 4, 8, 16)
POOL_CH = GROUP_W // len(POOL_WINDOWS)
MLA_HEADS = 4
MLA_NOPE = 64
MLA_ROPE = 32
MLA_V = 64
MLA_Q_RANK = 256
MLA_KV_RANK = 128
ROPE_BASE = 10000.0
Q_BLOCK = 128
N_CONV_IN = 2 * GROUP_W
N_POOL_IN = GROUP_W
N_Q_IN = MLA_Q_RANK
N_RW_IN = 3 * GROUP_W + RW_GATE_LORA + 2 * RW_DECAY_LORA + 2 * RW_A_LORA
N_KV_IN = MLA_KV_RANK + MLA_ROPE
OFF_POOL = N_CONV_IN
OFF_Q = OFF_POOL + N_POOL_IN
OFF_RW = OFF_Q + N_Q_IN
OFF_KV = OFF_RW + N_RW_IN
P_IN = OFF_KV + N_KV_IN
RW_R = 0
RW_K = GROUP_W
RW_V = 2 * GROUP_W
RW_G = 3 * GROUP_W
RW_W = RW_G + RW_GATE_LORA
RW_A = RW_W + 2 * RW_DECAY_LORA

kernel_name = "hybrid_parallel_mixer_prefix_dit"

def rms_norm(x, g, eps=NORM_EPS):
    xf = x.astype(jnp.float32)
    y = xf * lax.rsqrt(jnp.mean(xf * xf, axis=-1, keepdims=True) + eps)
    return (y * g.astype(jnp.float32)).astype(x.dtype)

def group_norm(x, n_groups, g, b, eps):
    shp = x.shape
    xf = x.astype(jnp.float32).reshape(*shp[:-1], n_groups, shp[-1] // n_groups)
    mu = jnp.mean(xf, axis=-1, keepdims=True)
    var = jnp.mean(jnp.square(xf - mu), axis=-1, keepdims=True)
    y = ((xf - mu) * lax.rsqrt(var + eps)).reshape(shp)
    return (y * g.astype(jnp.float32) + b.astype(jnp.float32)).astype(x.dtype)

def conv_module(p, dw, db, gn_g, gn_b, pw):
    u = p[..., :GROUP_W] * jax.nn.sigmoid(p[..., GROUP_W:])
    y = lax.conv_general_dilated(u, dw[:, None, :].astype(u.dtype), window_strides=(1,),
                                 padding=[(CONV_K // 2, CONV_K // 2)],
                                 dimension_numbers=("NWC", "WIO", "NWC"),
                                 feature_group_count=GROUP_W)
    y = jax.nn.silu(group_norm(y + db.astype(y.dtype), CONV_NORM_GROUPS, gn_g, gn_b, GN_EPS))
    return y @ pw.astype(y.dtype)

def multiscale_pool(p, pool_w, pool_scale):
    b, n, _ = p.shape
    u = p.astype(jnp.float32).reshape(b, n, len(POOL_WINDOWS), POOL_CH)
    cs = jnp.concatenate([jnp.zeros_like(u[:, :1]), jnp.cumsum(u, axis=1)], axis=1)
    t = jnp.arange(n)
    means = []
    for gi, w in enumerate(POOL_WINDOWS):
        lo = jnp.clip(t - w // 2, 0, n)
        hi = jnp.clip(t + w - w // 2, 0, n)
        cnt = (hi - lo).astype(jnp.float32)
        means.append((cs[:, hi, gi] - cs[:, lo, gi]) / cnt[None, :, None])
    d = jnp.stack(means, axis=2) - u
    y = jnp.einsum("bngc,gcd->bngd", d, pool_w.astype(jnp.float32)).reshape(b, n, GROUP_W)
    return (y * pool_scale.astype(jnp.float32)).astype(p.dtype)

def shift_mix(p, mu_prev, mu_next):
    prev = jnp.pad(p[:, :-1], ((0, 0), (1, 0), (0, 0)))
    nxt = jnp.pad(p[:, 1:], ((0, 0), (0, 1), (0, 0)))
    return p + mu_prev * (prev - p) + mu_next * (nxt - p)

def wkv7_scan(r, dec, k, v, kk, b):
    bsz, _, h, dh = r.shape
    xs = tuple(jnp.moveaxis(t, 1, 0) for t in (r, dec, k, v, kk, b))

    def step(S, inp):
        r_t, d_t, k_t, v_t, kk_t, b_t = inp
        sa = jnp.einsum("bhvk,bhk->bhv", S, kk_t)
        S = S * d_t[:, :, None, :] - sa[..., None] * b_t[:, :, None, :] + v_t[..., None] * k_t[:, :, None, :]
        return S, jnp.einsum("bhvk,bhk->bhv", S, r_t)

    _, ys = lax.scan(step, jnp.zeros((bsz, h, dh, dh), jnp.float32), xs)
    return jnp.moveaxis(ys, 0, 1)

def rwkv7_bidirectional(pl, pc, mu_prev, mu_next, w0, w2, a0, a2, g2, k_k, k_a, r_k, lnx_g, lnx_b, with_ctx):
    n_ctx = pc.shape[1]
    z = jnp.concatenate([shift_mix(pc, mu_prev, mu_next), shift_mix(pl, mu_prev, mu_next)],
                        axis=1).astype(jnp.float32)
    bsz, n, _ = z.shape

    def heads(t):
        return t.reshape(bsz, t.shape[1], RW_HEADS, RW_HEAD)

    def seg_flip(t):
        return jnp.concatenate([t[:, :n_ctx][:, ::-1], t[:, n_ctx:][:, ::-1]], axis=1)

    r = heads(z[..., RW_R:RW_K])
    k = z[..., RW_K:RW_V]
    v = heads(z[..., RW_V:RW_G])
    kk = heads(k * k_k)
    kk = kk / jnp.maximum(jnp.sqrt(jnp.sum(kk * kk, axis=-1, keepdims=True)), 1e-12)
    sel = slice(0, n) if with_ctx else slice(n_ctx, n)
    wkv, bonus = [], []
    for d in range(2):
        wl = z[..., RW_W + d * RW_DECAY_LORA: RW_W + (d + 1) * RW_DECAY_LORA]
        al = z[..., RW_A + d * RW_A_LORA: RW_A + (d + 1) * RW_A_LORA]
        log_w = -jax.nn.softplus(-(w0[d] + jnp.tanh(wl) @ w2[d])) - 0.5
        dec = heads(jnp.exp(-jnp.exp(log_w)))
        a = jax.nn.sigmoid(a0[d] + al @ a2[d])
        kd = heads(k * (1.0 + (a - 1.0) * k_a))
        ins = (r, dec, kd, v, kk, kk * heads(a))
        if d == 0:
            wkv.append(wkv7_scan(*ins))
        else:
            wkv.append(seg_flip(wkv7_scan(*[seg_flip(t) for t in ins])))
        bonus.append(jnp.sum(r[:, sel] * kd[:, sel] * r_k, axis=-1, keepdims=True) * v[:, sel])
    o = group_norm((wkv[0] + wkv[1])[:, sel].reshape(bsz, -1, GROUP_W), RW_HEADS, lnx_g, lnx_b, RW_LNX_EPS)
    gate = jax.nn.sigmoid(z[:, sel, RW_G:RW_W]) @ g2
    o = ((o + (bonus[0] + bonus[1]).reshape(bsz, -1, GROUP_W)) * gate).astype(pl.dtype)
    if with_ctx:
        return o[:, n_ctx:], o[:, :n_ctx]
    return o, None

def axial_angles(n):
    rows = n // GRID_W
    row = jnp.repeat(jnp.arange(rows), GRID_W).astype(jnp.float32)
    col = jnp.tile(jnp.arange(GRID_W), rows).astype(jnp.float32)
    n_freq = MLA_ROPE // 4
    freq = ROPE_BASE ** (-jnp.arange(n_freq, dtype=jnp.float32) / n_freq)
    return jnp.stack([row[:, None] * freq, col[:, None] * freq], axis=1)

def rope_2d(x, ang):
    xs = x.astype(jnp.float32).reshape(*x.shape[:-1], 2, 2, MLA_ROPE // 4)
    x1, x2 = xs[..., 0, :], xs[..., 1, :]
    cos, sin = jnp.cos(ang), jnp.sin(ang)
    y = jnp.stack([x1 * cos - x2 * sin, x1 * sin + x2 * cos], axis=-2)
    return y.reshape(x.shape).astype(x.dtype)

def mla_keys_values(pkv, kvn_g, wukv, ang):
    b, n, _ = pkv.shape
    c_kv = rms_norm(pkv[..., :MLA_KV_RANK], kvn_g)
    kv = (c_kv @ wukv.astype(c_kv.dtype)).reshape(b, n, MLA_HEADS, MLA_NOPE + MLA_V)
    k_rope = pkv[..., MLA_KV_RANK:]
    if ang is not None:
        k_rope = rope_2d(k_rope, ang)
    k = jnp.concatenate([kv[..., :MLA_NOPE],
                         jnp.broadcast_to(k_rope[:, :, None, :], (b, n, MLA_HEADS, MLA_ROPE))], axis=-1)
    return k, kv[..., MLA_NOPE:]

def mla_queries(pq, qn_g, wuq, ang):
    b, n, _ = pq.shape
    q = (rms_norm(pq, qn_g) @ wuq.astype(pq.dtype)).reshape(b, n, MLA_HEADS, MLA_NOPE + MLA_ROPE)
    q_rope = q[..., MLA_NOPE:]
    if ang is not None:
        q_rope = rope_2d(q_rope, ang[:, None])
    return jnp.concatenate([q[..., :MLA_NOPE], q_rope], axis=-1)

def block_attention(q, k, v):
    b, n, h, dq = q.shape
    nb = n // Q_BLOCK
    qb = jnp.moveaxis(q.reshape(b, nb, Q_BLOCK, h, dq), 1, 0)
    scale = dq ** -0.5

    def one_block(qi):
        s = jnp.einsum("bqhd,bkhd->bhqk", qi, k).astype(jnp.float32) * scale
        pr = jax.nn.softmax(s, axis=-1).astype(v.dtype)
        return jnp.einsum("bhqk,bkhd->bqhd", pr, v)

    o = lax.map(one_block, qb)
    return jnp.moveaxis(o, 0, 1).reshape(b, n, h * v.shape[-1])

def sq_relu_mlp(h, w1, w2):
    return jnp.square(jax.nn.relu(h @ w1)) @ w2

def setup_inputs(seed: int = 0) -> dict:
    key = jax.random.key(seed)
    ks = iter(jax.random.split(key, 40))

    def nrm(shape, s):
        return jax.random.normal(next(ks), shape, jnp.float32) * s

    def gain(shape):
        return 1.0 + nrm(shape, 0.1)

    L, D, G = DEPTH, D_MODEL, GROUP_W
    return {
        "x": nrm((BATCH, SEQ, D), 1.0),
        "c": nrm((BATCH, D), 1.0),
        "ctx": nrm((BATCH, CTX_LEN, D), 1.0),
        "c_ctx": nrm((D,), 1.0),
        "ada_w": nrm((L, D, 6 * D), D ** -0.5),
        "ada_b": nrm((L, 6 * D), 0.02),
        "norm1_g": gain((L, D)),
        "norm2_g": gain((L, D)),
        "w_in": nrm((L, D, P_IN), D ** -0.5),
        "w_out": nrm((L, D_MIX, D), D_MIX ** -0.5),
        "conv_dw": nrm((L, CONV_K, G), CONV_K ** -0.5),
        "conv_db": nrm((L, G), 0.01),
        "conv_gn_g": gain((L, G)),
        "conv_gn_b": nrm((L, G), 0.01),
        "conv_pw": nrm((L, G, G), G ** -0.5),
        "pool_w": nrm((L, len(POOL_WINDOWS), POOL_CH, POOL_CH), POOL_CH ** -0.5),
        "pool_scale": gain((L, G)),
        "rw_mu_prev": jax.random.uniform(next(ks), (L, N_RW_IN), jnp.float32, 0.0, 0.5),
        "rw_mu_next": jax.random.uniform(next(ks), (L, N_RW_IN), jnp.float32, 0.0, 0.5),
        "rw_w0": nrm((L, 2, G), 0.5),
        "rw_w2": nrm((L, 2, RW_DECAY_LORA, G), 0.5 * RW_DECAY_LORA ** -0.5),
        "rw_a0": nrm((L, 2, G), 0.1),
        "rw_a2": nrm((L, 2, RW_A_LORA, G), 0.5 * RW_A_LORA ** -0.5),
        "rw_g2": nrm((L, RW_GATE_LORA, G), RW_GATE_LORA ** -0.5),
        "rw_kk": gain((L, G)),
        "rw_ka": gain((L, G)),
        "rw_rk": nrm((L, RW_HEADS, RW_HEAD), 0.1),
        "rw_lnx_g": gain((L, G)),
        "rw_lnx_b": nrm((L, G), 0.01),
        "mla_qn_g": gain((L, MLA_Q_RANK)),
        "mla_wuq": nrm((L, MLA_Q_RANK, MLA_HEADS * (MLA_NOPE + MLA_ROPE)), MLA_Q_RANK ** -0.5),
        "mla_kvn_g": gain((L, MLA_KV_RANK)),
        "mla_wukv": nrm((L, MLA_KV_RANK, MLA_HEADS * (MLA_NOPE + MLA_V)), MLA_KV_RANK ** -0.5),
        "mlp_w1": nrm((L, D, D_FF), D ** -0.5),
        "mlp_w2": nrm((L, D_FF, D), D_FF ** -0.5),
        "final_g": gain((D,)),
    }

def reference(x, c, ctx, c_ctx, ada_w, ada_b, norm1_g, norm2_g, w_in, w_out, conv_dw, conv_db, conv_gn_g,
              conv_gn_b, conv_pw, pool_w, pool_scale, rw_mu_prev, rw_mu_next, rw_w0, rw_w2, rw_a0, rw_a2,
              rw_g2, rw_kk, rw_ka, rw_rk, rw_lnx_g, rw_lnx_b, mla_qn_g, mla_wuq, mla_kvn_g, mla_wukv,
              mlp_w1, mlp_w2, final_g):
    ang = axial_angles(x.shape[1])
    xc = ctx
    s_lat = jax.nn.silu(c)
    s_ctx = jax.nn.silu(c_ctx)
    for l in range(DEPTH):
        with_ctx = l < DEPTH - 1
        mod = jnp.split((s_lat @ ada_w[l] + ada_b[l])[:, None, :], 6, axis=-1)
        modc = jnp.split(s_ctx @ ada_w[l] + ada_b[l], 6, axis=-1)
        h = rms_norm(x, norm1_g[l]) * (1.0 + mod[1]) + mod[0]
        hc = rms_norm(xc, norm1_g[l]) * (1.0 + modc[1]) + modc[0]
        p = h @ w_in[l]
        pc_tail = hc @ w_in[l][:, OFF_RW:]

        y_conv = conv_module(p[..., :OFF_POOL], conv_dw[l], conv_db[l], conv_gn_g[l], conv_gn_b[l], conv_pw[l])
        y_pool = multiscale_pool(p[..., OFF_POOL:OFF_Q], pool_w[l], pool_scale[l])
        y_rw, yc_rw = rwkv7_bidirectional(p[..., OFF_RW:OFF_KV], pc_tail[..., :N_RW_IN], rw_mu_prev[l],
                                          rw_mu_next[l], rw_w0[l], rw_w2[l], rw_a0[l], rw_a2[l], rw_g2[l],
                                          rw_kk[l], rw_ka[l], rw_rk[l], rw_lnx_g[l], rw_lnx_b[l], with_ctx)
        k_l, v_l = mla_keys_values(p[..., OFF_KV:], mla_kvn_g[l], mla_wukv[l], ang)
        k_c, v_c = mla_keys_values(pc_tail[..., N_RW_IN:], mla_kvn_g[l], mla_wukv[l], None)
        q_l = mla_queries(p[..., OFF_Q:OFF_RW], mla_qn_g[l], mla_wuq[l], ang)
        y_att = block_attention(q_l, jnp.concatenate([k_c, k_l], axis=1), jnp.concatenate([v_c, v_l], axis=1))

        x = x + mod[2] * (jnp.concatenate([y_conv, y_rw, y_pool, y_att], axis=-1) @ w_out[l])
        x = x + mod[5] * sq_relu_mlp(rms_norm(x, norm2_g[l]) * (1.0 + mod[4]) + mod[3], mlp_w1[l], mlp_w2[l])

        if with_ctx:
            pc_head = hc @ w_in[l][:, :OFF_RW]
            yc_conv = conv_module(pc_head[..., :OFF_POOL], conv_dw[l], conv_db[l], conv_gn_g[l], conv_gn_b[l],
                                  conv_pw[l])
            yc_pool = multiscale_pool(pc_head[..., OFF_POOL:OFF_Q], pool_w[l], pool_scale[l])
            q_c = mla_queries(pc_head[..., OFF_Q:OFF_RW], mla_qn_g[l], mla_wuq[l], None)
            yc_att = block_attention(q_c, k_c, v_c)
            xc = xc + modc[2] * (jnp.concatenate([yc_conv, yc_rw, yc_pool, yc_att], axis=-1) @ w_out[l])
            xc = xc + modc[5] * sq_relu_mlp(rms_norm(xc, norm2_g[l]) * (1.0 + modc[4]) + modc[3],
                                            mlp_w1[l], mlp_w2[l])
    return rms_norm(x, final_g)


_drawn_inputs = setup_inputs


def setup_inputs(seed=0):
    import zlib

    import numpy as np

    out = dict(_drawn_inputs(seed))
    spreads = {}
    factors = {'ctx': 3.962,
     'conv_db': 8.0,
     'conv_gn_b': 21.615,
     'rw_a0': 4.341,
     'rw_lnx_g': 3.245,
     'rw_lnx_b': 23.64,
     'mla_qn_g': 8.0,
     'mla_kvn_g': 3.617}
    for name, (base, spread) in spreads.items():
        noise = np.random.default_rng([zlib.crc32(name.encode()), seed]).standard_normal(out[name].shape)
        drawn = base * np.exp(spread * noise) if base else spread * noise
        out[name] = __import__('jax').numpy.asarray(drawn.astype(out[name].dtype))
    for name, factor in factors.items():
        out[name] = (out[name] * factor).astype(out[name].dtype)
    return out
```

```python
from contextlib import ExitStack

import numpy as np
import concourse.bass as bass
from concourse import mybir

F32 = mybir.dt.float32
F32R = mybir.dt.float32r
U32 = mybir.dt.uint32
ALU = mybir.AluOpType
ACT = mybir.ActivationFunctionType
AX_X = mybir.AxisListType.X

P = 128
D = 1024
KT = D // P
CTX, LAT = 256, 512
TOK = CTX + LAT
DEPTH = 2
GW = 256
HD = 64
C = 64
NC = TOK // C
CCTX = CTX // C
TAPS = 31
HEADS = 4
NOPE, ROPE = 64, 32
QD = NOPE + ROPE
FF = 4 * D
GROUPS = 4
ADA_AFTER = {1: 2, **{j: 1 for j in range(2, 12)}}
UPG = 16
NT_MODS = 48
RAW = 4
SPL = 2
NORM_EPS, GN_EPS, LNX_EPS = 1e-6, 1e-5, 64e-5
C1 = float(-0.5 * np.exp(-0.5))
SCALE = float(QD) ** -0.5
T = TOK * 4

OFF_POOL, OFF_Q, OFF_RW, OFF_KV = 512, 768, 1024, 2176

IN_UNITS = ([(("q", i), OFF_Q + P * i) for i in range(2)] + [(("kv", 0), OFF_KV), (("rope", 0), OFF_KV + P)]
            + [(("z", i), OFF_RW + P * i) for i in (7, 8, 2, 3, 0, 1, 4, 5, 6)]
            + [(("cg", i), GW + P * i) for i in range(2)] + [(("cv", i), P * i) for i in range(2)]
            + [(("pool", i), OFF_POOL + P * i) for i in range(2)])
LAT_ONLY = {"q", "cg", "cv", "pool"}
N_IN = len(IN_UNITS)


def columns(names):
    at, n = {}, 0
    for name, width in names:
        at[name] = n
        n += width
    at["end"] = n
    return at


VEC = [("ada_b", 48), ("n1", 8), ("n2", 8), ("dw", 2 * TAPS), ("db", 2), ("cgg", 2), ("cgb", 2), ("psc", 2),
       ("mup", 9), ("mun", 9), ("w0", 4), ("a0", 4), ("kk", 2), ("ka", 2), ("rk", 2), ("lg", 2), ("lb", 2),
       ("qn", 2), ("kvn", 1)]
VEC_L = columns(VEC)
V_FINAL = DEPTH * VEC_L["end"]
N_VEC = V_FINAL + KT

CST = columns([("ident", P), ("ones", P), ("bones", P), ("lo", 6 * C), ("up", 6 * C), ("tri", 4 * C), ("istack", C),
               ("rot", P)])
BIG = columns([("reset", 2 * TOK), ("cos", LAT), ("sin", LAT), ("rcnt", 2 * TOK)])
SW_A = columns([("wuq", 2 * HEADS * QD), ("wukv", 4 * P), ("pw", 2 * GW), ("poolw", 2 * P)])
SW_R = columns([("w2", GW), ("a2", GW), ("g2", GW)])

DER = columns([("A1", 16), ("A2", 16), ("c0", 9), ("hw0", 4), ("ha0", 4), ("nkk", 2), ("s1", 2), ("s2", 2),
               ("hg", 2), ("hb", 2)])


class Steps:

    def __init__(self):
        self.n = 0

    def up(self):
        self.n += 1
        return 1


class Signal:

    def __init__(self, sem, keys):
        self.sem, self.at = sem, {k: n + 1 for n, k in enumerate(keys)}


class Slots:

    def __init__(self, tensor, full, free):
        self.tensor, self.sem_full, self.sem_free, self.n, self.at = tensor, full, free, 0, {}

    def claim(self, key):
        self.at[key] = self.n
        self.n += 1
        return self.slot(key)

    def slot(self, key):
        return self.tensor[:, self.at[key] % 2, :]

    def reused(self, key):
        return self.at[key] >= 2

    def use(self, key):
        return self.at[key] // 2 + 1

    def full(self, key):
        return self.sem_full[self.at[key] % 2]

    def free(self, key):
        return self.sem_free[self.at[key] % 2]


def chunk_order(d):
    if d == 0:
        return list(range(NC))
    return list(range(CCTX - 1, -1, -1)) + list(range(NC - 1, CCTX - 1, -1))


def attention_units(l):
    return [(h, q) for h in range(HEADS) for q in range(0 if l == 0 else 2, TOK // P)]


def bc(ap, shape, axis):
    return ap.unsqueeze(axis).to_broadcast(shape)


def trunk(nc, xT, stream, vecs, cond_in, consts, big, small_a, small_r, kept, out):
    es = ExitStack()
    with es:
        sem = lambda name: es.enter_context(nc.semaphore(name))
        base = (nc.sbuf_base + 31) // 32 * 32

        class Region:

            def __init__(self, offset):
                self.o = offset

            def __call__(self, name, shape, dt=F32):
                size = (int(np.prod(shape[1:])) * 4 + 31) // 32 * 32
                assert self.o + size <= nc.sbuf_usable_end, (name, self.o + size)
                t = nc.alloc_sbuf_tensor_at(name, shape, dt, offset=self.o)
                self.o += size
                return t

        R = Region(base)
        actH, actL, act_at = [], [], []
        for g in range(4):
            act_at.append(R.o)
            actH.append(R(f"act_hi{g}", [P, 2, TOK], F32R))
            actL.append(R(f"act_lo{g}", [P, 2, TOK], F32R))
        raw = R("raw_weights", [P, RAW, KT, P])
        whi = R("weights_hi", [P, SPL, KT, P], F32R)
        wlo = R("weights_lo", [P, SPL, KT, P], F32R)
        cst = R("consts_sb", [P, CST["end"]])
        vec = R("vecs_sb", [P, N_VEC])
        mods = R("mods", [P, DEPTH, NT_MODS, 2])
        cond = R("cond", [P, KT, 2])
        der = R("derived", [P, DER["end"]])
        sw_r = R("small_r_sb", [P, SW_R["end"]])
        stat_at = R.o
        stat = R("softmax_stats", [P, 4, HEADS * TOK // P])
        z_at = R.o
        zt = R("z_tiles", [P, 7, TOK])
        zv = R("z_v", [P, 2, TOK + 2 * C])
        free0 = R.o

        x = R("x_tiles", [P, KT, TOK])
        sq = R("squares", [P, 2, TOK])
        rinv = R("rinv", [P, TOK])
        tb = R("normed", [P, 2, TOK])
        hb = R("modulated", [P, 2, TOK])
        hid_lo = R("hidden_lo", [P, 8, TOK], F32R)
        relu = R("relu", [P, 2, TOK])
        hsq = R("hidden_sq", [P, 2, TOK])
        hid_hi = Region(z_at)("hidden_hi", [P, 8, TOK], F32R)

        R = Region(free0)
        wa = R("work_a", [P, 2, TOK])
        wb = R("work_b", [P, 2, TOK])
        q_sb = R("q_low_rank", [P, 2, TOK])
        ckv = R("kv_low_rank", [P, TOK])
        krope = R("k_rope", [P, TOK])
        ltmp = R("low_rank_tmp", [P, TOK])
        lrin = R("low_rank_rinv", [P, TOK])
        cs = R("cos_sin", [P, 2, LAT])
        sw_a = R("small_a_sb", [P, SW_A["end"]])
        UL = 15 + CTX + 15
        u_sb = R("conv_u", [P, 2, UL + LAT + 15])
        u_acc = R("conv_taps", [P, 2, CTX + 15 + LAT])
        PL = 8 + CTX + 16
        PWID = PL + LAT + 8
        pp = R("pool_p", [P, 2, PWID])
        ps = R("pool_sums", [P, 2, PWID])
        rcnt = R("pool_rcnt", [P, 2, TOK])
        qT = R("q_t", [P, 2, TOK])
        kT = R("k_t", [P, 2, TOK])
        rtmp = R("rope_tmp", [P, LAT])
        R = Region(act_at[1])
        v_tok = R("v_tok", [P, TOK // P, HEADS * HD])
        otok = R("o_tok", [P, TOK // P, HEADS * HD])
        R = Region(act_at[2])
        acc = R("conv_normed", [P, 2, TOK])
        ptmp = R("pool_tmp", [P, PWID])

        R = Region(free0)
        Q = R("rw_q", [P, 4, TOK])
        BK = R("rw_bk", [P, NC, 2, C])
        BKt = R("rw_bk_tok", [P, NC, P])
        XTd = R("rw_xt_diag", [P, NC, 2, C])
        UV = R("rw_uv", [P, NC, P])
        SV = R("rw_sv", [P, NC, P])
        LTd = R("rw_lt_diag", [P, NC, 2, C])
        Td = R("rw_t_diag", [P, NC, 2, C])
        b4_at = R.o
        M = R("rw_m", [P, 2, NC, C])
        b0_at = R.o
        X = R("rw_x", [P, NC, C])
        XT = R("rw_xt", [P, NC, C])
        Tc = R("rw_t", [P, NC, C])
        LT = R("rw_lt", [P, NC, C])
        nkk = R("rw_nkk", [P, TOK])
        kds = R("rw_kd_sum", [P, TOK])
        Y = R("rw_y", [P, TOK])
        reset = R("rw_reset", [P, 2, TOK])
        Wc = R("rw_w", [P, 2, C])
        R = Region(stat_at)
        SP = R("rw_s_decayed", [P, C])
        PC = R("rw_p_end", [P, NC])
        b = Region(b0_at)("rw_tmp", [P, 4, TOK])
        b45 = Region(b4_at)("rw_tmp2", [P, 2, TOK])

        psA = es.enter_context(nc.psum_tensor("psA", [P, 2, 1024], F32))
        psB = es.enter_context(nc.psum_tensor("psB", [P, 2, 1024], F32))
        A = Slots(psA, [sem("a0_full"), sem("a1_full")], [sem("a0_free"), sem("a1_free")])
        B = Slots(psB, [sem("b0_full"), sem("b1_full")], [sem("b0_free"), sem("b1_free")])

        V = lambda l, name, i=0, n=1: vec[:, l * VEC_L["end"] + VEC_L[name] + i:][:, 0:n]
        DR = lambda name, i=0, n=1: der[:, DER[name] + i:DER[name] + i + n]
        K = lambda name, n, i=0: cst[:, CST[name] + i:CST[name] + i + n]
        ident, ones, bones = K("ident", P), K("ones", P), K("bones", P)
        H = lambda k: actH[k // 2][:, k % 2, :]
        L = lambda k: actL[k // 2][:, k % 2, :]
        f32 = lambda ap: ap.bitcast(F32)
        PSC = 256
        first = lambda l: 0 if l == 0 else CTX
        segs = lambda c0: [(0, CTX, LAT)] + ([(1, 0, CTX)] if c0 == 0 else [])

        units = [("ada", 0)] * 16
        for i in range(N_IN):
            units += [("split", IN_UNITS[i][0])] + [("ada", 0)] * (2 if i < 16 else 0)
        units += [("split", "out")] * 8
        mlp0 = {0: len(units)}
        LOOP = {0: 28, 1: 16}
        ada_after = lambda l, j: ADA_AFTER.get(j, 0) if l == 0 else 0
        for g in range(GROUPS):
            for j in range(UPG):
                units += [("split", "mlp")] + [("ada", 1)] * ada_after(0, j)
        units += [("split", u[0]) for u in IN_UNITS] + [("split", "out")] * 8
        mlp0[1] = len(units)
        units += [("split", "mlp")] * (UPG * GROUPS)
        split_no, unit_of_split, n = {}, [], 0
        for i, (kind, _) in enumerate(units):
            if kind == "split":
                split_no[i] = len(unit_of_split)
                unit_of_split.append(i)
        ada_no = {i: k for k, i in enumerate(i for i, u in enumerate(units) if u[0] == "ada")}
        SPL_L = len(unit_of_split) // DEPTH
        S_OUT, S_MLP = N_IN, N_IN + 8
        assert N_IN + 8 + UPG * GROUPS == SPL_L

        c_in = sem("constants_in")
        mix_in = sem("mixing_constants_in")
        rw_in = sem("rwkv_constants_in")
        x_in = sem("x_loaded")
        x_kept = sem("x_kept")
        out_done = sem("out_stored")
        w_in = [sem(f"raw_full{i}") for i in range(RAW)]
        w_hi, w_lo, ada_used = sem("w_hi"), sem("w_lo"), sem("ada_used")
        cond_th, cond_ready = sem("cond_tanh"), sem("cond_ready")
        vector_step, pool_step = sem("vector_step"), sem("pool_step")
        relu_ready, hid_hi_ready, hid_ready = sem("relu_ready"), sem("hidden_hi_ready"), sem("hidden_ready")

        ls, hs = range(DEPTH), range(HEADS)
        norms = [(l, n) for l in ls for n in (1, 2)] + [(DEPTH, 0)]
        nk = [(n, k) for n in norms for k in range(KT)]
        li2 = [(l, i) for l in ls for i in range(2)]
        sq_ready = Signal(sem("squares_ready"), nk)
        sq_used = Signal(sem("squares_used"), [(n, k) for n in norms for k in range(KT - 1)])
        rms = Signal(sem("rms_ready"), norms)
        mod_ready = Signal(sem("modulated"), nk[:-KT])
        act_hi = Signal(sem("act_hi_ready"), nk[:-KT])
        act_lo = Signal(sem("act_lo_ready"), nk[:-KT])
        fin_ready = Signal(sem("final_tile"), [(k,) for k in range(KT)])
        der_ready = Signal(sem("derived_ready"), [(l,) for l in ls])

        lr_sq = Signal(sem("low_rank_squared"), [(l, i) for l in ls for i in range(3)])
        lr_rms = Signal(sem("low_rank_rms"), li2)
        lr_normed = Signal(sem("low_rank_normed"), li2)
        kr_ready = Signal(sem("k_rope_rotated"), [(l,) for l in ls])
        z_order = [u[0][1] for u in IN_UNITS if u[0][0] == "z"]
        z_mixed = Signal(sem("z_mixed"), [(l, i) for l in ls for i in z_order])
        pads = Signal(sem("pads_zeroed"), [(l,) for l in ls])
        lh = [(l, h) for l in ls for h in hs]
        q_rot = Signal(sem("q_rotated"), lh)
        k_full = Signal(sem("k_rope_copied"), lh)
        au = {l: attention_units(l) for l in ls}
        lau = [(l, i) for l in ls for i in range(len(au[l]))]
        rowmax = Signal(sem("row_max"), lau)
        y_hi = Signal(sem("y_hi_ready"), [(l, s, i) for l in ls for s in ("att", "conv", "pool", "rw") for i in range(2)])
        y_lo = Signal(sem("y_lo_ready"), li2)
        conv_sum = Signal(sem("conv_summed"), li2)
        conv_sq = Signal(sem("conv_squared"), li2)
        conv_std = Signal(sem("conv_std"), li2)
        conv_pre = Signal(sem("conv_scaled"), li2)
        conv_th = Signal(sem("conv_tanh"), li2)
        conv_act = Signal(sem("conv_silu"), li2)
        pool_d = Signal(sem("pool_diff"), li2)

        rw_zero = Signal(sem("rw_zeroed"), [(l,) for l in ls])
        l_lora = Signal(sem("decay_input"), [(l,) for l in ls])
        g_th = Signal(sem("gate_tanh"), [(l,) for l in ls])
        kk_sq = Signal(sem("kk_squared"), li2)
        kk_std = Signal(sem("kk_norm"), li2)
        ru = [(l, j, d) for l in ls for j in range(2) for d in range(2)]
        cum = Signal(sem("decay_summed"), ru)
        exps = Signal(sem("decay_exps"), [(u, i) for u in ru for i in range(3)])
        dk = Signal(sem("decay_before"), ru)
        prep = Signal(sem("chunk_operands"), ru)
        v_tp = Signal(sem("v_chunks"), [(l, j, w) for l in ls for j in range(2) for w in range(2)])
        ltd = Signal(sem("lt_diag"), ru)
        t_c = Signal(sem("t_copied"), [(u, i) for u in ru for i in range(1, 6)])
        x_one = Signal(sem("x_first"), ru)
        xt_one = Signal(sem("xt_first"), ru)
        xt_diag = Signal(sem("xt_first_diag"), ru)
        s_zero = Signal(sem("state_zeroed"), ru)
        s_dec = Signal(sem("state_decayed"), [(u, i) for u in ru for i in range(NC - 1)])
        rw_sq = Signal(sem("rw_squared"), li2)
        rw_std = Signal(sem("rw_std"), li2)
        bon = Signal(sem("bonus_product"), li2)

        block = es.enter_context(nc.Block())
        HALF = ((slice(0, 64), 0), (slice(64, P), 1))
        rp = slice(NOPE, QD)
        ZI = {0: 0, 1: 1, 2: 2, 3: 3, 6: 4, 7: 5, 8: 6}
        z_of = lambda i: zv[:, i - 4, C:C + TOK] if i in (4, 5) else zt[:, ZI[i], :]
        chunks = lambda ap: ap.rearrange("p (c t) -> p c t", t=C)

        @block.tensor
        def _(pe):
            def span(dst, lhsT, rhs, start, stop, c0=0, part=slice(0, P)):
                if c0 == 0:
                    pe.matmul(dst[part, PSC:PSC + CTX], lhsT, rhs[:, 0:CTX], start=start, stop=stop)
                return pe.matmul(dst[part, PSC + CTX:], lhsT, rhs[:, CTX:TOK], start=start, stop=stop)

            def unit_products(dst, w, hi, lo, c0):
                for k in range(KT):
                    span(dst, whi[:, w, k, :], lo(k), k == 0, False, c0)
                    span(dst, whi[:, w, k, :], hi(k), False, False, c0)
                    m = span(dst, wlo[:, w, k, :], hi(k), False, k == KT - 1, c0)
                return m

            def linear(n, key, c0, hi=H, lo=L, plus=0, slots=0):
                dst = A.claim(key)
                if A.reused(key):
                    pe.wait_ge(A.free(key), A.use(key) - 1 + slots)
                pe.wait_ge(w_lo, n + 1 + plus)
                unit_products(dst, n % SPL, hi, lo, c0).then_inc(A.full(key), 1)

            def modulation(i, dst, plus=0):
                r = i % RAW
                pe.wait_ge(w_in[r], 16 * (i // RAW + 1) + plus)
                for k in range(KT):
                    m = pe.matmul(dst, raw[:, r, k, :], cond[:, k, :],
                                  start=k == 0, stop=k == KT - 1)
                m.then_inc(ada_used, 1)

            def moments(key, n_sum, waits, srcs, c0, lhsT):
                dst = B.claim(key)
                if B.reused(key):
                    pe.wait_ge(B.free(key), B.use(key) - 1)
                for k in range(n_sum):
                    waits(k)
                    m = span(dst, lhsT, srcs(k), k == 0, k == n_sum - 1, c0)
                    if k < KT - 1:
                        m.then_inc(sq_used.sem, 1)
                m.then_inc(B.full(key), 1)

            def norm(key, c0):
                moments(("norm", key), KT, lambda k: pe.wait_ge(sq_ready.sem, sq_ready.at[key, k]),
                        lambda k: sq[:, k % 2, :], c0, ones)

            def small(pool, key, c0, pairs, part=slice(0, P)):
                dst = pool.claim(key)
                if pool.reused(key):
                    pe.wait_ge(pool.free(key), pool.use(key) - 1)
                for i, (lhsT, rhs) in enumerate(pairs):
                    m = span(dst, lhsT, rhs, i == 0, i == len(pairs) - 1, c0, part)
                m.then_inc(pool.full(key), 1)

            pe.wait_ge(c_in, 16 * 3)
            pe.wait_ge(cond_ready, 1)

            def ada_end(dst, key):
                pe.matmul(dst[:, 512:514], ident, cond[:, 0, :], start=True, stop=True).then_inc(B.full(key), 1)

            u = 0
            nsplit = 0
            dst = B.claim(("ada", 0, 0))
            if B.reused(("ada", 0, 0)):
                pe.wait_ge(B.free(("ada", 0, 0)), B.use(("ada", 0, 0)) - 1)
            for t in range(16):
                modulation(u, dst[:, 2 * t:2 * t + 2])
                u += 1
            ada_end(dst, ("ada", 0, 0))
            for l in ls:
                c0 = first(l)
                norm((l, 1), 0)
                if l == 0:
                    ada_dst = B.claim(("ada", 0, 1))
                    if B.reused(("ada", 0, 1)):
                        pe.wait_ge(B.free(("ada", 0, 1)), B.use(("ada", 0, 1)) - 1)
                for i, (name, _) in enumerate(IN_UNITS):
                    if i == 0:
                        pe.wait_ge(act_lo.sem, act_lo.at[(l, 1), KT - 1])
                    linear(nsplit, (l,) + name, c0 if name[0] in LAT_ONLY else 0)
                    nsplit += 1
                    u += 1
                    for t in range(2 * i, 2 * i + 2) if l == 0 and i < 16 else ():
                        modulation(u, ada_dst[:, 2 * t:2 * t + 2])
                        u += 1
                if l == 0:
                    ada_end(ada_dst, ("ada", 0, 1))

                pe.wait_ge(mix_in, 48 * (l + 1))
                pe.wait_ge(lr_sq.sem, lr_sq.at[l, 1])
                small(B, (l, "qstat"), c0, [(ones, ltmp[:, :]), (ones, lrin[:, :])])
                pe.wait_ge(lr_sq.sem, lr_sq.at[l, 2])
                small(B, (l, "kvstat"), 0, [(ones, kT[:, 0, :])])
                pe.wait_ge(A.free((l, "rope", 0)), A.use((l, "rope", 0)))

                def rotate(key, src):
                    dst = B.claim(key)
                    if B.reused(key):
                        pe.wait_ge(B.free(key), B.use(key) - 1)
                    pe.matmul(dst[rp, PSC + CTX:], K("rot", ROPE)[rp, :], src[rp, CTX:], start=True,
                                       stop=True).then_inc(B.full(key), 1)

                rotate((l, "krot"), krope[:, :])
                pe.wait_ge(lr_normed.sem, lr_normed.at[l, 1])
                for w, blocks in enumerate(((0, 1, 2, 3), (4, 5))):
                    dst = A.claim((l, "v", w))
                    if A.reused((l, "v", w)):
                        pe.wait_ge(A.free((l, "v", w)), A.use((l, "v", w)) - 1)
                    vw = sw_a[:, SW_A["wukv"]:][:, 0:4 * P].rearrange("p (h n) -> p h n", h=HEADS)[:, :, NOPE:]
                    for b_ in blocks:
                        m = pe.matmul(dst[:, GW * (b_ % 4):GW * (b_ % 4 + 1)], ckv[:, P * b_:P * (b_ + 1)], vw,
                                      start=True, stop=True)
                    m.then_inc(A.full((l, "v", w)), 1)

                def head_operands(h):
                    wq = lambda k: sw_a[:, SW_A["wuq"] + k * HEADS * QD + h * QD:][:, 0:QD]
                    wk = sw_a[:, SW_A["wukv"] + h * P:][:, 0:NOPE]
                    small(A, (l, "qh", h), c0, [(wq(k), q_sb[:, k, :]) for k in range(2)], slice(0, QD))
                    small(A, (l, "kh", h), 0, [(wk, ckv[:, :])], slice(0, NOPE))
                    pe.wait_ge(A.free((l, "qh", h)), A.use((l, "qh", h)))
                    rotate((l, "qrot", h), qT[:, h % 2, :])

                def scores(i):
                    h, q = au[l][i]
                    dst = A.claim((l, "s", i))
                    if A.reused((l, "s", i)):
                        pe.wait_ge(A.free((l, "s", i)), A.use((l, "s", i)) - 1)
                    if i == 0 or au[l][i - 1][0] != h:
                        pe.wait_ge(q_rot.sem, q_rot.at[l, h])
                        pe.wait_ge(A.free((l, "kh", h)), A.use((l, "kh", h)))
                        pe.wait_ge(k_full.sem, k_full.at[l, h])
                    m = pe.matmul(dst[:, PSC:PSC + CTX], qT[0:QD, h % 2, P * q:P * (q + 1)], kT[0:QD, h % 2, 0:CTX],
                                  start=True, stop=True)
                    if q >= CTX // P:
                        m = pe.matmul(dst[:, PSC + CTX:], qT[0:QD, h % 2, P * q:P * (q + 1)], kT[0:QD, h % 2, CTX:],
                                      start=True, stop=True)
                    m.then_inc(A.full((l, "s", i)), 1)

                def mix_values(i):
                    h, q = au[l][i]
                    nb = (CTX if q < CTX // P else TOK) // P
                    dst = B.claim((l, "pt", i))
                    if B.reused((l, "pt", i)):
                        pe.wait_ge(B.free((l, "pt", i)), B.use((l, "pt", i)) - 1)
                    pe.wait_ge(A.free((l, "s", i)), A.use((l, "s", i)))
                    for b_ in range(nb):
                        m = pe.transpose(dst[:, PSC + P * b_:PSC + P * (b_ + 1)], wa[:, i % 2, P * b_:P * (b_ + 1)], ident)
                    m.then_inc(B.full((l, "pt", i)), 1)
                    dst = B.claim((l, "o", i))
                    if B.reused((l, "o", i)):
                        pe.wait_ge(B.free((l, "o", i)), B.use((l, "o", i)) - 1)
                    if i == 0:
                        pe.wait_ge(A.free((l, "v", 0)), A.use((l, "v", 0)))
                        pe.wait_ge(A.free((l, "v", 1)), A.use((l, "v", 1)))
                    pe.wait_ge(B.free((l, "pt", i)), B.use((l, "pt", i)))
                    for b_ in range(nb):
                        m = pe.matmul(dst[:, 0:HD], wb[:, i % 2, P * b_:P * (b_ + 1)], v_tok[:, b_, HD * h:HD * (h + 1)],
                                      start=b_ == 0, stop=b_ == nb - 1)
                    m.then_inc(B.full((l, "o", i)), 1)

                head_operands(0)
                for i in range(len(au[l])):
                    h = au[l][i][0]
                    if (i == 0 or au[l][i - 1][0] != h) and h + 1 < HEADS:
                        head_operands(h + 1)
                    scores(i)
                    if i:
                        mix_values(i - 1)
                mix_values(len(au[l]) - 1)
                for i in range(2):
                    dst = A.claim((l, "att", i))
                    if A.reused((l, "att", i)):
                        pe.wait_ge(A.free((l, "att", i)), A.use((l, "att", i)) - 1)
                    if i == 0:
                        pe.wait_ge(B.free((l, "o", len(au[l]) - 1)), B.use((l, "o", len(au[l]) - 1)))
                        pe.wait_ge(B.free((l, "o", len(au[l]) - 2)), B.use((l, "o", len(au[l]) - 2)))
                    for q in range(c0 // P, TOK // P):
                        m = pe.transpose(dst[:, PSC + P * q:PSC + P * (q + 1)], otok[:, q, P * i:P * (i + 1)], ident)
                    m.then_inc(A.full((l, "att", i)), 1)

                for i in range(2):
                    pe.wait_ge(conv_sum.sem, conv_sum.at[l, i])
                    small(B, (l, "cmean", i), c0, [(bones, acc[:, i, :])])
                for i in range(2):
                    pe.wait_ge(conv_sq.sem, conv_sq.at[l, i])
                    small(B, (l, "cvar", i), c0, [(bones, u_sb[:, i, 0:TOK])])
                pe.wait_ge(conv_act.sem, conv_act.at[l, 1])
                for i in range(2):
                    small(A, (l, "convp", i), c0,
                          [(sw_a[:, SW_A["pw"] + k * GW + i * P:][:, 0:P], acc[:, k, :]) for k in range(2)])
                for i in range(2):
                    pe.wait_ge(pool_d.sem, pool_d.at[l, i])
                    small(A, (l, "poolp", i), c0, [(sw_a[:, SW_A["poolw"] + i * P:][:, 0:P], rcnt[:, i, :])])

                pe.wait_ge(rw_in, 32 * (l + 1))
                pe.wait_ge(l_lora.sem, l_lora.at[(l,)])
                pe.wait_ge(rw_zero.sem, rw_zero.at[(l,)])
                for j in range(2):
                    pe.wait_ge(kk_sq.sem, kk_sq.at[l, j])
                    small(B, (l, "kk", j), 0, [(bones, nkk[:, :])])
                    for d in range(2):
                        un = (l, j, d)
                        dp = slice(64 * d, 64 * d + 64)
                        small(A, (un, "w2"), 0, [(sw_r[dp, SW_R["w2"] + P * j:][:, 0:P], zt[dp, 5, :])])
                        small(A, (un, "a2"), 0, [(sw_r[dp, SW_R["a2"] + P * j:][:, 0:P], zt[dp, 6, :])])
                        if d == 0:
                            for w, ms in enumerate((range(0, 7), range(7, 13))):
                                dst = B.claim((l, j, "v", w))
                                if B.reused((l, j, "v", w)):
                                    pe.wait_ge(B.free((l, j, "v", w)), B.use((l, j, "v", w)) - 1)
                                for m_ in ms:
                                    o = m_ - ms[0]
                                    m = pe.transpose(dst[:, P * o:P * (o + 1)], zv[:, j, C * m_:C * m_ + P], ident)
                                m.then_inc(B.full((l, j, "v", w)), 1)
                        pe.wait_ge(prep.sem, prep.at[un])
                        for g in range(3):
                            dst = A.claim((un, "gram", g))
                            if A.reused((un, "gram", g)):
                                pe.wait_ge(A.free((un, "gram", g)), A.use((un, "gram", g)) - 1)
                            for c in range(4 * g, 4 * g + 4):
                                for part, s_ in HALF:
                                    m = pe.matmul(dst[:, 512 * s_ + P * (c % 4):][:, 0:P],
                                                  BK[part, c, :, :], Q[part, 2 * s_:2 * s_ + 2, C * c:C * (c + 1)],
                                                  start=True, stop=True)
                            m.then_inc(A.full((un, "gram", g)), 1)
                        for w in range(2):
                            dst = B.claim((un, "bkt", w))
                            if B.reused((un, "bkt", w)):
                                pe.wait_ge(B.free((un, "bkt", w)), B.use((un, "bkt", w)) - 1)
                            for c in range(8 * w, min(8 * w + 8, NC)):
                                m = pe.transpose(dst[:, P * (c % 8):][:, 0:P], BK[:, c, :, :], ident)
                            m.then_inc(B.full((un, "bkt", w)), 1)

                        def by_chunk(pool, key, lhsT, rhs):
                            dst = pool.claim(key)
                            if pool.reused(key):
                                pe.wait_ge(pool.free(key), pool.use(key) - 1)
                            for c in range(NC):
                                m = pe.matmul(dst[:, PSC + C * c:][:, 0:C], lhsT[:, c, :, :], rhs(c), start=True, stop=True)
                            m.then_inc(pool.full(key), 1)

                        pe.wait_ge(ltd.sem, ltd.at[un])
                        by_chunk(A, (un, "t", 0), LTd, lambda c: K("istack", C))
                        for i in range(1, 6):
                            if i == 1:
                                pe.wait_ge(x_one.sem, x_one.at[un])
                            else:
                                pe.wait_ge(B.free((un, "x", i - 1)), B.use((un, "x", i - 1)))
                            by_chunk(A, (un, "t", i), LTd, lambda c: X[:, c, :])
                            if i == 1:
                                pe.wait_ge(xt_diag.sem, xt_diag.at[un])
                            else:
                                pe.wait_ge(B.free((un, "xt", i - 1)), B.use((un, "xt", i - 1)))
                            if i < 5:
                                pe.wait_ge(t_c.sem, t_c.at[un, i])
                                by_chunk(B, (un, "x", i), XTd, lambda c: Tc[:, c, :])
                            pe.wait_ge(A.free((un, "t", i)), A.use((un, "t", i)))
                            by_chunk(B, (un, "xt", i), Td, lambda c: XT[:, c, :])

                        order = chunk_order(d)
                        pe.wait_ge(B.free((un, "xt", 5)), B.use((un, "xt", 5)))
                        pe.wait_ge(B.free((un, "bkt", 0)), B.use((un, "bkt", 0)))
                        pe.wait_ge(B.free((un, "bkt", 1)), B.use((un, "bkt", 1)))
                        ydst = B.claim((un, "y"))
                        if B.reused((un, "y")):
                            pe.wait_ge(B.free((un, "y")), B.use((un, "y")) - 1)
                        for n_, c in enumerate(order):
                            if n_ == 0:
                                pe.wait_ge(s_zero.sem, s_zero.at[un])
                            else:
                                pe.wait_ge(A.free((un, "s", n_ - 1)), A.use((un, "s", n_ - 1)))
                            dst = A.claim((un, "w", n_))
                            if A.reused((un, "w", n_)):
                                pe.wait_ge(A.free((un, "w", n_)), A.use((un, "w", n_)) - 1)
                            for part, s_ in HALF:
                                m = pe.matmul(dst[part, 0:C], Q[:, 2 * s_, C * c:C * (c + 1)],
                                              SV[:, c, HD * s_:HD * (s_ + 1)], start=True, stop=True)
                            m.then_inc(A.full((un, "w", n_)), 1)
                            dst = A.claim((un, "u", n_))
                            if A.reused((un, "u", n_)):
                                pe.wait_ge(A.free((un, "u", n_)), A.use((un, "u", n_)) - 1)
                            pe.wait_ge(A.free((un, "w", n_)), A.use((un, "w", n_)))
                            pe.matmul(dst[:, 0:C], XTd[:, c, :, :], Wc[:, n_ % 2, :], start=True, stop=True)\
                                .then_inc(A.full((un, "u", n_)), 1)
                            pe.wait_ge(A.free((un, "u", n_)), A.use((un, "u", n_)))
                            if n_ < NC - 1:
                                dst = A.claim((un, "s", n_))
                                if A.reused((un, "s", n_)):
                                    pe.wait_ge(A.free((un, "s", n_)), A.use((un, "s", n_)) - 1)
                                for part, s_ in HALF:
                                    m = pe.matmul(dst[part, 0:HD], BKt[:, c, HD * s_:HD * (s_ + 1)],
                                                  UV[:, c, HD * s_:HD * (s_ + 1)], start=True, stop=True)
                                m.then_inc(A.full((un, "s", n_)), 1)
                            if c * C >= c0:
                                for part, s_ in HALF:
                                    o = PSC + C * c
                                    hv = slice(HD * s_, HD * (s_ + 1))
                                    pe.matmul(ydst[part, o:o + C], SV[:, c, hv], Q[:, 2 * s_ + 1, C * c:C * (c + 1)],
                                              start=True, stop=False)
                                    m = pe.matmul(ydst[part, o:o + C], UV[:, c, hv], M[:, s_, c, :],
                                                  start=False, stop=True)
                        m.then_inc(B.full((un, "y")), 1)
                    pe.wait_ge(bon.sem, bon.at[l, j])
                    small(A, (l, j, "bonus"), c0, [(bones, b[:, 1, :])])
                    pe.wait_ge(B.free(((l, j, 1), "y")), B.use(((l, j, 1), "y")))
                    small(B, (l, j, "mean"), c0, [(bones, Y[:, :])])
                    pe.wait_ge(rw_sq.sem, rw_sq.at[l, j])
                    small(B, (l, j, "var"), c0, [(bones, b[:, 0, :])])
                    small(A, (l, j, "gate"), c0, [(sw_r[:, SW_R["g2"] + P * j:][:, 0:P], zt[:, 4, :])])

                for key in ("att", "convp", "poolp"):
                    for i in range(2):
                        pe.wait_ge(A.free((l, key, i)), A.use((l, key, i)))
                pe.wait_ge(y_lo.sem, y_lo.at[l, 1])
                for m_ in range(KT):
                    linear(nsplit, (l, "out", m_), c0)
                    nsplit += 1
                    u += 1
                norm((l, 2), c0)

                hh, hl = (lambda k: hid_hi[:, k, :]), (lambda k: hid_lo[:, k, :])

                if l == 0:
                    adst = B.claim((l, "ada1"))
                    if B.reused((l, "ada1")):
                        pe.wait_ge(B.free((l, "ada1")), B.use((l, "ada1")) - 1)

                def group(g0, g):
                    n, i, t = nsplit + UPG * g0, mlp0[l] + LOOP[l] * g0, 0
                    for j in range(UPG):
                        if j == 8:
                            pe.wait_ge(hid_ready, 8 * (l * GROUPS + g0 + 1) + 8 * g)
                        linear(n + j, (l, "mlp", g0, j), c0, *((H, L) if j < 8 else (hh, hl)), UPG * g, 8 * g)
                        i += 1
                        for _ in range(ada_after(l, j)):
                            modulation(i, adst[:, bass.ds(2 * t + 24 * g, 2)], 16 * (LOOP[l] // RAW) * g)
                            i, t = i + 1, t + 1

                pe.wait_ge(act_lo.sem, act_lo.at[(l, 2), KT - 1])
                if l == 0:
                    with pe.Fori(0, GROUPS) as g:
                        group(0, g)
                    A.n += UPG * (GROUPS - 1)
                    ada_end(adst, (l, "ada1"))
                else:
                    with pe.Fori(0, GROUPS - 1) as g:
                        group(0, g)
                    A.n += UPG * (GROUPS - 2)
                    group(GROUPS - 1, 0)
                nsplit += UPG * GROUPS
                u += LOOP[l] * GROUPS
            norm((DEPTH, 0), CTX)

        @block.scalar
        def _(act):
            cp = lambda o, i, **k: act.activation(o, i, ACT.Copy, **k)

            def split_hi(n, plus=0, i_plus=0):
                i = unit_of_split[n]
                act.wait_ge(w_in[i % RAW], 16 * (i // RAW + 1) + i_plus)
                act.activation(whi[:, n % SPL], raw[:, i % RAW], ACT.Copy).then_inc(w_hi, 1)

            def ahead(n, key, plus=0, i_plus=0, last=False):
                act.wait_ge(A.full(key), A.use(key) + plus)
                src = A.slot(key)
                if not last:
                    split_hi(n + SPL, i_plus=i_plus)
                return src

            def norm(key, c0, updated):
                for k in range(KT):
                    updated(k)
                    if k >= 2:
                        act.wait_ge(sq_used.sem, sq_used.at[key, k - 2])
                    act.activation(sq[:, k % 2, c0:], x[:, k, c0:], ACT.Square).then_inc(sq_ready.sem, 1)
                act.wait_ge(B.full(("norm", key)), B.use(("norm", key)))
                src = B.slot(("norm", key))
                act.activation(rinv[:, c0:], src[:, PSC + c0:], ACT.Sqrt, scale=1.0 / D, bias=NORM_EPS)\
                    .then_inc(rms.sem, 1)

            def operand_hi(key, c0):
                for k in range(KT):
                    act.wait_ge(mod_ready.sem, mod_ready.at[key, k])
                    cp(H(k)[:, c0:], hb[:, k % 2, c0:]).then_inc(act_hi.sem, 1)

            act.wait_ge(c_in, 48)
            act.activation(mods[:, 1, 0:8, :], cond[:, :, :], ACT.Tanh, scale=0.5).then_inc(cond_th, 1)
            split_hi(0)
            split_hi(1)
            n = 0
            for l in ls:
                c0 = first(l)
                if l == 0:
                    norm((0, 1), 0, lambda k: act.wait_ge(x_in, 16))
                else:
                    norm((1, 1), 0, lambda k: act.wait_ge(A.free((0, "mlp", 0, 8 + k)),
                                                           A.use((0, "mlp", 0, 8 + k)) + 8 * (GROUPS - 1)))
                operand_hi((l, 1), 0)
                act.wait_ge(der_ready.sem, der_ready.at[(l,)])
                if l == 1:
                    act.wait_ge(x_kept, 16)
                nz = 0
                for name, i in (u[0] for u in IN_UNITS):
                    key = (l, name, i)
                    src = ahead(n, key)
                    n += 1
                    if name == "q":
                        cp(q_sb[:, i, c0:], src[:, PSC + c0:]).then_inc(A.free(key), 1)
                        act.wait_ge(A.free(key), A.use(key))
                        act.activation((ltmp, lrin)[i][:, c0:], q_sb[:, i, c0:], ACT.Square).then_inc(lr_sq.sem, 1)
                    elif name == "kv":
                        cp(ckv[:, :], src[:, PSC:]).then_inc(A.free(key), 1)
                        act.wait_ge(A.free(key), A.use(key))
                        act.activation(kT[:, 0, :], ckv[:, :], ACT.Square).then_inc(lr_sq.sem, 1)
                    elif name == "rope":
                        cp(krope[rp, :], src[rp, PSC:]).then_inc(A.free(key), 1)
                    elif name == "z":
                        if nz >= 2:
                            act.wait_ge(z_mixed.sem, z_mixed.at[l, z_order[nz - 2]])
                        cp(wa[:, nz % 2, :], src[:, PSC:])
                        act.activation(z_of(i), src[:, PSC:], ACT.Identity, scale=DR("c0", i)).then_inc(A.free(key), 1)
                        nz += 1
                    elif name == "cg":
                        act.activation(wb[:, i, c0:], src[:, PSC + c0:], ACT.Tanh, scale=0.5).then_inc(A.free(key), 1)
                    elif name == "pool":
                        if i == 0:
                            act.wait_ge(pads.sem, pads.at[(l,)])
                        if l == 0:
                            cp(pp[:, i, 8:8 + CTX], src[:, PSC:PSC + CTX])
                        cp(pp[:, i, PL:PL + LAT], src[:, PSC + CTX:]).then_inc(A.free(key), 1)
                act.wait_ge(B.full((l, "qstat")), B.use((l, "qstat")))
                src = B.slot((l, "qstat"))
                act.activation(lrin[:, c0:], src[:, PSC + c0:], ACT.Sqrt, scale=1.0 / GW, bias=NORM_EPS)\
                    .then_inc(lr_rms.sem, 1)
                act.wait_ge(B.full((l, "kvstat")), B.use((l, "kvstat")))
                src = B.slot((l, "kvstat"))
                act.activation(ltmp[:, :], src[:, PSC:], ACT.Sqrt, scale=1.0 / P, bias=NORM_EPS).then_inc(lr_rms.sem, 1)
                for w, nb in enumerate((4, 2)):
                    act.wait_ge(A.full((l, "v", w)), A.use((l, "v", w)))
                    src = A.slot((l, "v", w))
                    cp(v_tok[:, 4 * w:4 * w + nb, :], src[:, 0:GW * nb]).then_inc(A.free((l, "v", w)), 1)

                def head_operands(h):
                    act.wait_ge(A.full((l, "qh", h)), A.use((l, "qh", h)))
                    src = A.slot((l, "qh", h))
                    cp(qT[0:QD, h % 2, c0:], src[0:QD, PSC + c0:]).then_inc(A.free((l, "qh", h)), 1)
                    act.wait_ge(A.full((l, "kh", h)), A.use((l, "kh", h)))
                    src = A.slot((l, "kh", h))
                    cp(kT[0:NOPE, h % 2, :], src[0:NOPE, PSC:]).then_inc(A.free((l, "kh", h)), 1)

                def softmax(i):
                    e = PSC + (CTX if au[l][i][1] < CTX // P else TOK)
                    act.wait_ge(rowmax.sem, rowmax.at[l, i])
                    act.activation(wa[:, i % 2, 0:e - PSC], psA[:, A.at[(l, "s", i)] % 2, PSC:e], ACT.Exp,
                                           scale=SCALE, bias=stat[:, 1, i:i + 1], accum_out=stat[:, 2, i:i + 1])\
                                               .then_inc(A.free((l, "s", i)), 1)

                def turned(i):
                    e = PSC + (CTX if au[l][i][1] < CTX // P else TOK)
                    if i >= 2:
                        act.wait_ge(B.full((l, "o", i - 2)), B.use((l, "o", i - 2)))
                    act.wait_ge(B.full((l, "pt", i)), B.use((l, "pt", i)))
                    src = B.slot((l, "pt", i))
                    cp(wb[:, i % 2, 0:e - PSC], src[:, PSC:e]).then_inc(B.free((l, "pt", i)), 1)

                head_operands(0)
                for i in range(len(au[l])):
                    h = au[l][i][0]
                    if (i == 0 or au[l][i - 1][0] != h) and h + 1 < HEADS:
                        head_operands(h + 1)
                    softmax(i)
                    if i:
                        turned(i - 1)
                turned(len(au[l]) - 1)
                for i in range(2):
                    act.wait_ge(A.full((l, "att", i)), A.use((l, "att", i)))
                    src = A.slot((l, "att", i))
                    cp(H(6 + i)[:, c0:], src[:, PSC + c0:]).then_inc(y_hi.sem, 1)
                for i in range(2):
                    act.wait_ge(B.free((l, "cmean", i)), B.use((l, "cmean", i)))
                    act.activation(u_sb[:, i, c0:TOK], acc[:, i, c0:], ACT.Square).then_inc(conv_sq.sem, 1)
                for i in range(2):
                    act.wait_ge(B.full((l, "cvar", i)), B.use((l, "cvar", i)))
                    src = B.slot((l, "cvar", i))
                    act.activation(q_sb[:, i, c0:], src[:, PSC + c0:], ACT.Sqrt, scale=1.0 / 64, bias=GN_EPS)\
                        .then_inc(conv_std.sem, 1)
                for i in range(2):
                    act.wait_ge(conv_pre.sem, conv_pre.at[l, i])
                    act.activation(q_sb[:, i, c0:], acc[:, i, c0:], ACT.Tanh).then_inc(conv_th.sem, 1)
                for i in range(2):
                    act.wait_ge(A.full((l, "convp", i)), A.use((l, "convp", i)))
                    src = A.slot((l, "convp", i))
                    cp(H(i)[:, c0:], src[:, PSC + c0:]).then_inc(y_hi.sem, 1)
                for i in range(2):
                    act.wait_ge(A.full((l, "poolp", i)), A.use((l, "poolp", i)))
                    src = A.slot((l, "poolp", i))
                    act.activation(H(4 + i)[:, c0:], src[:, PSC + c0:], ACT.Identity, scale=V(l, "psc", i))\
                        .then_inc(y_hi.sem, 1)
                act.wait_ge(A.free((l, "poolp", 1)), A.use((l, "poolp", 1)))
                act.wait_ge(z_mixed.sem, z_mixed.at[l, z_order[-1]])
                act.activation(zt[:, 5, :], zt[:, 5, :], ACT.Tanh).then_inc(l_lora.sem, 1)
                act.activation(zt[:, 4, c0:], zt[:, 4, c0:], ACT.Tanh, scale=0.5).then_inc(g_th.sem, 1)
                for j in range(2):
                    if j:
                        act.wait_ge(prep.sem, prep.at[l, 0, 1])
                    act.activation(nkk[:, :], zt[:, 2 + j, :], ACT.Square, scale=V(l, "kk", j)).then_inc(kk_sq.sem, 1)
                    act.wait_ge(B.full((l, "kk", j)), B.use((l, "kk", j)))
                    src = B.slot((l, "kk", j))
                    act.activation(nkk[:, :], src[:, PSC:], ACT.Sqrt).then_inc(kk_std.sem, 1)
                    for d in range(2):
                        un = (l, j, d)
                        act.wait_ge(A.full((un, "w2")), A.use((un, "w2")))
                        src = A.slot((un, "w2"))
                        act.activation(b[:, 0, :], src[:, PSC:], ACT.Tanh, scale=0.5, bias=DR("hw0", 2 * d + j))\
                            .then_inc(A.free((un, "w2")), 1)
                        act.wait_ge(A.full((un, "a2")), A.use((un, "a2")))
                        src = A.slot((un, "a2"))
                        act.activation(b45[:, 0, :], src[:, PSC:], ACT.Tanh, scale=0.5, bias=DR("ha0", 2 * d + j))\
                            .then_inc(A.free((un, "a2")), 1)
                        if d == 0:
                            for w, (m0, m1) in enumerate(((0, 7), (7, 13))):
                                act.wait_ge(B.full((l, j, "v", w)), B.use((l, j, "v", w)))
                                src = B.slot((l, j, "v", w)).rearrange("p (m n) -> p m n", n=P)
                                e = min(m1, NC)
                                cp(UV[64:, m0:e, 0:HD], src[64:, 0:e - m0, 0:HD])
                                s_ = max(m0, 1)
                                cp(UV[0:64, s_ - 1:m1 - 1, HD:], src[0:64, s_ - m0:m1 - m0, HD:]).then_inc(v_tp.sem, 1)
                        act.wait_ge(cum.sem, cum.at[un])
                        act.activation(b[:, 2, :], b[:, 1, :], ACT.Exp, scale=C1).then_inc(exps.sem, 1)
                        act.activation(b[:, 3, :], b[:, 1, :], ACT.Exp, scale=-C1).then_inc(exps.sem, 1)
                        act.wait_ge(dk.sem, dk.at[un])
                        act.activation(b[:, 0, :], b[:, 0, :], ACT.Exp, scale=C1).then_inc(exps.sem, 1)
                        for w in range(2):
                            act.wait_ge(B.full((un, "bkt", w)), B.use((un, "bkt", w)))
                            src = B.slot((un, "bkt", w))
                            k = min(8, NC - 8 * w)
                            cp(BKt[:, 8 * w:8 * w + k, :], src[:, 0:P * k]).then_inc(B.free((un, "bkt", w)), 1)
                        act.wait_ge(A.free((un, "gram", 2)), A.use((un, "gram", 2)))
                        cp(LTd[0:64, :, 0, :], LT[0:64, :, :])
                        cp(LTd[64:, :, 1, :], LT[64:, :, :]).then_inc(ltd.sem, 1)
                        act.wait_ge(xt_one.sem, xt_one.at[un])
                        cp(XTd[0:64, :, 0, :], XT[0:64, :, :])
                        cp(XTd[64:, :, 1, :], XT[64:, :, :]).then_inc(xt_diag.sem, 1)
                        for i in range(1, 6):
                            act.wait_ge(A.full((un, "t", i)), A.use((un, "t", i)))
                            src = chunks(A.slot((un, "t", i))[:, PSC:])
                            cp(Tc[:, :, :], src).then_inc(t_c.sem, 1)
                            cp(Td[0:64, :, 0, :], src[0:64])
                            cp(Td[64:, :, 1, :], src[64:]).then_inc(A.free((un, "t", i)), 1)
                    act.wait_ge(B.free((l, j, "mean")), B.use((l, j, "mean")))
                    act.activation(b[:, 0, c0:], Y[:, c0:], ACT.Square).then_inc(rw_sq.sem, 1)
                    act.wait_ge(B.full((l, j, "var")), B.use((l, j, "var")))
                    src = B.slot((l, j, "var"))
                    act.activation(b[:, 2, c0:], src[:, PSC + c0:], ACT.Sqrt, scale=1.0 / 64, bias=LNX_EPS)\
                        .then_inc(rw_std.sem, 1)
                    act.wait_ge(A.free((l, j, "gate")), A.use((l, j, "gate")))
                    cp(H(2 + j)[:, c0:], Y[:, c0:]).then_inc(y_hi.sem, 1)
                for m in range(KT):
                    ahead(n, (l, "out", m))
                    n += 1
                norm((l, 2), c0, lambda k: act.wait_ge(A.free((l, "out", k)), A.use((l, "out", k))))
                operand_hi((l, 2), c0)

                def group(g0, g, end):
                    for j in range(UPG):
                        key, nj = (l, "mlp", g0, j), n + UPG * g0 + j
                        done = 8 * (l * GROUPS + g0) + j + 1
                        act.wait_ge(A.full(key), A.use(key) + 8 * g)
                        src = A.slot(key)
                        if j < 8:
                            if j >= 2:
                                act.wait_ge(A.free((l, "mlp", g0, j - 2)), A.use((l, "mlp", g0, j - 2)) + 8 * g)
                            act.activation(relu[:, j % 2, c0:], src[:, PSC + c0:], ACT.Relu).then_inc(relu_ready, 1)
                        if not (end and j >= UPG - SPL):
                            split_hi(nj + SPL, i_plus=16 * (LOOP[l] // RAW) * g)
                        if j < 8:
                            act.wait_ge(A.free(key), A.use(key) + 8 * g)
                            cp(hid_hi[:, j, c0:], hsq[:, j % 2, c0:]).then_inc(hid_hi_ready, 1)

                if l == 0:
                    with act.Fori(0, GROUPS) as g:
                        group(0, g, False)
                else:
                    with act.Fori(0, GROUPS - 1) as g:
                        group(0, g, False)
                    group(GROUPS - 1, 0, True)
                n += UPG * GROUPS
            norm((DEPTH, 0), CTX, lambda k: act.wait_ge(A.free((1, "mlp", GROUPS - 1, 8 + k)),
                                                       A.use((1, "mlp", GROUPS - 1, 8 + k))))

        @block.vector
        def _(dve):
            step = Steps()
            tt, ts, stt = dve.tensor_tensor, dve.tensor_scalar, dve.scalar_tensor_tensor

            def derive(l):
                stt(DR("c0", 0, 9), V(l, "mup", 0, 9), -1.0, V(l, "mun", 0, 9), ALU.mult, ALU.subtract)
                ts(DR("hw0", 0, 4), V(l, "w0", 0, 4), 0.5, None, ALU.mult)
                ts(DR("ha0", 0, 4), V(l, "a0", 0, 4), 0.5, None, ALU.mult)
                ts(DR("nkk", 0, 2), V(l, "kk", 0, 2), -1.0, None, ALU.mult)
                ts(DR("s1", 0, 2), V(l, "ka", 0, 2), 0.5, None, ALU.mult)
                ts(DR("s2", 0, 2), V(l, "ka", 0, 2), -0.5, 1.0, ALU.mult, ALU.add)
                ts(DR("hg", 0, 2), V(l, "cgg", 0, 2), 0.5, None, ALU.mult)
                ts(DR("hb", 0, 2), V(l, "cgb", 0, 2), 0.5, None, ALU.mult).then_inc(vector_step, step.up())
                dve.wait_ge(vector_step, step.n)
                ts(DR("c0", 0, 9), DR("c0", 0, 9), 1.0, None, ALU.add).then_inc(der_ready.sem, 1)

            def modulations(l, key, t0, t1):
                dve.wait_ge(B.full(key), B.use(key))
                src = B.slot(key)[:, 0:2 * (t1 - t0)].rearrange("p (t s) -> p t s", s=2)
                tt(mods[:, l, t0:t1, :], src, bc(V(l, "ada_b", t0, t1 - t0), [P, t1 - t0, 2], 2), ALU.add)\
                    .then_inc(B.free(key), 1)
                dve.wait_ge(B.free(key), B.use(key))

            def gains(l, name, scale, g):
                o = DR(name, 0, 16).rearrange("p (t s) -> p t s", s=2)
                stt(o, mods[:, l, 8 * scale:8 * scale + 8, :], 1.0, bc(V(l, g, 0, 8), [P, 8, 2], 2), ALU.add, ALU.mult)\
                    .then_inc(vector_step, step.up())
                dve.wait_ge(vector_step, step.n)

            def norm(key, c0, name, shift):
                l = key[0]
                dve.wait_ge(rms.sem, rms.at[key])
                dve.reciprocal(rinv[:, c0:], rinv[:, c0:]).then_inc(B.free(("norm", key)), 1)
                dve.wait_ge(B.free(("norm", key)), B.use(("norm", key)))
                for k in range(KT):
                    if k >= 2:
                        dve.wait_ge(act_lo.sem, act_lo.at[key, k - 2])
                    tt(tb[:, k % 2, c0:], x[:, k, c0:], rinv[:, c0:], ALU.mult).then_inc(vector_step, step.up())
                    dve.wait_ge(vector_step, step.n)
                    for s_, t0, tn in reversed(segs(c0)):
                        i = ts(hb[:, k % 2, t0:t0 + tn], tb[:, k % 2, t0:t0 + tn], DR(name, 2 * k + s_),
                               mods[:, l, 8 * shift + k, s_:s_ + 1], ALU.mult, ALU.add)
                    i.then_inc(mod_ready.sem, 1)

            def add_gated(l, src, m, gate, c0, key):
                for s_, t0, tn in reversed(segs(c0)):
                    i = stt(x[:, m, t0:t0 + tn], src[:, PSC + t0:PSC + t0 + tn], mods[:, l, 8 * gate + m, s_:s_ + 1],
                            x[:, m, t0:t0 + tn], ALU.mult, ALU.add)
                i.then_inc(A.free(key), 1)

            def masked_copy(o, mask, src):
                return dve.copy_predicated(o, mask.bitcast(U32).unsqueeze(1).to_broadcast(list(o.shape)), src)

            turned = []
            dve.wait_ge(c_in, 48)
            dve.wait_ge(cond_th, 1)
            stt(mods[:, 1, 8:16, :], mods[:, 1, 0:8, :], 1.0, cond[:, :, :], ALU.add, ALU.mult)\
                .then_inc(vector_step, step.up())
            dve.wait_ge(vector_step, step.n)
            ts(cond[:, :, :], mods[:, 1, 8:16, :], 0.5, None, ALU.mult).then_inc(cond_ready, 1)
            for l in ls:
                c0 = first(l)
                derive(l)
                if l == 0:
                    modulations(0, ("ada", 0, 0), 0, 16)
                gains(l, "A1", 1, "n1")
                norm((l, 1), 0, "A1", 0)
                if l == 1:
                    dve.wait_ge(x_kept, 16)
                nz = 0
                for name, i in (u[0] for u in IN_UNITS):
                    key = (l, name, i)
                    if name == "z":
                        dve.wait_ge(A.free(key), A.use(key))
                        z, p = z_of(i), wa[:, nz % 2, :]
                        for o, s_, t in ((1, 0, CTX - 1), (CTX + 1, CTX, LAT - 1)):
                            k = stt(z[:, o:o + t], p[:, s_:s_ + t], V(l, "mup", i), z[:, o:o + t], ALU.mult, ALU.add)
                        k.then_inc(vector_step, step.up())
                        nz += 1
                        dve.wait_ge(vector_step, step.n)
                        for o, s_, t in ((0, 1, CTX - 1), (CTX, CTX + 1, LAT - 1)):
                            k = stt(z[:, o:o + t], p[:, s_:s_ + t], V(l, "mun", i), z[:, o:o + t], ALU.mult, ALU.add)
                        k.then_inc(z_mixed.sem, 1)
                    elif name == "cg":
                        dve.wait_ge(A.free(key), A.use(key))
                        ts(wb[:, i, c0:], wb[:, i, c0:], 0.5, 0.5, ALU.mult, ALU.add).then_inc(vector_step, step.up())
                    elif name == "cv":
                        dve.wait_ge(A.full(key), A.use(key))
                        src = A.slot(key)
                        if i == 0:
                            dve.wait_ge(pads.sem, pads.at[(l,)])
                            dve.wait_ge(vector_step, step.n)
                        if l == 0:
                            tt(u_sb[:, i, 15:15 + CTX], src[:, PSC:PSC + CTX], wb[:, i, 0:CTX], ALU.mult)
                        tt(u_sb[:, i, UL:UL + LAT], src[:, PSC + CTX:], wb[:, i, CTX:], ALU.mult)\
                            .then_inc(A.free(key), 1)
                if l == 0:
                    modulations(0, ("ada", 0, 1), 16, 48)

                dve.wait_ge(lr_rms.sem, lr_rms.at[l, 0])
                dve.reciprocal(lrin[:, c0:], lrin[:, c0:]).then_inc(B.free((l, "qstat")), 1)
                dve.wait_ge(B.free((l, "qstat")), B.use((l, "qstat")))
                for i in range(2):
                    q = stt(q_sb[:, i, c0:], q_sb[:, i, c0:], V(l, "qn", i), lrin[:, c0:], ALU.mult, ALU.mult)
                q.then_inc(lr_normed.sem, 1)
                dve.wait_ge(lr_rms.sem, lr_rms.at[l, 1])
                dve.reciprocal(ltmp[:, :], ltmp[:, :]).then_inc(B.free((l, "kvstat")), 1)
                dve.wait_ge(B.free((l, "kvstat")), B.use((l, "kvstat")))
                stt(ckv[:, :], ckv[:, :], V(l, "kvn"), ltmp[:, :], ALU.mult, ALU.mult).then_inc(lr_normed.sem, 1)
                dve.wait_ge(mix_in, 48 * (l + 1))

                def rotate(key, o, signal, skey):
                    dve.wait_ge(B.full(key), B.use(key))
                    src = B.slot(key)
                    if turned:
                        dve.wait_ge(turned[-1][0].sem, turned[-1][0].at[turned[-1][1]])
                    turned.append((signal, skey))
                    tt(rtmp[rp, :], src[rp, PSC + CTX:], cs[rp, 1, :], ALU.mult).then_inc(B.free(key), 1)
                    tt(o, o, cs[rp, 0, :], ALU.mult).then_inc(vector_step, step.up())
                    dve.wait_ge(vector_step, step.n)
                    dve.wait_ge(B.free(key), B.use(key))
                    tt(o, o, rtmp[rp, :], ALU.add).then_inc(signal.sem, 1)

                rotate((l, "krot"), krope[rp, CTX:], kr_ready, (l,))

                span0, width = (0, CTX + 15 + LAT) if l == 0 else (UL - 15, LAT)
                ctap = u_acc
                taps = [(t, i) for t in range(TAPS) for i in range(2)]
                done_taps = [0]
                marks = {}

                def tap(count):
                    for _ in range(count):
                        if done_taps[0] >= len(taps):
                            return
                        t, i = taps[done_taps[0]]
                        done_taps[0] += 1
                        w = V(l, "dw", 2 * t + i)
                        u = u_sb[:, i, span0 + t:span0 + t + width]
                        o = ctap[:, i, 0:width]
                        if t == 0:
                            if i == 0:
                                dve.wait_ge(A.free((l, "cv", 0)), A.use((l, "cv", 0)))
                                dve.wait_ge(A.free((l, "cv", 1)), A.use((l, "cv", 1)))
                            k = ts(o, u, w, V(l, "db", i), ALU.mult, ALU.add)
                        else:
                            dve.wait_ge(vector_step, marks[i])
                            k = stt(o, u, w, o, ALU.mult, ALU.add)
                        k.then_inc(vector_step, step.up())
                        marks[i] = step.n

                def head_rotation(h):
                    dve.wait_ge(A.free((l, "qh", h)), A.use((l, "qh", h)))
                    rotate((l, "qrot", h), qT[rp, h % 2, CTX:], q_rot, (l, h))

                def maxima(i):
                    e = PSC + (CTX if au[l][i][1] < CTX // P else TOK)
                    dve.wait_ge(A.full((l, "s", i)), A.use((l, "s", i)))
                    src = A.slot((l, "s", i))
                    dve.tensor_reduce(stat[:, 0, i:i + 1], src[:, PSC:e], AX_X, ALU.max, negate=True)\
                        .then_inc(vector_step, step.up())
                    dve.wait_ge(vector_step, step.n)
                    ts(stat[:, 1, i:i + 1], stat[:, 0, i:i + 1], SCALE, None, ALU.mult).then_inc(rowmax.sem, 1)

                def mixed(i):
                    h, q = au[l][i]
                    dve.wait_ge(A.free((l, "s", i)), A.use((l, "s", i)))
                    dve.reciprocal(stat[:, 3, i:i + 1], stat[:, 2, i:i + 1]).then_inc(vector_step, step.up())
                    dve.wait_ge(vector_step, step.n)
                    dve.wait_ge(B.full((l, "o", i)), B.use((l, "o", i)))
                    src = B.slot((l, "o", i))
                    ts(otok[:, q, HD * h:HD * (h + 1)], src[:, 0:HD], stat[:, 3, i:i + 1], None, ALU.mult)\
                        .then_inc(B.free((l, "o", i)), 1)

                head_rotation(0)
                per = -(-len(taps) // len(au[l]))
                for i in range(len(au[l])):
                    h = au[l][i][0]
                    if (i == 0 or au[l][i - 1][0] != h) and h + 1 < HEADS:
                        head_rotation(h + 1)
                    maxima(i)
                    tap(per)
                    if i:
                        mixed(i - 1)
                mixed(len(au[l]) - 1)

                def low_part(k, key, ykey, scale=None):
                    dve.wait_ge(y_hi.sem, y_hi.at[ykey])
                    src = psA[:, A.at[key] % 2, PSC + c0:]
                    if scale is None:
                        i = tt(L(k)[:, c0:], src, f32(H(k))[:, c0:], ALU.subtract)
                    else:
                        i = stt(L(k)[:, c0:], src, scale, f32(H(k))[:, c0:], ALU.mult, ALU.subtract)
                    i.then_inc(A.free(key), 1)

                for i in range(2):
                    low_part(6 + i, (l, "att", i), (l, "att", i))
                dve.wait_ge(vector_step, step.n)
                for i in range(2):
                    if l == 0:
                        ts(acc[:, i, 0:CTX], ctap[:, i, 0:CTX], 1.0, None, ALU.mult)
                        o = CTX + 15
                    else:
                        o = 0
                    ts(acc[:, i, CTX:], ctap[:, i, o:o + LAT], 1.0, None, ALU.mult).then_inc(conv_sum.sem, 1)
                for i in range(2):
                    dve.wait_ge(B.full((l, "cmean", i)), B.use((l, "cmean", i)))
                    src = B.slot((l, "cmean", i))
                    dve.wait_ge(conv_sum.sem, conv_sum.at[l, i])
                    stt(acc[:, i, c0:], src[:, PSC + c0:], -1.0 / 64, acc[:, i, c0:], ALU.mult, ALU.add)\
                        .then_inc(B.free((l, "cmean", i)), 1)
                for i in range(2):
                    dve.wait_ge(conv_std.sem, conv_std.at[l, i])
                    dve.reciprocal(q_sb[:, i, c0:], q_sb[:, i, c0:]).then_inc(B.free((l, "cvar", i)), 1)
                    dve.wait_ge(B.free((l, "cvar", i)), B.use((l, "cvar", i)))
                    tt(acc[:, i, c0:], acc[:, i, c0:], q_sb[:, i, c0:], ALU.mult).then_inc(vector_step, step.up())
                    dve.wait_ge(vector_step, step.n)
                    ts(acc[:, i, c0:], acc[:, i, c0:], DR("hg", i), DR("hb", i), ALU.mult, ALU.add)\
                        .then_inc(conv_pre.sem, 1)
                for i in range(2):
                    dve.wait_ge(conv_th.sem, conv_th.at[l, i])
                    stt(acc[:, i, c0:], q_sb[:, i, c0:], 1.0, acc[:, i, c0:], ALU.add, ALU.mult)\
                        .then_inc(conv_act.sem, 1)
                for i in range(2):
                    low_part(i, (l, "convp", i), (l, "conv", i))
                for i in range(2):
                    low_part(4 + i, (l, "poolp", i), (l, "pool", i), V(l, "psc", i))

                dve.wait_ge(rw_in, 32 * (l + 1))
                dve.wait_ge(g_th.sem, g_th.at[(l,)])
                ts(zt[:, 4, c0:], zt[:, 4, c0:], 0.5, 0.5, ALU.mult, ALU.add).then_inc(vector_step, step.up())
                for j in range(2):
                    dve.wait_ge(kk_std.sem, kk_std.at[l, j])
                    ts(nkk[:, :], nkk[:, :], 1e-12, None, ALU.max).then_inc(B.free((l, "kk", j)), 1)
                    dve.wait_ge(B.free((l, "kk", j)), B.use((l, "kk", j)))
                    dve.reciprocal(nkk[:, :], nkk[:, :]).then_inc(vector_step, step.up())
                    dve.wait_ge(vector_step, step.n)
                    stt(nkk[:, :], zt[:, 2 + j, :], DR("nkk", j), nkk[:, :], ALU.mult, ALU.mult)\
                        .then_inc(vector_step, step.up())
                    for d in range(2):
                        un = (l, j, d)
                        dve.wait_ge(A.free((un, "w2")), A.use((un, "w2")))
                        ts(b[:, 0, :], b[:, 0, :], 1.0, None, ALU.add).then_inc(vector_step, step.up())
                        dve.wait_ge(vector_step, step.n)
                        way = slice(None) if d == 0 else slice(None, None, -1)
                        dve.tensor_tensor_scan(b[:, 1, way], reset[:, d, way], b[:, 0, way], 0.0, ALU.mult,
                                                        ALU.add).then_inc(cum.sem, 1)
                        dve.wait_ge(cum.sem, cum.at[un])
                        tt(b[:, 0, :], b[:, 1, :], b[:, 0, :], ALU.subtract).then_inc(dk.sem, 1)
                        dve.wait_ge(A.free((un, "a2")), A.use((un, "a2")))
                        ts(b45[:, 1, :], b45[:, 0, :], -0.5, -0.5, ALU.mult, ALU.add).then_inc(vector_step, step.up())
                        dve.wait_ge(vector_step, step.n)
                        ts(b45[:, 0, :], b45[:, 0, :], DR("s1", j), DR("s2", j), ALU.mult, ALU.add)\
                            .then_inc(vector_step, step.up())
                        dve.wait_ge(vector_step, step.n)
                        tt(b45[:, 1, :], b45[:, 1, :], nkk[:, :], ALU.mult)
                        tt(b45[:, 0, :], b45[:, 0, :], zt[:, 2 + j, :], ALU.mult).then_inc(vector_step, step.up())
                        dve.wait_ge(vector_step, step.n)
                        if d == 0:
                            ts(kds[:, :], b45[:, 0, :], 1.0, None, ALU.mult)
                            for w, (m0, m1) in enumerate(((0, 7), (7, 13))):
                                dve.wait_ge(v_tp.sem, v_tp.at[l, j, w])
                                src = psB[:, B.at[(l, j, "v", w)] % 2, :].rearrange("p (m n) -> p m n", n=P)
                                e = min(m1, NC)
                                ts(SV[64:, m0:e, 0:HD], src[64:, 0:e - m0, 0:HD], 1.0, None, ALU.mult)
                                s_ = max(m0, 1)
                                ts(SV[0:64, s_ - 1:m1 - 1, HD:], src[0:64, s_ - m0:m1 - m0, HD:], 1.0, None,
                                           ALU.mult).then_inc(B.free((l, j, "v", w)), 1)
                        else:
                            tt(kds[:, :], kds[:, :], b45[:, 0, :], ALU.add)
                        dve.wait_ge(exps.sem, exps.at[un, 1])
                        for part, s_ in HALF:
                            tt(BK[part, :, s_, :], chunks(b45[part, 1, :]), chunks(b[part, 3, :]), ALU.mult)
                            tt(BK[part, :, 1 - s_, :], chunks(b45[part, 0, :]), chunks(b[part, 3, :]), ALU.mult)
                            tt(Q[part, 2 * s_ + 1, :], zt[part, j, :], b[part, 2, :], ALU.mult)
                        end = C - 1 if d == 0 else 0
                        ts(PC[:, :], chunks(b[:, 2, :])[:, :, end], 1.0, None, ALU.mult)
                        dve.wait_ge(exps.sem, exps.at[un, 2])
                        for part, s_ in HALF:
                            k = tt(Q[part, 2 * s_, :], nkk[part, :], b[part, 0, :], ALU.mult)
                        k.then_inc(prep.sem, 1)
                        dve.wait_ge(prep.sem, prep.at[un])
                        tri = lambda incl: K("tri", C, (2 * d + incl) * C)
                        for g in range(3):
                            dve.wait_ge(A.full((un, "gram", g)), A.use((un, "gram", g)))
                            src = A.slot((un, "gram", g)).rearrange("p (h c n) -> p h c n", h=2, n=P)
                            tt(M[:, :, 4 * g:4 * g + 4, :], src[:, :, :, C:],
                               bc(tri(1), [P, 1, C], 1).unsqueeze(1).to_broadcast([P, 2, 4, C]), ALU.mult)
                            for part, s_ in HALF:
                                other = HALF[1 - s_][0]
                                mask = lambda p_: tri(0)[p_].unsqueeze(1).to_broadcast([64, 4, C])
                                tt(chunks(Q[other, 2 * s_, :])[:, 4 * g:4 * g + 4, :], src[other, s_, :, 0:C], mask(other),
                                   ALU.mult)
                                k = tt(LT[part, 4 * g:4 * g + 4, :], src[part, s_, :, 0:C], mask(part), ALU.mult)
                            k.then_inc(A.free((un, "gram", g)), 1)
                        lo = lambda i: K("lo" if d == 0 else "up", C, i * C)
                        up = lambda i: K("up" if d == 0 else "lo", C, i * C)
                        m3 = lambda m: m.unsqueeze(1).to_broadcast([P, NC, C])
                        dve.wait_ge(A.free((un, "gram", 2)), A.use((un, "gram", 2)))
                        tt(XT[:, :, :], LT[:, :, :], m3(up(0)), ALU.mult).then_inc(vector_step, step.up())
                        dve.wait_ge(vector_step, step.n)
                        tt(XT[:, :, :], XT[:, :, :], m3(K("istack", C)), ALU.add).then_inc(xt_one.sem, 1)
                        dve.wait_ge(A.full((un, "t", 0)), A.use((un, "t", 0)))
                        src = chunks(A.slot((un, "t", 0))[:, PSC:])
                        tt(X[:, :, :], src, m3(lo(0)), ALU.mult).then_inc(A.free((un, "t", 0)), 1)
                        dve.wait_ge(A.free((un, "t", 0)), A.use((un, "t", 0)))
                        tt(X[:, :, :], X[:, :, :], m3(K("istack", C)), ALU.add).then_inc(x_one.sem, 1)
                        for i in range(1, 6):
                            if i < 5:
                                dve.wait_ge(B.full((un, "x", i)), B.use((un, "x", i)))
                                src = chunks(B.slot((un, "x", i))[:, PSC:])
                                masked_copy(X[:, :, :], lo(i), src).then_inc(B.free((un, "x", i)), 1)
                            dve.wait_ge(B.full((un, "xt", i)), B.use((un, "xt", i)))
                            src = chunks(B.slot((un, "xt", i))[:, PSC:])
                            if i < 5:
                                masked_copy(XT[:, :, :], up(i), src)
                            for part, s_ in HALF:
                                k = masked_copy(XTd[part, :, s_, :], up(i)[part], src[part])
                            k.then_inc(B.free((un, "xt", i)), 1)
                        order = chunk_order(d)
                        for n_, c in enumerate(order):
                            dve.wait_ge(A.full((un, "w", n_)), A.use((un, "w", n_)))
                            src = A.slot((un, "w", n_))
                            ts(Wc[:, n_ % 2, :], src[:, 0:C], 1.0, None, ALU.mult).then_inc(A.free((un, "w", n_)), 1)
                            dve.wait_ge(A.full((un, "u", n_)), A.use((un, "u", n_)))
                            src = A.slot((un, "u", n_))
                            for part, s_ in HALF:
                                k = ts(UV[part, c, HD * s_:HD * (s_ + 1)], src[part, 0:C], 1.0, None, ALU.mult)
                            k.then_inc(A.free((un, "u", n_)), 1)
                            if n_ < NC - 1:
                                dve.wait_ge(A.full((un, "s", n_)), A.use((un, "s", n_)))
                                src = A.slot((un, "s", n_))
                                dve.wait_ge(s_dec.sem, s_dec.at[un, n_])
                                for part, s_ in HALF:
                                    k = stt(SV[part, order[n_ + 1], HD * s_:HD * (s_ + 1)], src[part, 0:HD],
                                            PC[part, c:c + 1], SP[part, :], ALU.mult, ALU.add)
                                k.then_inc(A.free((un, "s", n_)), 1)
                        dve.wait_ge(B.full((un, "y")), B.use((un, "y")))
                        src = B.slot((un, "y"))[:, PSC + c0:]
                        if d == 0:
                            if j:
                                dve.wait_ge(y_lo.sem, y_lo.at[l, 0])
                            ts(Y[:, c0:], src, 1.0, None, ALU.mult).then_inc(B.free((un, "y")), 1)
                        else:
                            tt(Y[:, c0:], src, Y[:, c0:], ALU.add).then_inc(B.free((un, "y")), 1)
                    stt(b[:, 1, c0:], zt[:, j, c0:], V(l, "rk", j), kds[:, c0:], ALU.mult, ALU.mult)\
                        .then_inc(bon.sem, 1)
                    dve.wait_ge(B.full((l, j, "mean")), B.use((l, j, "mean")))
                    src = B.slot((l, j, "mean"))
                    dve.wait_ge(B.free(((l, j, 1), "y")), B.use(((l, j, 1), "y")))
                    stt(Y[:, c0:], src[:, PSC + c0:], -1.0 / 64, Y[:, c0:], ALU.mult, ALU.add)\
                        .then_inc(B.free((l, j, "mean")), 1)
                    dve.wait_ge(A.full((l, j, "bonus")), A.use((l, j, "bonus")))
                    src = A.slot((l, j, "bonus"))
                    tt(b[:, 3, c0:], src[:, PSC + c0:], zv[:, j, C + c0:C + TOK], ALU.mult)\
                        .then_inc(A.free((l, j, "bonus")), 1)
                    dve.wait_ge(rw_std.sem, rw_std.at[l, j])
                    dve.reciprocal(b[:, 2, c0:], b[:, 2, c0:]).then_inc(B.free((l, j, "var")), 1)
                    dve.wait_ge(B.free((l, j, "var")), B.use((l, j, "var")))
                    tt(Y[:, c0:], Y[:, c0:], b[:, 2, c0:], ALU.mult).then_inc(vector_step, step.up())
                    dve.wait_ge(vector_step, step.n)
                    ts(Y[:, c0:], Y[:, c0:], V(l, "lg", j), V(l, "lb", j), ALU.mult, ALU.add)\
                        .then_inc(vector_step, step.up())
                    dve.wait_ge(vector_step, step.n)
                    tt(Y[:, c0:], Y[:, c0:], b[:, 3, c0:], ALU.add).then_inc(vector_step, step.up())
                    dve.wait_ge(vector_step, step.n)
                    dve.wait_ge(A.full((l, j, "gate")), A.use((l, j, "gate")))
                    src = A.slot((l, j, "gate"))
                    tt(Y[:, c0:], src[:, PSC + c0:], Y[:, c0:], ALU.mult).then_inc(A.free((l, j, "gate")), 1)
                dve.wait_ge(x_in, 16 * (l + 2))
                for m in range(KT):
                    key = (l, "out", m)
                    dve.wait_ge(A.full(key), A.use(key))
                    add_gated(l, A.slot(key), m, 2, c0, key)
                gains(l, "A2", 4, "n2")
                norm((l, 2), c0, "A2", 3)

                def group(g0, g):
                    for j in range(UPG):
                        key = (l, "mlp", g0, j)
                        dve.wait_ge(A.full(key), A.use(key) + 8 * g)
                        src = A.slot(key)
                        done = 8 * (l * GROUPS + g0) + j + 1
                        if j < 8:
                            dve.wait_ge(relu_ready, done + 8 * g)
                            stt(hsq[:, j % 2, c0:], src[:, PSC + c0:], 0.0, relu[:, j % 2, c0:], ALU.max, ALU.mult)\
                                .then_inc(A.free(key), 1)
                            dve.wait_ge(hid_hi_ready, done + 8 * g)
                            tt(hid_lo[:, j, c0:], hsq[:, j % 2, c0:], f32(hid_hi[:, j, c0:]), ALU.subtract)\
                                .then_inc(hid_ready, 1)
                        else:
                            add_gated(l, src, j - 8, 5, c0, key)

                if l == 0:
                    with dve.Fori(0, GROUPS) as g:
                        group(0, g)
                    modulations(1, (0, "ada1"), 0, 48)
                else:
                    with dve.Fori(0, GROUPS - 1) as g:
                        group(0, g)
                    group(GROUPS - 1, 0)
            key = (DEPTH, 0)
            dve.wait_ge(rms.sem, rms.at[key])
            dve.reciprocal(rinv[:, CTX:], rinv[:, CTX:]).then_inc(B.free(("norm", key)), 1)
            dve.wait_ge(B.free(("norm", key)), B.use(("norm", key)))
            for k in range(KT):
                stt(x[:, k, CTX:], x[:, k, CTX:], vec[:, V_FINAL + k:V_FINAL + k + 1], rinv[:, CTX:],
                                   ALU.mult, ALU.mult).then_inc(fin_ready.sem, 1)

        @block.gpsimd
        def _(pool):
            step = Steps()

            def split_lo(n, plus=0, i_plus=0):
                i = unit_of_split[n]
                pool.wait_ge(w_hi, n + 1 + plus)
                pool.tensor_tensor(wlo[:, n % SPL], raw[:, i % RAW], f32(whi[:, n % SPL]), ALU.subtract)\
                    .then_inc(w_lo, 1)

            def operand_lo(key, c0):
                for k in range(KT):
                    pool.wait_ge(act_hi.sem, act_hi.at[key, k])
                    pool.tensor_tensor(L(k)[:, c0:], hb[:, k % 2, c0:], f32(H(k))[:, c0:], ALU.subtract)\
                        .then_inc(act_lo.sem, 1)

            n = 0
            split_lo(0)
            split_lo(1)
            for l in ls:
                c0 = first(l)
                operand_lo((l, 1), 0)
                pool.wait_ge(act_lo.sem, act_lo.at[(l, 1), KT - 1])
                if l == 1:
                    pool.wait_ge(x_kept, 16)
                pool.memset(u_sb[:, :, :], 0.0)
                pool.memset(zv[:, :, :], 0.0)
                pool.memset(pp[:, :, :], 0.0).then_inc(pads.sem, 1)
                for i in range(N_IN):
                    split_lo(n + SPL)
                    n += 1
                pool.wait_ge(pads.sem, pads.at[(l,)])
                pool.wait_ge(mix_in, 48 * (l + 1))
                for i in range(2):
                    pool.wait_ge(A.free((l, "pool", i)), A.use((l, "pool", i)))
                for i in range(2):
                    cur, buf = pp[:, i, :], ps[:, i, :]
                    pool.tensor_tensor(buf[:, 1:PWID], cur[:, 0:PWID - 1], cur[:, 1:PWID], ALU.add)\
                        .then_inc(pool_step, step.up())
                    widths = ((2, 4), (8, 16))[i]
                    w, src, dst = 2, buf, ptmp[:, :]
                    for part, want in ((slice(0, 64), widths[0]), (slice(64, P), widths[1])):
                        while w < want:
                            h = w // 2
                            pool.wait_ge(pool_step, step.n)
                            pool.tensor_tensor(dst[:, w:PWID - w], src[:, w - h:PWID - w - h], src[:, w + h:PWID - w + h],
                                                    ALU.add).then_inc(pool_step, step.up())
                            src, dst, w = dst, src, 2 * w
                        pool.wait_ge(pool_step, step.n)
                        for s_, t0, tn in segs(c0):
                            o = PL if s_ == 0 else 8
                            pool.tensor_tensor(rcnt[part, i, t0:t0 + tn], src[part, o:o + tn], rcnt[part, i, t0:t0 + tn],
                                                    ALU.mult).then_inc(pool_step, step.up())
                    pool.wait_ge(pool_step, step.n)
                    for s_, t0, tn in segs(c0):
                        o = PL if s_ == 0 else 8
                        k = pool.tensor_tensor(rcnt[:, i, t0:t0 + tn], rcnt[:, i, t0:t0 + tn], cur[:, o:o + tn], ALU.subtract)
                    k.then_inc(pool_d.sem, 1)
                    pool.wait_ge(pool_d.sem, pool_d.at[l, i])
                pool.wait_ge(kr_ready.sem, kr_ready.at[(l,)])
                for h in hs:
                    if h >= 2:
                        last = max(i for i, (hh_, _) in enumerate(au[l]) if hh_ == h - 2)
                        pool.wait_ge(A.full((l, "s", last)), A.use((l, "s", last)))
                    pool.tensor_copy(kT[rp, h % 2, :], krope[rp, :]).then_inc(k_full.sem, 1)
                pool.wait_ge(A.free((l, "poolp", 1)), A.use((l, "poolp", 1)))
                pool.wait_ge(k_full.sem, k_full.at[l, HEADS - 1])
                pool.memset(Q[64:, 1, :], 0.0)
                pool.memset(Q[0:64, 3, :], 0.0).then_inc(pool_step, step.up())
                pool.wait_ge(pool_step, step.n)
                pool.memset(XTd[:, :, :, :], 0.0)
                pool.memset(LTd[:, :, :, :], 0.0)
                pool.memset(Td[:, :, :, :], 0.0).then_inc(rw_zero.sem, 1)
                for j in range(2):
                    for d in range(2):
                        un = (l, j, d)
                        order = chunk_order(d)
                        if (j, d) != (0, 0):
                            y_before = ((l, j, 0) if d else (l, 0, 1), "y")
                            pool.wait_ge(B.free(y_before), B.use(y_before))
                        else:
                            pool.wait_ge(rw_zero.sem, rw_zero.at[(l,)])
                        pool.memset(SV[0:64, order[0], 0:HD], 0.0)
                        pool.memset(SV[64:, order[0], HD:], 0.0).then_inc(s_zero.sem, 1)
                        pool.wait_ge(prep.sem, prep.at[un])
                        pool.wait_ge(s_zero.sem, s_zero.at[un])
                        for n_, c in enumerate(order[:-1]):
                            if n_:
                                pool.wait_ge(A.free((un, "s", n_ - 1)), A.use((un, "s", n_ - 1)))
                            for part, s_ in HALF:
                                k = pool.tensor_scalar(SP[part, :], SV[part, c, HD * s_:HD * (s_ + 1)], PC[part, c:c + 1],
                                                       0.0, ALU.mult, ALU.add)
                            k.then_inc(s_dec.sem, 1)
                    pool.wait_ge(s_dec.sem, s_dec.at[(l, j, 1), NC - 2])
                    pool.wait_ge(y_hi.sem, y_hi.at[l, "rw", j])
                    pool.tensor_tensor(L(2 + j)[:, c0:], Y[:, c0:], f32(H(2 + j))[:, c0:], ALU.subtract)\
                        .then_inc(y_lo.sem, 1)
                    pool.wait_ge(y_lo.sem, y_lo.at[l, j])
                for m in range(KT):
                    split_lo(n + SPL)
                    n += 1
                operand_lo((l, 2), c0)

                def group(g0, g, end):
                    for j in range(UPG - (SPL if end else 0)):
                        split_lo(n + UPG * g0 + j + SPL, UPG * g)

                if l == 0:
                    with pool.Fori(0, GROUPS) as g:
                        group(0, g, False)
                else:
                    with pool.Fori(0, GROUPS - 1) as g:
                        group(0, g, False)
                    group(GROUPS - 1, 0, True)
                n += UPG * GROUPS

        @block.sync
        def _(sp):
            def load(i, plus_lo=0, plus_ada=0, at=None, plus=0):
                if i >= RAW:
                    before = i - RAW
                    if before in split_no:
                        sp.wait_ge(w_lo, split_no[before] + 1 + plus_lo)
                    else:
                        sp.wait_ge(ada_used, ada_no[before] + 1 + plus_ada)
                src = stream[i] if at is None else stream[bass.ds(at, 1)].rearrange("a p n -> (a p) n")
                sp.dma_start(raw[:, i % RAW], src.rearrange("p (k m) -> p k m", k=KT)).then_inc(w_in[i % RAW], 16)

            sp.dma_start(cond[:, :, :], cond_in).then_inc(c_in, 16)
            sp.dma_start(cst[:, :], consts).then_inc(c_in, 16)
            sp.dma_start(vec[:, :], vecs).then_inc(c_in, 16)
            for i in range(RAW):
                load(i)
            sp.dma_start(x[:, :, :], xT).then_inc(x_in, 16)
            n = RAW
            for l in ls:
                first_in = 16 if l == 0 else mlp0[0] + LOOP[0] * GROUPS
                while n < first_in + RAW:
                    load(n)
                    n += 1
                if l == 1:
                    sp.wait_ge(A.free((0, "mlp", 0, 15)), A.use((0, "mlp", 0, 15)) + 8 * (GROUPS - 1))
                    sp.wait_ge(A.free((0, "mlp", 0, 14)), A.use((0, "mlp", 0, 14)) + 8 * (GROUPS - 1))
                    sp.dma_start(kept, x[:, :, CTX:]).then_inc(x_kept, 16)
                sp.wait_ge(act_lo.sem, act_lo.at[(l, 1), KT - 1])
                if l == 1:
                    sp.wait_ge(x_kept, 16)
                sp.dma_start(cs[:, :, :], big[:, BIG["cos"]:BIG["cos"] + 2 * LAT].rearrange("p (a n) -> p a n", a=2))\
                    .then_inc(mix_in, 16)
                sp.dma_start(rcnt[:, :, :], big[:, BIG["rcnt"]:].rearrange("p (a n) -> p a n", a=2))\
                    .then_inc(mix_in, 16)
                sp.dma_start(sw_a[:, :], small_a[l]).then_inc(mix_in, 16)
                while n < mlp0[l] - 8 + RAW:
                    load(n)
                    n += 1
                sp.wait_ge(A.free((l, "poolp", 1)), A.use((l, "poolp", 1)))
                sp.dma_start(reset[:, :, :], big[:, 0:2 * TOK].rearrange("p (a n) -> p a n", a=2)).then_inc(rw_in, 16)
                sp.dma_start(sw_r[:, :], small_r[l]).then_inc(rw_in, 16)
                sp.wait_ge(y_lo.sem, y_lo.at[l, 1])
                if l == 0:
                    sp.dma_start(x[:, :, :], xT).then_inc(x_in, 16)
                else:
                    sp.dma_start(x[:, :, CTX:], kept).then_inc(x_in, 16)
                while n < mlp0[l]:
                    load(n)
                    n += 1
                per = LOOP[l]
                with sp.Fori(0, GROUPS) as g:
                    for i in range(per):
                        load(mlp0[l] + i, UPG * g, 12 * g, mlp0[l] + i + per * g)
                n = mlp0[l] + per * GROUPS
            for k in range(KT):
                sp.wait_ge(fin_ready.sem, fin_ready.at[(k,)])
                sp.dma_start(out[:, k, :], x[:, k, CTX:]).then_inc(out_done, 16)
            sp.wait_ge(out_done, 16 * KT)


def _tables():
    c = np.zeros((P, CST["end"]), np.float32)
    r, q = np.arange(P)[:, None], np.arange(P)[None, :]
    c[:, CST["ident"]:][:, :P] = r == q
    c[:, CST["ones"]:][:, :P] = 1
    c[:, CST["bones"]:][:, :P] = r // 64 == q // 64
    r, q = r % 64, np.arange(64)[None, :]
    for i in range(6):
        h = 1 << i
        lo = (r // (2 * h) == q // (2 * h)) & (r // h % 2 == 1) & (q // h % 2 == 0)
        up = (r // (2 * h) == q // (2 * h)) & (r // h % 2 == 0) & (q // h % 2 == 1)
        c[:, CST["lo"] + 64 * i:][:, :64] = lo
        c[:, CST["up"] + 64 * i:][:, :64] = up
    for i, m in enumerate((r < q, r <= q, r > q, r >= q)):
        c[:, CST["tri"] + 64 * i:][:, :64] = m
    c[:, CST["istack"]:][:, :64] = r == q
    for a in (0, 16):
        for m in range(8):
            c[NOPE + a + 8 + m, CST["rot"] + a + m] = -1
            c[NOPE + a + m, CST["rot"] + a + 8 + m] = 1
    g = np.zeros((P, BIG["end"]), np.float32)
    t = np.arange(TOK)
    g[:, BIG["reset"]:][:, :TOK] = t % C != 0
    g[:, BIG["reset"] + TOK:][:, :TOK] = t % C != C - 1
    nf = ROPE // 4
    freq = (10000.0 ** (-np.arange(nf, dtype=np.float32) / nf)).astype(np.float32)
    for row in range(ROPE):
        pos = (np.arange(LAT) // 64 if row < 16 else np.arange(LAT) % 64).astype(np.float32)
        ang = pos * freq[row % 8]
        g[NOPE + row, BIG["cos"]:][:LAT] = np.cos(ang)
        g[NOPE + row, BIG["sin"]:][:LAT] = np.sin(ang)
    for i, w in enumerate((2, 4, 8, 16)):
        for t0, n in ((0, CTX), (CTX, LAT)):
            s = np.arange(n)
            cnt = np.clip(s + w - w // 2, 0, n) - np.clip(s - w // 2, 0, n)
            g[64 * (i % 2):64 * (i % 2) + 64, BIG["rcnt"] + TOK * (i // 2) + t0:][:, :n] = 1.0 / cnt.astype(np.float32)
    return c, g


def _layout(a):
    cols = lambda v: np.asarray(v).reshape(-1, P).T
    tile = lambda w: w.reshape(KT, P, P).transpose(1, 0, 2).reshape(P, KT * P)
    ada = lambda l, t: tile(a["ada_w"][l][:, P * t:P * (t + 1)])

    def projection(l, i):
        (name, _), c = IN_UNITS[i]
        if name != "rope":
            return tile(a["w_in"][l][:, c:c + P])
        w = np.zeros((D, P), a["w_in"].dtype)
        w[:, NOPE:QD] = a["w_in"][l][:, c:c + ROPE]
        return tile(w)

    def mlp(l, g, j):
        if j < 8:
            return tile(a["mlp_w1"][l][:, D * g + P * j:][:, :P])
        return tile(a["mlp_w2"][l][D * g:D * (g + 1), P * (j - 8):P * (j - 7)])

    units, t1 = [ada(0, t) for t in range(16)], 0
    for l in range(DEPTH):
        for i in range(N_IN):
            units.append(projection(l, i))
            if l == 0 and i < 16:
                units += [ada(0, 16 + 2 * i), ada(0, 17 + 2 * i)]
        units += [tile(a["w_out"][l][:, P * m:P * (m + 1)]) for m in range(KT)]
        for g in range(GROUPS):
            for j in range(UPG):
                units.append(mlp(l, g, j))
                for _ in range(ADA_AFTER.get(j, 0) if l == 0 else 0):
                    units.append(ada(1, t1))
                    t1 += 1
    stream = np.stack(units)
    vecs = []
    for l in range(DEPTH):
        for name in ("ada_b", "norm1_g", "norm2_g", "conv_dw", "conv_db", "conv_gn_g", "conv_gn_b", "pool_scale",
                     "rw_mu_prev", "rw_mu_next", "rw_w0", "rw_a0", "rw_kk", "rw_ka", "rw_rk", "rw_lnx_g", "rw_lnx_b",
                     "mla_qn_g", "mla_kvn_g"):
            vecs.append(cols(a[name][l]))
    vecs.append(cols(a["final_g"]))
    vecs = np.concatenate(vecs, 1)
    cond = np.stack([cols(a["c"][0]), cols(a["c_ctx"])], 2)
    rows = lambda w: w.reshape(-1, P, w.shape[-1]).transpose(1, 0, 2).reshape(P, -1)
    sa, sr = [], []
    for l in range(DEPTH):
        pw = np.zeros((P, 2, P), np.float32)
        for i in range(4):
            o = 64 * (i % 2)
            pw[o:o + 64, i // 2, o:o + 64] = a["pool_w"][l][i]
        sa.append(np.concatenate([rows(a["mla_wuq"][l]), a["mla_wukv"][l], rows(a["conv_pw"][l]), pw.reshape(P, -1)], 1))
        sr.append(np.concatenate([a["rw_w2"][l].reshape(P, GW), a["rw_a2"][l].reshape(P, GW), a["rw_g2"][l]], 1))
    xs = np.concatenate([a["ctx"][0], a["x"][0]], 0).T.reshape(KT, P, TOK).transpose(1, 0, 2)
    c, g = _tables()
    return {"xT": xs, "stream": stream, "vecs": vecs, "cond_in": cond, "consts": c, "big": g, "small_a": np.stack(sa),
            "small_r": np.stack(sr)}


def kernel(**inputs):
    import concourse.bacc as _bacc
    from concourse.bass_utils import run_bass_kernel_spmd as _run

    nc = _bacc.Bacc("TRN2", target_bir_lowering=False, num_devices=1)
    arrays = {k: np.ascontiguousarray(v) for k, v in _layout({k: np.asarray(v) for k, v in inputs.items()}).items()}
    args = {k: nc.dram_tensor(k, v.shape, mybir.dt.from_np(v.dtype), kind="ExternalInput").ap() for k, v in arrays.items()}
    kept = nc.dram_tensor("kept", (P, KT, LAT), F32, kind="Internal").ap()
    out = nc.dram_tensor("out_t", (P, KT, LAT), F32, kind="ExternalOutput").ap()
    trunk(nc, kept=kept, out=out, **args)
    r = _run(nc, [arrays], core_ids=[0])
    y = r.results[0]["out_t"]
    return y.transpose(2, 1, 0).reshape(1, LAT, D)
```

```python
from contextlib import ExitStack

import numpy as np
import concourse.bass as bass
from concourse import mybir

F32 = mybir.dt.float32
F32R = mybir.dt.float32r
U32 = mybir.dt.uint32
ALU = mybir.AluOpType
ACT = mybir.ActivationFunctionType
AX_X = mybir.AxisListType.X

P = 128
D = 1024
KT = D // P
CTX, LAT = 256, 512
TOK = CTX + LAT
DEPTH = 2
GW = 256
HD = 64
C = 64
NC = TOK // C
CCTX = CTX // C
TAPS = 31
HEADS = 4
NOPE, ROPE = 64, 32
QD = NOPE + ROPE
FF = 4 * D
GROUPS = 4
ADA_AFTER = {1: 2, **{j: 1 for j in range(2, 12)}}
IN_ADA = [3, 3, 3, 3] + [1] * 9 + [2, 2, 1, 1, 2, 3]
UPG = 16
NT_MODS = 48
RAW = 4
SPL = 2
NORM_EPS, GN_EPS, LNX_EPS = 1e-6, 1e-5, 64e-5
C1 = float(-0.5 * np.exp(-0.5))
SCALE = float(QD) ** -0.5
T = TOK * 4

OFF_POOL, OFF_Q, OFF_RW, OFF_KV = 512, 768, 1024, 2176

IN_UNITS = ([(("q", i), OFF_Q + P * i) for i in range(2)] + [(("kv", 0), OFF_KV), (("rope", 0), OFF_KV + P)]
            + [(("z", i), OFF_RW + P * i) for i in (7, 8, 2, 3, 0, 1, 4, 5, 6)]
            + [(("cg", i), GW + P * i) for i in range(2)] + [(("cv", i), P * i) for i in range(2)]
            + [(("pool", i), OFF_POOL + P * i) for i in range(2)])
LAT_ONLY = {"q", "cg", "cv", "pool"}
N_IN = len(IN_UNITS)


def columns(names):
    at, n = {}, 0
    for name, width in names:
        at[name] = n
        n += width
    at["end"] = n
    return at


VEC = [("ada_b", 48), ("n1", 8), ("n2", 8), ("dw", 2 * TAPS), ("db", 2), ("cgg", 2), ("cgb", 2), ("psc", 2),
       ("mup", 9), ("mun", 9), ("w0", 4), ("a0", 4), ("kk", 2), ("ka", 2), ("rk", 2), ("lg", 2), ("lb", 2),
       ("qn", 2), ("kvn", 1)]
VEC_L = columns(VEC)
V_FINAL = DEPTH * VEC_L["end"]
N_VEC = V_FINAL + KT

CST = columns([("ident", P), ("ones", P), ("bones", P), ("lo", 6 * C), ("up", 6 * C), ("tri", 4 * C), ("istack", C),
               ("rot", P)])
BIG = columns([("reset", TOK), ("cos", LAT), ("sin", LAT), ("rcnt", 2 * TOK)])
SW_A = columns([("wuq", 2 * HEADS * QD), ("wukv", 4 * P), ("pw", 2 * GW), ("poolw", 2 * P)])
SW_R = columns([("w2", GW), ("a2", GW), ("g2", GW)])

DER = columns([("A1", 16), ("A2", 16), ("c0", 9), ("hw0", 4), ("ha0", 4), ("nkk", 2), ("s1", 2), ("s2", 2),
               ("hg", 2), ("hb", 2)])


class Steps:

    def __init__(self):
        self.n = 0

    def up(self):
        self.n += 1
        return 1


class Signal:

    def __init__(self, sem, keys):
        self.sem, self.at = sem, {k: n + 1 for n, k in enumerate(keys)}


class Slots:

    def __init__(self, tensor, full, free):
        self.tensor, self.sem_full, self.sem_free, self.n, self.at = tensor, full, free, 0, {}

    def claim(self, key):
        self.at[key] = self.n
        self.n += 1
        return self.slot(key)

    def slot(self, key):
        return self.tensor[:, self.at[key] % 2, :]

    def reused(self, key):
        return self.at[key] >= 2

    def use(self, key):
        return self.at[key] // 2 + 1

    def full(self, key):
        return self.sem_full[self.at[key] % 2]

    def free(self, key):
        return self.sem_free[self.at[key] % 2]


def chunk_order(d):
    if d == 0:
        return list(range(NC))
    return list(range(CCTX - 1, -1, -1)) + list(range(NC - 1, CCTX - 1, -1))


def attention_units(l):
    return [(h, q) for h in range(HEADS) for q in range(0 if l == 0 else 2, TOK // P)]


def front(i):
    steps = [("kk", i)] if i % 2 == 0 else []
    steps += [("lora", i)] + [("prep", i, n) for n in range(6)] + [("gram", i, g) for g in range(3)] + [("bkt", i)]
    steps.append(("t", i, 0))
    for n in range(1, 6):
        steps += [("t", i, n)] + [("x", i, n)] * (n < 5) + [("xt", i, n)]
    return steps


def scan(i):
    return [(s, i, n) for n in range(NC) for s in ("w", "u", "s")]


def rwkv_schedule():
    order = front(0) + [("v", 0)]
    for i in range(4):
        chain, other = scan(i), front(i + 1) if i < 3 else []
        for n, step in enumerate(other):
            order.append(step)
            take = 2 if step[0] in ("prep", "lora", "bkt") else 1
            order += chain[:take]
            chain = chain[take:]
        order += chain
        if i % 2:
            order.append(("post", i // 2))
        if i == 1:
            order.append(("v", 1))
    return order


def bc(ap, shape, axis):
    return ap.unsqueeze(axis).to_broadcast(shape)


def trunk(nc, xT, stream, vecs, cond_in, consts, big, small_a, small_r, kept, kept_rows, out):
    es = ExitStack()
    with es:
        sem = lambda name: es.enter_context(nc.semaphore(name))
        base = (nc.sbuf_base + 31) // 32 * 32

        class Region:

            def __init__(self, offset):
                self.o = offset

            def __call__(self, name, shape, dt=F32):
                size = (int(np.prod(shape[1:])) * 4 + 31) // 32 * 32
                assert self.o + size <= nc.sbuf_usable_end, (name, self.o + size)
                t = nc.alloc_sbuf_tensor_at(name, shape, dt, offset=self.o)
                self.o += size
                return t

        R = Region(base)
        actH, actL, act_at = [], [], []
        for g in range(4):
            act_at.append(R.o)
            actH.append(R(f"act_hi{g}", [P, 2, TOK], F32R))
            actL.append(R(f"act_lo{g}", [P, 2, TOK], F32R))
        raw = R("raw_weights", [P, RAW, KT, P])
        whi = R("weights_hi", [P, SPL, KT, P], F32R)
        wlo = R("weights_lo", [P, SPL, KT, P], F32R)
        cst = R("consts_sb", [P, CST["end"]])
        vec = R("vecs_sb", [P, N_VEC])
        mods = R("mods", [P, DEPTH, NT_MODS, 2])
        der = R("derived", [P, DER["end"]])
        sw_r = R("small_r_sb", [P, SW_R["end"]])
        stat_at = R.o
        stat = R("softmax_stats", [P, 4, HEADS * TOK // P])
        z_at = R.o
        zt = R("z_tiles", [P, 7, TOK])
        zv = R("z_v", [P, 2, TOK + 2 * C])
        free0 = R.o

        x = R("x_tiles", [P, KT, TOK])
        sq = R("squares", [P, 2, TOK])
        rinv = R("rinv", [P, TOK])
        tb_at = R.o
        tb = R("normed", [P, 2, TOK])
        hb = R("modulated", [P, 2, TOK])
        hid_lo = R("hidden_lo", [P, 8, TOK], F32R)
        relu = R("relu", [P, 2, TOK])
        hsq = R("hidden_sq", [P, 2, TOK])
        hid_hi = Region(z_at)("hidden_hi", [P, 8, TOK], F32R)
        rows2 = Region(tb_at)("silu_rows2", [P, 2, D])

        R = Region(free0)
        wa = R("work_a", [P, 2, TOK])
        wb = R("work_b", [P, 2, TOK])
        q_sb = R("q_low_rank", [P, 2, TOK])
        ckv = R("kv_low_rank", [P, TOK])
        krope = R("k_rope", [P, TOK])
        ltmp = R("low_rank_tmp", [P, TOK])
        lrin = R("low_rank_rinv", [P, TOK])
        cs = R("cos_sin", [P, 2, LAT])
        sw_a = R("small_a_sb", [P, SW_A["end"]])
        UL = 15 + CTX + 15
        u_sb = R("conv_u", [P, 2, UL + LAT + 15])
        PL = 8 + CTX + 16
        PWID = PL + LAT + 8
        pp = R("pool_p", [P, 2, PWID])
        rows_at = R.o
        u_acc = R("conv_taps", [P, 2, CTX + 15 + LAT])
        ps = R("pool_sums", [P, 2, PWID])
        rcnt = R("pool_rcnt", [P, 2, TOK])
        qT = R("q_t", [P, 2, TOK])
        kT = R("k_t", [P, 2, TOK])
        rtmp = R("rope_tmp", [P, LAT])
        R = Region(rows_at)
        rows = R("silu_rows", [P, 2, D])
        rows_tmp = R("silu_rows_tmp", [P, 2, D])
        R = Region(act_at[1])
        v_tok = R("v_tok", [P, TOK // P, HEADS * HD])
        otok = R("o_tok", [P, TOK // P, HEADS * HD])
        R = Region(act_at[2])
        acc = R("conv_normed", [P, 2, TOK])
        ptmp = R("pool_tmp", [P, PWID])

        R = Region(free0)
        Q = R("rw_q", [P, 2, 4, TOK])
        BKt = R("rw_bk_tok", [P, 2, NC, P])
        XT_at = R.o
        XT = R("rw_xt", [P, 2, NC, C])
        M_at = R.o
        M = R("rw_m", [P, 2, 2, NC, C])
        BK = R("rw_bk", [P, NC, 2, C])
        UV = R("rw_uv", [P, NC, P])
        SV = R("rw_sv", [P, NC, P])
        b_at = R.o
        X = R("rw_x", [P, NC, C])
        Tc = R("rw_t", [P, NC, C])
        LT = R("rw_lt", [P, NC, C])
        Y = R("rw_y", [P, TOK])
        reset = R("rw_reset", [P, TOK])
        Wc = R("rw_w", [P, 2, C])
        R = Region(stat_at)
        SP = R("rw_s_decayed", [P, C])
        PC = R("rw_p_end", [P, 2, NC])
        R = Region(act_at[1] + T)
        nkk = R("rw_nkk", [P, TOK])
        kds = R("rw_kd_sum", [P, 2, TOK])
        b = Region(b_at)("rw_tmp", [P, 3, TOK])
        b3 = Region(XT_at)("rw_tmp3", [P, 2, TOK])
        b45 = Region(M_at)("rw_tmp45", [P, 2, 2, TOK])

        psA = es.enter_context(nc.psum_tensor("psA", [P, 2, 1024], F32))
        psB = es.enter_context(nc.psum_tensor("psB", [P, 2, 1024], F32))
        A = Slots(psA, [sem("a0_full"), sem("a1_full")], [sem("a0_free"), sem("a1_free")])
        B = Slots(psB, [sem("b0_full"), sem("b1_full")], [sem("b0_free"), sem("b1_free")])

        V = lambda l, name, i=0, n=1: vec[:, l * VEC_L["end"] + VEC_L[name] + i:][:, 0:n]
        DR = lambda name, i=0, n=1: der[:, DER[name] + i:DER[name] + i + n]
        K = lambda name, n, i=0: cst[:, CST[name] + i:CST[name] + i + n]
        ident, ones, bones = K("ident", P), K("ones", P), K("bones", P)
        H = lambda k: actH[k // 2][:, k % 2, :]
        L = lambda k: actL[k // 2][:, k % 2, :]
        f32 = lambda ap: ap.bitcast(F32)
        PSC = 256
        first = lambda l: 0 if l == 0 else CTX
        segs = lambda c0: [(0, CTX, LAT)] + ([(1, 0, CTX)] if c0 == 0 else [])

        units = [("ada", 0)] * 16
        for i in range(N_IN):
            units += [("split", IN_UNITS[i][0])] + [("ada", 0)] * IN_ADA[i]
        units += [("split", "out")] * 8
        mlp0 = {0: len(units)}
        LOOP = {0: 28, 1: 16}
        ada_after = lambda l, j: ADA_AFTER.get(j, 0) if l == 0 else 0
        for g in range(GROUPS):
            for j in range(UPG):
                units += [("split", "mlp")] + [("ada", 1)] * ada_after(0, j)
        units += [("split", u[0]) for u in IN_UNITS] + [("split", "out")] * 8
        mlp0[1] = len(units)
        units += [("split", "mlp")] * (UPG * GROUPS)
        split_no, unit_of_split, n = {}, [], 0
        for i, (kind, _) in enumerate(units):
            if kind == "split":
                split_no[i] = len(unit_of_split)
                unit_of_split.append(i)
        ada_no = {i: k for k, i in enumerate(i for i, u in enumerate(units) if u[0] == "ada")}
        SPL_L = len(unit_of_split) // DEPTH
        S_OUT, S_MLP = N_IN, N_IN + 8
        assert N_IN + 8 + UPG * GROUPS == SPL_L

        c_in = sem("constants_in")
        mix_in = sem("mixing_constants_in")
        rw_in = sem("rwkv_constants_in")
        x_in = sem("x_loaded")
        x_kept = sem("x_kept")
        out_done = sem("out_stored")
        w_in = [sem(f"raw_full{i}") for i in range(RAW)]
        w_hi, w_lo, ada_used = sem("w_hi"), sem("w_lo"), sem("ada_used")
        cond_th, cond_ready = sem("cond_tanh"), sem("cond_ready")
        rows_kept, rows_in = sem("silu_rows_kept"), sem("silu_rows_in")
        vector_step, pool_step = sem("vector_step"), sem("pool_step")
        relu_ready, hid_hi_ready, hid_ready = sem("relu_ready"), sem("hidden_hi_ready"), sem("hidden_ready")

        ls, hs = range(DEPTH), range(HEADS)
        norms = [(l, n) for l in ls for n in (1, 2)] + [(DEPTH, 0)]
        nk = [(n, k) for n in norms for k in range(KT)]
        li2 = [(l, i) for l in ls for i in range(2)]
        sq_ready = Signal(sem("squares_ready"), nk)
        sq_used = Signal(sem("squares_used"), [(n, k) for n in norms for k in range(KT - 1)])
        rms = Signal(sem("rms_ready"), norms)
        mod_ready = Signal(sem("modulated"), nk[:-KT])
        act_hi = Signal(sem("act_hi_ready"), nk[:-KT])
        act_lo = Signal(sem("act_lo_ready"), nk[:-KT])
        fin_ready = Signal(sem("final_tile"), [(k,) for k in range(KT)])
        der_ready = Signal(sem("derived_ready"), [(l,) for l in ls])

        lr_sq = Signal(sem("low_rank_squared"), [(l, i) for l in ls for i in range(3)])
        lr_rms = Signal(sem("low_rank_rms"), li2)
        lr_normed = Signal(sem("low_rank_normed"), li2)
        kr_ready = Signal(sem("k_rope_rotated"), [(l,) for l in ls])
        z_order = [u[0][1] for u in IN_UNITS if u[0][0] == "z"]
        z_mixed = Signal(sem("z_mixed"), [(l, i) for l in ls for i in z_order])
        pads = Signal(sem("pads_zeroed"), [(l,) for l in ls])
        lh = [(l, h) for l in ls for h in hs]
        q_rot = Signal(sem("q_rotated"), lh)
        k_full = Signal(sem("k_rope_copied"), lh)
        au = {l: attention_units(l) for l in ls}
        lau = [(l, i) for l in ls for i in range(len(au[l]))]
        rowmax = Signal(sem("row_max"), lau)
        y_hi = Signal(sem("y_hi_ready"), [(l, s, i) for l in ls for s in ("att", "conv", "pool", "rw") for i in range(2)])
        y_lo = Signal(sem("y_lo_ready"), li2)
        conv_sum = Signal(sem("conv_summed"), li2)
        conv_sq = Signal(sem("conv_squared"), li2)
        conv_std = Signal(sem("conv_std"), li2)
        conv_pre = Signal(sem("conv_scaled"), li2)
        conv_th = Signal(sem("conv_tanh"), li2)
        conv_act = Signal(sem("conv_silu"), li2)
        pool_d = Signal(sem("pool_diff"), li2)

        rw_zero = Signal(sem("rw_zeroed"), [(l,) for l in ls])
        l_lora = Signal(sem("decay_input"), [(l,) for l in ls])
        g_th = Signal(sem("gate_tanh"), [(l,) for l in ls])
        kk_sq = Signal(sem("kk_squared"), li2)
        kk_std = Signal(sem("kk_norm"), li2)
        ru = [(l, j, d) for l in ls for j in range(2) for d in range(2)]
        cum = Signal(sem("decay_summed"), ru)
        exps = Signal(sem("decay_exps"), [(u, i) for u in ru for i in range(3)])
        dk = Signal(sem("decay_before"), ru)
        prep = Signal(sem("chunk_operands"), ru)
        v_tp = Signal(sem("v_chunks"), [(l, j, w) for l in ls for j in range(2) for w in range(2)])
        x_one = Signal(sem("x_first"), ru)
        xt_one = Signal(sem("xt_first"), ru)
        scan_keys = [(u, s_, n) for u in ru for n in range(NC) for s_ in ("w", "u", "s") if s_ != "s" or n < NC - 1]
        scan_full = Signal(sem("scan_product"), scan_keys)
        scan_read = Signal(sem("scan_product_read"), scan_keys)
        y_full = Signal(sem("scan_y_summed"), ru)
        y_read = Signal(sem("scan_y_read"), ru)
        s_zero = Signal(sem("state_zeroed"), ru)
        s_dec = Signal(sem("state_decayed"), [(u, i) for u in ru for i in range(NC - 1)])
        rw_sq = Signal(sem("rw_squared"), li2)
        rw_std = Signal(sem("rw_std"), li2)
        bon = Signal(sem("bonus_product"), li2)

        block = es.enter_context(nc.Block())
        RW = rwkv_schedule()
        scan_w, scan_u, scan_s = psB[:, 1, 0:C], psB[:, 1, 512:512 + C], psB[:, 1, C:2 * C]
        HALF = ((slice(0, 64), 0), (slice(64, P), 1))
        rp = slice(NOPE, QD)
        ZI = {0: 0, 1: 1, 2: 2, 3: 3, 6: 4, 7: 5, 8: 6}
        z_of = lambda i: zv[:, i - 4, C:C + TOK] if i in (4, 5) else zt[:, ZI[i], :]
        chunks = lambda ap: ap.rearrange("p (c t) -> p c t", t=C)

        @block.tensor
        def _(pe):
            def span(dst, lhsT, rhs, start, stop, c0=0, part=slice(0, P)):
                if c0 == 0:
                    pe.matmul(dst[part, PSC:PSC + CTX], lhsT, rhs[:, 0:CTX], start=start, stop=stop)
                return pe.matmul(dst[part, PSC + CTX:], lhsT, rhs[:, CTX:TOK], start=start, stop=stop)

            def unit_products(dst, w, hi, lo, c0, each):
                for k in range(KT):
                    if each:
                        each(k)
                    span(dst, whi[:, w, k, :], lo(k), k == 0, False, c0)
                    span(dst, whi[:, w, k, :], hi(k), False, False, c0)
                    m = span(dst, wlo[:, w, k, :], hi(k), False, k == KT - 1, c0)
                return m

            def linear(n, key, c0, hi=H, lo=L, plus=0, slots=0, each=None):
                dst = A.claim(key)
                if A.reused(key):
                    pe.wait_ge(A.free(key), A.use(key) - 1 + slots)
                pe.wait_ge(w_lo, n + 1 + plus)
                unit_products(dst, n % SPL, hi, lo, c0, each).then_inc(A.full(key), 1)

            def norm_sum(key, k, c0):
                if k == 0:
                    dst = B.claim(("norm", key))
                    if B.reused(("norm", key)):
                        pe.wait_ge(B.free(("norm", key)), B.use(("norm", key)) - 1)
                pe.wait_ge(sq_ready.sem, sq_ready.at[key, k])
                m = span(B.slot(("norm", key)), ones, sq[:, k % 2, :], k == 0, k == KT - 1, c0)
                m.then_inc(sq_used.sem if k < KT - 1 else B.full(("norm", key)), 1)

            def small(pool, key, c0, pairs, part=slice(0, P)):
                dst = pool.claim(key)
                if pool.reused(key):
                    pe.wait_ge(pool.free(key), pool.use(key) - 1)
                for i, (lhsT, rhs) in enumerate(pairs):
                    m = span(dst, lhsT, rhs, i == 0, i == len(pairs) - 1, c0, part)
                m.then_inc(pool.full(key), 1)

            pe.wait_ge(c_in, 16 * 3)
            nsplit = 0
            for l in ls:
                c0 = first(l)
                if l:
                    pe.wait_ge(ada_used, 2 * NT_MODS)
                for k in range(KT):
                    norm_sum((l, 1), k, 0)
                for i, (name, _) in enumerate(IN_UNITS):
                    normed = lambda k: pe.wait_ge(act_lo.sem, act_lo.at[(l, 1), k])
                    linear(nsplit, (l,) + name, c0 if name[0] in LAT_ONLY else 0, each=None if i else normed)
                    nsplit += 1

                if l == 0:
                    pe.wait_ge(ada_used, NT_MODS)
                pe.wait_ge(mix_in, 48 * (l + 1))
                pe.wait_ge(lr_sq.sem, lr_sq.at[l, 1])
                small(B, (l, "qstat"), c0, [(ones, ltmp[:, :]), (ones, lrin[:, :])])
                pe.wait_ge(lr_sq.sem, lr_sq.at[l, 2])
                small(B, (l, "kvstat"), 0, [(ones, kT[:, 0, :])])
                pe.wait_ge(A.free((l, "rope", 0)), A.use((l, "rope", 0)))

                def rotate(key, src):
                    dst = B.claim(key)
                    if B.reused(key):
                        pe.wait_ge(B.free(key), B.use(key) - 1)
                    pe.matmul(dst[rp, PSC + CTX:], K("rot", ROPE)[rp, :], src[rp, CTX:], start=True,
                                       stop=True).then_inc(B.full(key), 1)

                rotate((l, "krot"), krope[:, :])
                pe.wait_ge(lr_normed.sem, lr_normed.at[l, 1])
                for w, blocks in enumerate(((0, 1, 2, 3), (4, 5))):
                    dst = A.claim((l, "v", w))
                    if A.reused((l, "v", w)):
                        pe.wait_ge(A.free((l, "v", w)), A.use((l, "v", w)) - 1)
                    vw = sw_a[:, SW_A["wukv"]:][:, 0:4 * P].rearrange("p (h n) -> p h n", h=HEADS)[:, :, NOPE:]
                    for b_ in blocks:
                        m = pe.matmul(dst[:, GW * (b_ % 4):GW * (b_ % 4 + 1)], ckv[:, P * b_:P * (b_ + 1)], vw,
                                      start=True, stop=True)
                    m.then_inc(A.full((l, "v", w)), 1)

                def head_operands(h):
                    wq = lambda k: sw_a[:, SW_A["wuq"] + k * HEADS * QD + h * QD:][:, 0:QD]
                    wk = sw_a[:, SW_A["wukv"] + h * P:][:, 0:NOPE]
                    small(A, (l, "qh", h), c0, [(wq(k), q_sb[:, k, :]) for k in range(2)], slice(0, QD))
                    small(A, (l, "kh", h), 0, [(wk, ckv[:, :])], slice(0, NOPE))
                    pe.wait_ge(A.free((l, "qh", h)), A.use((l, "qh", h)))
                    rotate((l, "qrot", h), qT[:, h % 2, :])

                def scores(i):
                    h, q = au[l][i]
                    dst = A.claim((l, "s", i))
                    if A.reused((l, "s", i)):
                        pe.wait_ge(A.free((l, "s", i)), A.use((l, "s", i)) - 1)
                    if i == 0 or au[l][i - 1][0] != h:
                        pe.wait_ge(q_rot.sem, q_rot.at[l, h])
                        pe.wait_ge(A.free((l, "kh", h)), A.use((l, "kh", h)))
                        pe.wait_ge(k_full.sem, k_full.at[l, h])
                    m = pe.matmul(dst[:, PSC:PSC + CTX], qT[0:QD, h % 2, P * q:P * (q + 1)], kT[0:QD, h % 2, 0:CTX],
                                  start=True, stop=True)
                    if q >= CTX // P:
                        m = pe.matmul(dst[:, PSC + CTX:], qT[0:QD, h % 2, P * q:P * (q + 1)], kT[0:QD, h % 2, CTX:],
                                      start=True, stop=True)
                    m.then_inc(A.full((l, "s", i)), 1)

                blocks_of = lambda q: (CTX if q < CTX // P else TOK) // P

                def turn(i):
                    dst = B.claim((l, "pt", i))
                    if B.reused((l, "pt", i)):
                        pe.wait_ge(B.free((l, "pt", i)), B.use((l, "pt", i)) - 1)
                    pe.wait_ge(A.free((l, "s", i)), A.use((l, "s", i)))
                    for b_ in range(blocks_of(au[l][i][1])):
                        m = pe.transpose(dst[:, PSC + P * b_:PSC + P * (b_ + 1)], wa[:, i % 2, P * b_:P * (b_ + 1)], ident)
                    m.then_inc(B.full((l, "pt", i)), 1)

                def mix_values(i):
                    h, q = au[l][i]
                    nb = blocks_of(q)
                    dst = B.claim((l, "o", i))
                    if B.reused((l, "o", i)):
                        pe.wait_ge(B.free((l, "o", i)), B.use((l, "o", i)) - 1)
                    if i == 0:
                        pe.wait_ge(A.free((l, "v", 0)), A.use((l, "v", 0)))
                        pe.wait_ge(A.free((l, "v", 1)), A.use((l, "v", 1)))
                    pe.wait_ge(B.free((l, "pt", i)), B.use((l, "pt", i)))
                    for b_ in range(nb):
                        m = pe.matmul(dst[:, 0:HD], wb[:, i % 2, P * b_:P * (b_ + 1)], v_tok[:, b_, HD * h:HD * (h + 1)],
                                      start=b_ == 0, stop=b_ == nb - 1)
                    m.then_inc(B.full((l, "o", i)), 1)

                head_operands(0)
                for i in range(len(au[l])):
                    h = au[l][i][0]
                    if (i == 0 or au[l][i - 1][0] != h) and h + 1 < HEADS:
                        head_operands(h + 1)
                    scores(i)
                    if i:
                        turn(i - 1)
                    if i > 1:
                        mix_values(i - 2)
                turn(len(au[l]) - 1)
                mix_values(len(au[l]) - 2)
                mix_values(len(au[l]) - 1)
                for i in range(2):
                    dst = A.claim((l, "att", i))
                    if A.reused((l, "att", i)):
                        pe.wait_ge(A.free((l, "att", i)), A.use((l, "att", i)) - 1)
                    if i == 0:
                        pe.wait_ge(B.free((l, "o", len(au[l]) - 1)), B.use((l, "o", len(au[l]) - 1)))
                        pe.wait_ge(B.free((l, "o", len(au[l]) - 2)), B.use((l, "o", len(au[l]) - 2)))
                    for q in range(c0 // P, TOK // P):
                        m = pe.transpose(dst[:, PSC + P * q:PSC + P * (q + 1)], otok[:, q, P * i:P * (i + 1)], ident)
                    m.then_inc(A.full((l, "att", i)), 1)

                for i in range(2):
                    pe.wait_ge(conv_sum.sem, conv_sum.at[l, i])
                    small(B, (l, "cmean", i), c0, [(bones, acc[:, i, :])])
                for i in range(2):
                    pe.wait_ge(conv_sq.sem, conv_sq.at[l, i])
                    small(B, (l, "cvar", i), c0, [(bones, u_sb[:, i, 0:TOK])])
                pe.wait_ge(conv_act.sem, conv_act.at[l, 1])
                for i in range(2):
                    small(A, (l, "convp", i), c0,
                          [(sw_a[:, SW_A["pw"] + k * GW + i * P:][:, 0:P], acc[:, k, :]) for k in range(2)])
                for i in range(2):
                    pe.wait_ge(pool_d.sem, pool_d.at[l, i])
                    small(A, (l, "poolp", i), c0, [(sw_a[:, SW_A["poolw"] + i * P:][:, 0:P], rcnt[:, i, :])])

                pe.wait_ge(rw_in, 32 * (l + 1))
                pe.wait_ge(l_lora.sem, l_lora.at[(l,)])
                pe.wait_ge(rw_zero.sem, rw_zero.at[(l,)])
                def by_chunk(key, lhsT, rhs):
                    dst = A.claim(key)
                    if A.reused(key):
                        pe.wait_ge(A.free(key), A.use(key) - 1)
                    for c in range(NC):
                        for part, _ in HALF:
                            m = pe.matmul(dst[part, PSC + C * c:][:, 0:C], lhsT[part, c, :], rhs(c)[part], start=True,
                                          stop=True)
                    m.then_inc(A.full(key), 1)

                for what, i, *rest in RW:
                    j, d, p = i // 2, i % 2, i % 2
                    un, n_ = (l, j, d), rest[0] if rest else 0
                    if what == "kk":
                        pe.wait_ge(kk_sq.sem, kk_sq.at[l, j])
                        small(A, (l, "kk", j), 0, [(bones, nkk[:, :])])
                    elif what == "lora":
                        dp = slice(64 * d, 64 * d + 64)
                        small(A, (un, "w2"), 0, [(sw_r[dp, SW_R["w2"] + P * j:][:, 0:P], zt[dp, 5, :])])
                        small(A, (un, "a2"), 0, [(sw_r[dp, SW_R["a2"] + P * j:][:, 0:P], zt[dp, 6, :])])
                    elif what == "v":
                        for w, ms in enumerate((range(0, 7), range(7, 13))):
                            key = (l, i, "v", w)
                            dst = A.claim(key)
                            if A.reused(key):
                                pe.wait_ge(A.free(key), A.use(key) - 1)
                            for m_ in ms:
                                o = m_ - ms[0]
                                m = pe.transpose(dst[:, P * o:P * (o + 1)], zv[:, i, C * m_:C * m_ + P], ident)
                            m.then_inc(A.full(key), 1)
                    elif what == "gram":
                        if n_ == 0:
                            pe.wait_ge(prep.sem, prep.at[un])
                        key = (un, "gram", n_)
                        dst = A.claim(key)
                        if A.reused(key):
                            pe.wait_ge(A.free(key), A.use(key) - 1)
                        for c in range(4 * n_, 4 * n_ + 4):
                            for part, s_ in HALF:
                                m = pe.matmul(dst[:, 512 * s_ + P * (c % 4):][:, 0:P], BK[part, c, :, :],
                                              Q[part, p, 2 * s_:2 * s_ + 2, C * c:C * (c + 1)], start=True, stop=True)
                        m.then_inc(A.full(key), 1)
                    elif what == "bkt":
                        for w in range(2):
                            key = (un, "bkt", w)
                            dst = A.claim(key)
                            if A.reused(key):
                                pe.wait_ge(A.free(key), A.use(key) - 1)
                            for c in range(8 * w, min(8 * w + 8, NC)):
                                m = pe.transpose(dst[:, P * (c % 8):][:, 0:P], BK[:, c, :, :], ident)
                            m.then_inc(A.full(key), 1)
                    elif what == "t":
                        if n_ == 0:
                            pe.wait_ge(A.free((un, "gram", 2)), A.use((un, "gram", 2)))
                            by_chunk((un, "t", 0), LT, lambda c: K("istack", C))
                        else:
                            if n_ == 1:
                                pe.wait_ge(x_one.sem, x_one.at[un])
                            else:
                                pe.wait_ge(A.free((un, "x", n_ - 1)), A.use((un, "x", n_ - 1)))
                            by_chunk((un, "t", n_), LT, lambda c: X[:, c, :])
                    elif what == "x":
                        if n_ == 1:
                            pe.wait_ge(xt_one.sem, xt_one.at[un])
                        else:
                            pe.wait_ge(A.free((un, "xt", n_ - 1)), A.use((un, "xt", n_ - 1)))
                        pe.wait_ge(A.free((un, "t", n_)), A.use((un, "t", n_)))
                        by_chunk((un, "x", n_), XT[:, p], lambda c: Tc[:, c, :])
                    elif what == "xt":
                        if n_ == 5:
                            pe.wait_ge(A.free((un, "xt", 4)), A.use((un, "xt", 4)))
                            pe.wait_ge(A.free((un, "t", 5)), A.use((un, "t", 5)))
                        by_chunk((un, "xt", n_), Tc, lambda c: XT[:, p, c, :])
                    elif what == "w":
                        c = chunk_order(d)[n_]
                        if n_ == 0:
                            pe.wait_ge(A.free((un, "xt", 5)), A.use((un, "xt", 5)))
                            pe.wait_ge(A.free((un, "bkt", 1)), A.use((un, "bkt", 1)))
                            pe.wait_ge(A.free((l, j, "v", 1)), A.use((l, j, "v", 1)))
                            pe.wait_ge(s_zero.sem, s_zero.at[un])
                            if i:
                                pe.wait_ge(y_read.sem, y_read.at[un] - 1)
                            else:
                                pe.wait_ge(B.free((l, "cvar", 0)), B.use((l, "cvar", 0)))
                                pe.wait_ge(B.free((l, "cvar", 1)), B.use((l, "cvar", 1)))
                        else:
                            pe.wait_ge(scan_read.sem, scan_read.at[un, "s", n_ - 1])
                        for part, s_ in HALF:
                            m = pe.matmul(scan_w[part], Q[:, p, 2 * s_, C * c:C * (c + 1)],
                                          SV[:, c, HD * s_:HD * (s_ + 1)], start=True, stop=True)
                        m.then_inc(scan_full.sem, 1)
                    elif what == "u":
                        c = chunk_order(d)[n_]
                        pe.wait_ge(scan_read.sem, scan_read.at[un, "w", n_])
                        for part, _ in HALF:
                            m = pe.matmul(scan_u[part], XT[part, p, c, :], Wc[part, n_ % 2, :], start=True, stop=True)
                        m.then_inc(scan_full.sem, 1)
                    elif what == "s":
                        c = chunk_order(d)[n_]
                        pe.wait_ge(scan_read.sem, scan_read.at[un, "u", n_])
                        if n_ < NC - 1:
                            for part, s_ in HALF:
                                m = pe.matmul(scan_s[part], BKt[:, p, c, HD * s_:HD * (s_ + 1)],
                                              UV[:, c, HD * s_:HD * (s_ + 1)], start=True, stop=True)
                            m.then_inc(scan_full.sem, 1)
                        if c * C >= c0:
                            o = PSC + C * c
                            for part, s_ in HALF:
                                hv = slice(HD * s_, HD * (s_ + 1))
                                pe.matmul(psB[part, 0, o:o + C], SV[:, c, hv], Q[:, p, 2 * s_ + 1, C * c:C * (c + 1)],
                                          start=True, stop=False)
                                m = pe.matmul(psB[part, 0, o:o + C], UV[:, c, hv], M[:, p, s_, c, :], start=False,
                                              stop=True)
                        if n_ == NC - 1:
                            m.then_inc(y_full.sem, 1)
                    elif what == "post":
                        pe.wait_ge(bon.sem, bon.at[l, i])
                        small(A, (l, i, "bonus"), c0, [(bones, b[:, 1, :])])
                        pe.wait_ge(y_read.sem, y_read.at[l, i, 1])
                        small(A, (l, i, "mean"), c0, [(bones, Y[:, :])])
                        pe.wait_ge(rw_sq.sem, rw_sq.at[l, i])
                        small(A, (l, i, "var"), c0, [(bones, b[:, 0, :])])
                        small(A, (l, i, "gate"), c0, [(sw_r[:, SW_R["g2"] + P * i:][:, 0:P], zt[:, 4, :])])

                for key in ("att", "convp", "poolp"):
                    for i in range(2):
                        pe.wait_ge(A.free((l, key, i)), A.use((l, key, i)))
                pe.wait_ge(y_lo.sem, y_lo.at[l, 1])
                for m_ in range(KT):
                    linear(nsplit, (l, "out", m_), c0)
                    nsplit += 1
                    if m_:
                        norm_sum((l, 2), m_ - 1, c0)
                norm_sum((l, 2), KT - 1, c0)

                hh, hl = (lambda k: hid_hi[:, k, :]), (lambda k: hid_lo[:, k, :])

                def group(g0, g, end=False):
                    normed = lambda k: pe.wait_ge(act_lo.sem, act_lo.at[(l, 2), k])
                    hidden = lambda k: pe.wait_ge(hid_ready, 8 * (l * GROUPS + g0) + k + 1 + 8 * g)
                    n = nsplit + UPG * g0
                    for j in range(UPG):
                        linear(n + j, (l, "mlp", g0, j), c0, *((H, L) if j < 8 else (hh, hl)), UPG * g, 8 * g,
                               {0: normed, 8: hidden}.get(j))
                        if end and j > 8:
                            norm_sum((DEPTH, 0), j - 9, CTX)

                if l == 0:
                    with pe.Fori(0, GROUPS) as g:
                        group(0, g)
                    A.n += UPG * (GROUPS - 1)
                else:
                    with pe.Fori(0, GROUPS - 1) as g:
                        group(0, g)
                    A.n += UPG * (GROUPS - 2)
                    group(GROUPS - 1, 0, True)
                nsplit += UPG * GROUPS
            norm_sum((DEPTH, 0), KT - 1, CTX)

        @block.scalar
        def _(act):
            cp = lambda o, i, **k: act.activation(o, i, ACT.Copy, **k)

            def split_hi(n, plus=0, i_plus=0):
                i = unit_of_split[n]
                act.wait_ge(w_in[i % RAW], 16 * (i // RAW + 1) + i_plus)
                act.activation(whi[:, n % SPL], raw[:, i % RAW], ACT.Copy).then_inc(w_hi, 1)

            def ahead(n, key, plus=0, i_plus=0, last=False):
                act.wait_ge(A.full(key), A.use(key) + plus)
                src = A.slot(key)
                if not last:
                    split_hi(n + SPL, i_plus=i_plus)
                return src

            def square(key, k, c0):
                if k >= 2:
                    act.wait_ge(sq_used.sem, sq_used.at[key, k - 2])
                act.activation(sq[:, k % 2, c0:], x[:, k, c0:], ACT.Square).then_inc(sq_ready.sem, 1)

            def norm_root(key, c0):
                act.wait_ge(B.full(("norm", key)), B.use(("norm", key)))
                src = B.slot(("norm", key))
                act.activation(rinv[:, c0:], src[:, PSC + c0:], ACT.Sqrt, scale=1.0 / D, bias=NORM_EPS)\
                    .then_inc(rms.sem, 1)

            def operand_hi(key, c0):
                for k in range(KT):
                    act.wait_ge(mod_ready.sem, mod_ready.at[key, k])
                    cp(H(k)[:, c0:], hb[:, k % 2, c0:]).then_inc(act_hi.sem, 1)

            act.wait_ge(c_in, 48)
            act.activation(rows_tmp[:, :, :], rows[:, :, :], ACT.Tanh, scale=0.5).then_inc(cond_th, 1)
            n = 0
            for l in ls:
                c0 = first(l)
                for k in range(KT):
                    if l == 0:
                        act.wait_ge(x_in, 16)
                    else:
                        key = (0, "mlp", 0, 8 + k)
                        act.wait_ge(A.free(key), A.use(key) + 8 * (GROUPS - 1))
                    square((l, 1), k, 0)
                norm_root((l, 1), 0)
                if l == 0:
                    split_hi(0)
                    split_hi(1)
                operand_hi((l, 1), 0)
                act.wait_ge(der_ready.sem, der_ready.at[(l,)])
                if l == 1:
                    act.wait_ge(x_kept, 16)
                nz = 0
                for name, i in (u[0] for u in IN_UNITS):
                    key = (l, name, i)
                    src = ahead(n, key)
                    n += 1
                    if name == "q":
                        cp(q_sb[:, i, c0:], src[:, PSC + c0:]).then_inc(A.free(key), 1)
                        act.wait_ge(A.free(key), A.use(key))
                        act.activation((ltmp, lrin)[i][:, c0:], q_sb[:, i, c0:], ACT.Square).then_inc(lr_sq.sem, 1)
                    elif name == "kv":
                        cp(ckv[:, :], src[:, PSC:]).then_inc(A.free(key), 1)
                        act.wait_ge(A.free(key), A.use(key))
                        act.activation(kT[:, 0, :], ckv[:, :], ACT.Square).then_inc(lr_sq.sem, 1)
                    elif name == "rope":
                        cp(krope[rp, :], src[rp, PSC:]).then_inc(A.free(key), 1)
                    elif name == "z":
                        if nz >= 2:
                            act.wait_ge(z_mixed.sem, z_mixed.at[l, z_order[nz - 2]])
                        cp(wa[:, nz % 2, :], src[:, PSC:])
                        act.activation(z_of(i), src[:, PSC:], ACT.Identity, scale=DR("c0", i)).then_inc(A.free(key), 1)
                        nz += 1
                    elif name == "cg":
                        act.activation(wb[:, i, c0:], src[:, PSC + c0:], ACT.Tanh, scale=0.5).then_inc(A.free(key), 1)
                    elif name == "pool":
                        if i == 0:
                            act.wait_ge(pads.sem, pads.at[(l,)])
                        if l == 0:
                            cp(pp[:, i, 8:8 + CTX], src[:, PSC:PSC + CTX])
                        cp(pp[:, i, PL:PL + LAT], src[:, PSC + CTX:]).then_inc(A.free(key), 1)
                act.wait_ge(B.full((l, "qstat")), B.use((l, "qstat")))
                src = B.slot((l, "qstat"))
                act.activation(lrin[:, c0:], src[:, PSC + c0:], ACT.Sqrt, scale=1.0 / GW, bias=NORM_EPS)\
                    .then_inc(lr_rms.sem, 1)
                act.wait_ge(B.full((l, "kvstat")), B.use((l, "kvstat")))
                src = B.slot((l, "kvstat"))
                act.activation(ltmp[:, :], src[:, PSC:], ACT.Sqrt, scale=1.0 / P, bias=NORM_EPS).then_inc(lr_rms.sem, 1)
                for w, nb in enumerate((4, 2)):
                    act.wait_ge(A.full((l, "v", w)), A.use((l, "v", w)))
                    src = A.slot((l, "v", w))
                    cp(v_tok[:, 4 * w:4 * w + nb, :], src[:, 0:GW * nb]).then_inc(A.free((l, "v", w)), 1)

                def head_operands(h):
                    act.wait_ge(A.full((l, "qh", h)), A.use((l, "qh", h)))
                    src = A.slot((l, "qh", h))
                    cp(qT[0:QD, h % 2, c0:], src[0:QD, PSC + c0:]).then_inc(A.free((l, "qh", h)), 1)
                    act.wait_ge(A.full((l, "kh", h)), A.use((l, "kh", h)))
                    src = A.slot((l, "kh", h))
                    cp(kT[0:NOPE, h % 2, :], src[0:NOPE, PSC:]).then_inc(A.free((l, "kh", h)), 1)

                def softmax(i):
                    e = PSC + (CTX if au[l][i][1] < CTX // P else TOK)
                    act.wait_ge(rowmax.sem, rowmax.at[l, i])
                    act.activation(wa[:, i % 2, 0:e - PSC], psA[:, A.at[(l, "s", i)] % 2, PSC:e], ACT.Exp,
                                           scale=SCALE, bias=stat[:, 1, i:i + 1], accum_out=stat[:, 2, i:i + 1])\
                                               .then_inc(A.free((l, "s", i)), 1)

                def turned(i):
                    e = PSC + (CTX if au[l][i][1] < CTX // P else TOK)
                    if i >= 2:
                        act.wait_ge(B.full((l, "o", i - 2)), B.use((l, "o", i - 2)))
                    act.wait_ge(B.full((l, "pt", i)), B.use((l, "pt", i)))
                    src = B.slot((l, "pt", i))
                    cp(wb[:, i % 2, 0:e - PSC], src[:, PSC:e]).then_inc(B.free((l, "pt", i)), 1)

                head_operands(0)
                for i in range(len(au[l])):
                    h = au[l][i][0]
                    if (i == 0 or au[l][i - 1][0] != h) and h + 1 < HEADS:
                        head_operands(h + 1)
                    softmax(i)
                    if i:
                        turned(i - 1)
                turned(len(au[l]) - 1)
                for i in range(2):
                    act.wait_ge(A.full((l, "att", i)), A.use((l, "att", i)))
                    src = A.slot((l, "att", i))
                    cp(H(6 + i)[:, c0:], src[:, PSC + c0:]).then_inc(y_hi.sem, 1)
                for i in range(2):
                    act.wait_ge(B.free((l, "cmean", i)), B.use((l, "cmean", i)))
                    act.activation(u_sb[:, i, c0:TOK], acc[:, i, c0:], ACT.Square).then_inc(conv_sq.sem, 1)
                for i in range(2):
                    act.wait_ge(B.full((l, "cvar", i)), B.use((l, "cvar", i)))
                    src = B.slot((l, "cvar", i))
                    act.activation(q_sb[:, i, c0:], src[:, PSC + c0:], ACT.Sqrt, scale=1.0 / 64, bias=GN_EPS)\
                        .then_inc(conv_std.sem, 1)
                for i in range(2):
                    act.wait_ge(conv_pre.sem, conv_pre.at[l, i])
                    act.activation(q_sb[:, i, c0:], acc[:, i, c0:], ACT.Tanh).then_inc(conv_th.sem, 1)
                for i in range(2):
                    act.wait_ge(A.full((l, "convp", i)), A.use((l, "convp", i)))
                    src = A.slot((l, "convp", i))
                    cp(H(i)[:, c0:], src[:, PSC + c0:]).then_inc(y_hi.sem, 1)
                for i in range(2):
                    act.wait_ge(A.full((l, "poolp", i)), A.use((l, "poolp", i)))
                    src = A.slot((l, "poolp", i))
                    act.activation(H(4 + i)[:, c0:], src[:, PSC + c0:], ACT.Identity, scale=V(l, "psc", i))\
                        .then_inc(y_hi.sem, 1)
                act.wait_ge(A.free((l, "poolp", 1)), A.use((l, "poolp", 1)))
                act.wait_ge(z_mixed.sem, z_mixed.at[l, z_order[-1]])
                act.activation(zt[:, 5, :], zt[:, 5, :], ACT.Tanh).then_inc(l_lora.sem, 1)
                act.activation(zt[:, 4, c0:], zt[:, 4, c0:], ACT.Tanh, scale=0.5).then_inc(g_th.sem, 1)
                for what, i, *rest in RW:
                    j, d, p = i // 2, i % 2, i % 2
                    un, n_ = (l, j, d), rest[0] if rest else 0
                    if what == "kk":
                        if j:
                            act.wait_ge(prep.sem, prep.at[l, 0, 1])
                        act.activation(nkk[:, :], zt[:, 2 + j, :], ACT.Square, scale=V(l, "kk", j)).then_inc(kk_sq.sem, 1)
                        act.wait_ge(A.full((l, "kk", j)), A.use((l, "kk", j)))
                        src = A.slot((l, "kk", j))
                        act.activation(nkk[:, :], src[:, PSC:], ACT.Sqrt).then_inc(kk_std.sem, 1)
                    elif what == "lora":
                        act.wait_ge(A.full((un, "w2")), A.use((un, "w2")))
                        act.activation(b[:, 0, :], A.slot((un, "w2"))[:, PSC:], ACT.Tanh, scale=0.5,
                                       bias=DR("hw0", 2 * d + j)).then_inc(A.free((un, "w2")), 1)
                        act.wait_ge(A.full((un, "a2")), A.use((un, "a2")))
                        act.activation(b45[:, p, 0, :], A.slot((un, "a2"))[:, PSC:], ACT.Tanh, scale=0.5,
                                       bias=DR("ha0", 2 * d + j)).then_inc(A.free((un, "a2")), 1)
                    elif what == "v":
                        for w, (m0, m1) in enumerate(((0, 7), (7, 13))):
                            act.wait_ge(A.full((l, i, "v", w)), A.use((l, i, "v", w)))
                            src = A.slot((l, i, "v", w)).rearrange("p (m n) -> p m n", n=P)
                            e = min(m1, NC)
                            cp(UV[64:, m0:e, 0:HD], src[64:, 0:e - m0, 0:HD])
                            s_ = max(m0, 1)
                            cp(UV[0:64, s_ - 1:m1 - 1, HD:], src[0:64, s_ - m0:m1 - m0, HD:]).then_inc(v_tp.sem, 1)
                    elif what == "prep" and n_ == 0:
                        act.wait_ge(cum.sem, cum.at[un])
                        act.activation(b[:, 2, :], b[:, 1, :], ACT.Exp, scale=C1).then_inc(exps.sem, 1)
                        act.activation(b3[:, p, :], b[:, 1, :], ACT.Exp, scale=-C1).then_inc(exps.sem, 1)
                    elif what == "prep" and n_ == 1:
                        act.wait_ge(dk.sem, dk.at[un])
                        act.activation(b[:, 0, :], b[:, 0, :], ACT.Exp, scale=C1).then_inc(exps.sem, 1)
                    elif what == "bkt":
                        for w in range(2):
                            act.wait_ge(A.full((un, "bkt", w)), A.use((un, "bkt", w)))
                            k = min(8, NC - 8 * w)
                            cp(BKt[:, p, 8 * w:8 * w + k, :], A.slot((un, "bkt", w))[:, 0:P * k])\
                                .then_inc(A.free((un, "bkt", w)), 1)
                    elif what == "t" and n_:
                        act.wait_ge(A.full((un, "t", n_)), A.use((un, "t", n_)))
                        cp(Tc[:, :, :], chunks(A.slot((un, "t", n_))[:, PSC:])).then_inc(A.free((un, "t", n_)), 1)
                    elif what == "post":
                        act.wait_ge(A.free((l, i, "mean")), A.use((l, i, "mean")))
                        act.activation(b[:, 0, c0:], Y[:, c0:], ACT.Square).then_inc(rw_sq.sem, 1)
                        act.wait_ge(A.full((l, i, "var")), A.use((l, i, "var")))
                        act.activation(b[:, 2, c0:], A.slot((l, i, "var"))[:, PSC + c0:], ACT.Sqrt, scale=1.0 / 64,
                                       bias=LNX_EPS).then_inc(rw_std.sem, 1)
                        act.wait_ge(A.free((l, i, "gate")), A.use((l, i, "gate")))
                        cp(H(2 + i)[:, c0:], Y[:, c0:]).then_inc(y_hi.sem, 1)
                for m in range(KT):
                    ahead(n, (l, "out", m))
                    n += 1
                    if m:
                        act.wait_ge(A.free((l, "out", m - 1)), A.use((l, "out", m - 1)))
                        square((l, 2), m - 1, c0)
                act.wait_ge(A.free((l, "out", KT - 1)), A.use((l, "out", KT - 1)))
                square((l, 2), KT - 1, c0)
                norm_root((l, 2), c0)
                operand_hi((l, 2), c0)
                if l == 0:
                    act.wait_ge(act_lo.sem, act_lo.at[(0, 2), KT - 1])
                    act.wait_ge(rows_kept, 16)
                    act.dma_start(rows2[:, :, :].rearrange("p s n -> p (s n)"), kept_rows.to_broadcast([P, 2 * D]))\
                        .then_inc(rows_in, 16)

                def group(g0, g, end):
                    for j in range(UPG):
                        key, nj = (l, "mlp", g0, j), n + UPG * g0 + j
                        done = 8 * (l * GROUPS + g0) + j + 1
                        act.wait_ge(A.full(key), A.use(key) + 8 * g)
                        src = A.slot(key)
                        if j < 8:
                            if j >= 2:
                                act.wait_ge(A.free((l, "mlp", g0, j - 2)), A.use((l, "mlp", g0, j - 2)) + 8 * g)
                            act.activation(relu[:, j % 2, c0:], src[:, PSC + c0:], ACT.Relu).then_inc(relu_ready, 1)
                        if not (end and j >= UPG - SPL):
                            split_hi(nj + SPL, i_plus=16 * (LOOP[l] // RAW) * g)
                        if j < 8:
                            act.wait_ge(A.free(key), A.use(key) + 8 * g)
                            cp(hid_hi[:, j, c0:], hsq[:, j % 2, c0:]).then_inc(hid_hi_ready, 1)
                        if end and j > 8:
                            before = (l, "mlp", g0, j - 1)
                            act.wait_ge(A.free(before), A.use(before))
                            square((DEPTH, 0), j - 9, CTX)

                if l == 0:
                    with act.Fori(0, GROUPS) as g:
                        group(0, g, False)
                else:
                    with act.Fori(0, GROUPS - 1) as g:
                        group(0, g, False)
                    group(GROUPS - 1, 0, True)
                n += UPG * GROUPS
            last = (DEPTH - 1, "mlp", GROUPS - 1, UPG - 1)
            act.wait_ge(A.free(last), A.use(last))
            square((DEPTH, 0), KT - 1, CTX)
            norm_root((DEPTH, 0), CTX)

        @block.vector
        def _(dve):
            step = Steps()
            tt, ts, stt = dve.tensor_tensor, dve.tensor_scalar, dve.scalar_tensor_tensor

            def derive(l):
                stt(DR("c0", 0, 9), V(l, "mup", 0, 9), -1.0, V(l, "mun", 0, 9), ALU.mult, ALU.subtract)
                ts(DR("hw0", 0, 4), V(l, "w0", 0, 4), 0.5, None, ALU.mult)
                ts(DR("ha0", 0, 4), V(l, "a0", 0, 4), 0.5, None, ALU.mult)
                ts(DR("nkk", 0, 2), V(l, "kk", 0, 2), -1.0, None, ALU.mult)
                ts(DR("s1", 0, 2), V(l, "ka", 0, 2), 0.5, None, ALU.mult)
                ts(DR("s2", 0, 2), V(l, "ka", 0, 2), -0.5, 1.0, ALU.mult, ALU.add)
                ts(DR("hg", 0, 2), V(l, "cgg", 0, 2), 0.5, None, ALU.mult)
                ts(DR("hb", 0, 2), V(l, "cgb", 0, 2), 0.5, None, ALU.mult).then_inc(vector_step, step.up())
                dve.wait_ge(vector_step, step.n)
                ts(DR("c0", 0, 9), DR("c0", 0, 9), 1.0, None, ALU.add).then_inc(der_ready.sem, 1)

            def modulate(l, i, silu, junk, t, plus=0, used=0):
                unit = raw[:, i % RAW].rearrange("p k m -> p (k m)")
                dve.wait_ge(w_in[i % RAW], 16 * (i // RAW + 1) + plus)
                if ada_no[i]:
                    dve.wait_ge(ada_used, ada_no[i] + used)
                for s_ in range(2):
                    feature = mods_flat[:, bass.ds(2 * NT_MODS * l + 2 * t + s_, 1)]
                    k = stt(junk[:, s_, :], unit, 0.5, silu[:, s_, :], ALU.mult, ALU.mult, accum_out=feature)
                k.then_inc(ada_used, 1)

            def modulations(l, t0, t1, used):
                dve.wait_ge(ada_used, used)
                tt(mods[:, l, t0:t1, :], mods[:, l, t0:t1, :], bc(V(l, "ada_b", t0, t1 - t0), [P, t1 - t0, 2], 2), ALU.add)\
                    .then_inc(vector_step, step.up())
                dve.wait_ge(vector_step, step.n)

            def gains(l, name, scale, g):
                o = DR(name, 0, 16).rearrange("p (t s) -> p t s", s=2)
                stt(o, mods[:, l, 8 * scale:8 * scale + 8, :], 1.0, bc(V(l, g, 0, 8), [P, 8, 2], 2), ALU.add, ALU.mult)\
                    .then_inc(vector_step, step.up())
                dve.wait_ge(vector_step, step.n)

            def inverse(key, c0):
                dve.wait_ge(rms.sem, rms.at[key])
                dve.reciprocal(rinv[:, c0:], rinv[:, c0:]).then_inc(B.free(("norm", key)), 1)
                dve.wait_ge(B.free(("norm", key)), B.use(("norm", key)))

            def norm(key, c0, name, shift):
                l = key[0]
                for k in range(KT):
                    if k >= 2:
                        dve.wait_ge(act_lo.sem, act_lo.at[key, k - 2])
                    tt(tb[:, k % 2, c0:], x[:, k, c0:], rinv[:, c0:], ALU.mult).then_inc(vector_step, step.up())
                    dve.wait_ge(vector_step, step.n)
                    for s_, t0, tn in reversed(segs(c0)):
                        i = ts(hb[:, k % 2, t0:t0 + tn], tb[:, k % 2, t0:t0 + tn], DR(name, 2 * k + s_),
                               mods[:, l, 8 * shift + k, s_:s_ + 1], ALU.mult, ALU.add)
                    i.then_inc(mod_ready.sem, 1)

            def add_gated(l, src, m, gate, c0, key):
                for s_, t0, tn in reversed(segs(c0)):
                    i = stt(x[:, m, t0:t0 + tn], src[:, PSC + t0:PSC + t0 + tn], mods[:, l, 8 * gate + m, s_:s_ + 1],
                            x[:, m, t0:t0 + tn], ALU.mult, ALU.add)
                i.then_inc(A.free(key), 1)

            def masked_copy(o, mask, src):
                return dve.copy_predicated(o, mask.bitcast(U32).unsqueeze(1).to_broadcast(list(o.shape)), src)

            turned = []
            mods_flat = mods[:, :, :, :].rearrange("p l t s -> p (l t s)")
            dve.wait_ge(c_in, 48)
            dve.wait_ge(cond_th, 1)
            stt(rows[:, :, :], rows_tmp[:, :, :], 1.0, rows[:, :, :], ALU.add, ALU.mult).then_inc(cond_ready, 1)
            dve.wait_ge(cond_ready, 1)
            for l in ls:
                c0 = first(l)
                derive(l)
                if l == 0:
                    for t in range(16):
                        modulate(0, t, rows, rows_tmp, t)
                        if t == 7:
                            inverse((0, 1), 0)
                    modulations(0, 0, 16, 16)
                gains(l, "A1", 1, "n1")
                if l:
                    inverse((l, 1), 0)
                norm((l, 1), 0, "A1", 0)
                if l == 1:
                    dve.wait_ge(x_kept, 16)
                nz, feature, at = 0, 16, 16
                for n_, (name, i) in enumerate(u[0] for u in IN_UNITS):
                    key = (l, name, i)
                    at += 1
                    for _ in range(IN_ADA[n_] if l == 0 else 0):
                        modulate(0, at, rows, psB, feature)
                        at, feature = at + 1, feature + 1
                    if name == "z":
                        dve.wait_ge(A.free(key), A.use(key))
                        z, p = z_of(i), wa[:, nz % 2, :]
                        for o, s_, t in ((1, 0, CTX - 1), (CTX + 1, CTX, LAT - 1)):
                            k = stt(z[:, o:o + t], p[:, s_:s_ + t], V(l, "mup", i), z[:, o:o + t], ALU.mult, ALU.add)
                        k.then_inc(vector_step, step.up())
                        nz += 1
                        dve.wait_ge(vector_step, step.n)
                        for o, s_, t in ((0, 1, CTX - 1), (CTX, CTX + 1, LAT - 1)):
                            k = stt(z[:, o:o + t], p[:, s_:s_ + t], V(l, "mun", i), z[:, o:o + t], ALU.mult, ALU.add)
                        k.then_inc(z_mixed.sem, 1)
                    elif name == "cg":
                        dve.wait_ge(A.free(key), A.use(key))
                        ts(wb[:, i, c0:], wb[:, i, c0:], 0.5, 0.5, ALU.mult, ALU.add).then_inc(vector_step, step.up())
                    elif name == "cv":
                        dve.wait_ge(A.full(key), A.use(key))
                        src = A.slot(key)
                        if i == 0:
                            dve.wait_ge(pads.sem, pads.at[(l,)])
                            dve.wait_ge(vector_step, step.n)
                        if l == 0:
                            tt(u_sb[:, i, 15:15 + CTX], src[:, PSC:PSC + CTX], wb[:, i, 0:CTX], ALU.mult)
                        tt(u_sb[:, i, UL:UL + LAT], src[:, PSC + CTX:], wb[:, i, CTX:], ALU.mult)\
                            .then_inc(A.free(key), 1)
                if l == 0:
                    modulations(0, 16, 48, 48)

                dve.wait_ge(lr_rms.sem, lr_rms.at[l, 0])
                dve.reciprocal(lrin[:, c0:], lrin[:, c0:]).then_inc(B.free((l, "qstat")), 1)
                dve.wait_ge(B.free((l, "qstat")), B.use((l, "qstat")))
                for i in range(2):
                    q = stt(q_sb[:, i, c0:], q_sb[:, i, c0:], V(l, "qn", i), lrin[:, c0:], ALU.mult, ALU.mult)
                q.then_inc(lr_normed.sem, 1)
                dve.wait_ge(lr_rms.sem, lr_rms.at[l, 1])
                dve.reciprocal(ltmp[:, :], ltmp[:, :]).then_inc(B.free((l, "kvstat")), 1)
                dve.wait_ge(B.free((l, "kvstat")), B.use((l, "kvstat")))
                stt(ckv[:, :], ckv[:, :], V(l, "kvn"), ltmp[:, :], ALU.mult, ALU.mult).then_inc(lr_normed.sem, 1)
                dve.wait_ge(mix_in, 48 * (l + 1))

                def rotate(key, o, signal, skey):
                    dve.wait_ge(B.full(key), B.use(key))
                    src = B.slot(key)
                    if turned:
                        dve.wait_ge(turned[-1][0].sem, turned[-1][0].at[turned[-1][1]])
                    turned.append((signal, skey))
                    tt(rtmp[rp, :], src[rp, PSC + CTX:], cs[rp, 1, :], ALU.mult).then_inc(B.free(key), 1)
                    tt(o, o, cs[rp, 0, :], ALU.mult).then_inc(vector_step, step.up())
                    dve.wait_ge(vector_step, step.n)
                    dve.wait_ge(B.free(key), B.use(key))
                    tt(o, o, rtmp[rp, :], ALU.add).then_inc(signal.sem, 1)

                rotate((l, "krot"), krope[rp, CTX:], kr_ready, (l,))

                span0, width = (0, CTX + 15 + LAT) if l == 0 else (UL - 15, LAT)
                ctap = u_acc
                taps = [(t, i) for t in range(TAPS) for i in range(2)]
                done_taps = [0]
                marks = {}

                def tap(count):
                    for _ in range(count):
                        if done_taps[0] >= len(taps):
                            return
                        t, i = taps[done_taps[0]]
                        done_taps[0] += 1
                        w = V(l, "dw", 2 * t + i)
                        u = u_sb[:, i, span0 + t:span0 + t + width]
                        o = ctap[:, i, 0:width]
                        if t == 0:
                            if i == 0:
                                dve.wait_ge(A.free((l, "cv", 0)), A.use((l, "cv", 0)))
                                dve.wait_ge(A.free((l, "cv", 1)), A.use((l, "cv", 1)))
                            k = ts(o, u, w, V(l, "db", i), ALU.mult, ALU.add)
                        else:
                            dve.wait_ge(vector_step, marks[i])
                            k = stt(o, u, w, o, ALU.mult, ALU.add)
                        k.then_inc(vector_step, step.up())
                        marks[i] = step.n

                def head_rotation(h):
                    dve.wait_ge(A.free((l, "qh", h)), A.use((l, "qh", h)))
                    rotate((l, "qrot", h), qT[rp, h % 2, CTX:], q_rot, (l, h))

                def maxima(i):
                    e = PSC + (CTX if au[l][i][1] < CTX // P else TOK)
                    dve.wait_ge(A.full((l, "s", i)), A.use((l, "s", i)))
                    src = A.slot((l, "s", i))
                    dve.tensor_reduce(stat[:, 0, i:i + 1], src[:, PSC:e], AX_X, ALU.max, negate=True)\
                        .then_inc(vector_step, step.up())
                    dve.wait_ge(vector_step, step.n)
                    ts(stat[:, 1, i:i + 1], stat[:, 0, i:i + 1], SCALE, None, ALU.mult).then_inc(rowmax.sem, 1)

                def mixed(i):
                    h, q = au[l][i]
                    dve.wait_ge(A.free((l, "s", i)), A.use((l, "s", i)))
                    dve.reciprocal(stat[:, 3, i:i + 1], stat[:, 2, i:i + 1]).then_inc(vector_step, step.up())
                    dve.wait_ge(vector_step, step.n)
                    dve.wait_ge(B.full((l, "o", i)), B.use((l, "o", i)))
                    src = B.slot((l, "o", i))
                    ts(otok[:, q, HD * h:HD * (h + 1)], src[:, 0:HD], stat[:, 3, i:i + 1], None, ALU.mult)\
                        .then_inc(B.free((l, "o", i)), 1)

                head_rotation(0)
                per = -(-len(taps) // len(au[l]))
                for i in range(len(au[l])):
                    h = au[l][i][0]
                    if (i == 0 or au[l][i - 1][0] != h) and h + 1 < HEADS:
                        head_rotation(h + 1)
                    maxima(i)
                    tap(per)
                    if i > 1:
                        mixed(i - 2)
                mixed(len(au[l]) - 2)
                mixed(len(au[l]) - 1)

                def low_part(k, key, ykey, scale=None):
                    dve.wait_ge(y_hi.sem, y_hi.at[ykey])
                    src = psA[:, A.at[key] % 2, PSC + c0:]
                    if scale is None:
                        i = tt(L(k)[:, c0:], src, f32(H(k))[:, c0:], ALU.subtract)
                    else:
                        i = stt(L(k)[:, c0:], src, scale, f32(H(k))[:, c0:], ALU.mult, ALU.subtract)
                    i.then_inc(A.free(key), 1)

                for i in range(2):
                    low_part(6 + i, (l, "att", i), (l, "att", i))
                dve.wait_ge(vector_step, step.n)
                for i in range(2):
                    if l == 0:
                        ts(acc[:, i, 0:CTX], ctap[:, i, 0:CTX], 1.0, None, ALU.mult)
                        o = CTX + 15
                    else:
                        o = 0
                    ts(acc[:, i, CTX:], ctap[:, i, o:o + LAT], 1.0, None, ALU.mult).then_inc(conv_sum.sem, 1)
                for i in range(2):
                    dve.wait_ge(B.full((l, "cmean", i)), B.use((l, "cmean", i)))
                    src = B.slot((l, "cmean", i))
                    dve.wait_ge(conv_sum.sem, conv_sum.at[l, i])
                    stt(acc[:, i, c0:], src[:, PSC + c0:], -1.0 / 64, acc[:, i, c0:], ALU.mult, ALU.add)\
                        .then_inc(B.free((l, "cmean", i)), 1)
                for i in range(2):
                    dve.wait_ge(conv_std.sem, conv_std.at[l, i])
                    dve.reciprocal(q_sb[:, i, c0:], q_sb[:, i, c0:]).then_inc(B.free((l, "cvar", i)), 1)
                    dve.wait_ge(B.free((l, "cvar", i)), B.use((l, "cvar", i)))
                    tt(acc[:, i, c0:], acc[:, i, c0:], q_sb[:, i, c0:], ALU.mult).then_inc(vector_step, step.up())
                    dve.wait_ge(vector_step, step.n)
                    ts(acc[:, i, c0:], acc[:, i, c0:], DR("hg", i), DR("hb", i), ALU.mult, ALU.add)\
                        .then_inc(conv_pre.sem, 1)
                for i in range(2):
                    dve.wait_ge(conv_th.sem, conv_th.at[l, i])
                    stt(acc[:, i, c0:], q_sb[:, i, c0:], 1.0, acc[:, i, c0:], ALU.add, ALU.mult)\
                        .then_inc(conv_act.sem, 1)
                for i in range(2):
                    low_part(i, (l, "convp", i), (l, "conv", i))
                for i in range(2):
                    low_part(4 + i, (l, "poolp", i), (l, "pool", i), V(l, "psc", i))

                dve.wait_ge(rw_in, 32 * (l + 1))
                dve.wait_ge(g_th.sem, g_th.at[(l,)])
                ts(zt[:, 4, c0:], zt[:, 4, c0:], 0.5, 0.5, ALU.mult, ALU.add).then_inc(vector_step, step.up())
                for what, i, *rest in RW:
                    j, d, p = i // 2, i % 2, i % 2
                    un, n_ = (l, j, d), rest[0] if rest else 0
                    ba, bk = b45[:, p, 0, :], b45[:, p, 1, :]
                    tri = lambda incl: K("tri", C, (2 * d + incl) * C)
                    lo = lambda i_: K("lo" if d == 0 else "up", C, i_ * C)
                    up = lambda i_: K("up" if d == 0 else "lo", C, i_ * C)
                    m3 = lambda m: m.unsqueeze(1).to_broadcast([P, NC, C])
                    if what == "kk":
                        dve.wait_ge(kk_std.sem, kk_std.at[l, j])
                        ts(nkk[:, :], nkk[:, :], 1e-12, None, ALU.max).then_inc(A.free((l, "kk", j)), 1)
                        dve.wait_ge(A.free((l, "kk", j)), A.use((l, "kk", j)))
                        dve.reciprocal(nkk[:, :], nkk[:, :]).then_inc(vector_step, step.up())
                        dve.wait_ge(vector_step, step.n)
                        stt(nkk[:, :], zt[:, 2 + j, :], DR("nkk", j), nkk[:, :], ALU.mult, ALU.mult)\
                            .then_inc(vector_step, step.up())
                        dve.wait_ge(vector_step, step.n)
                    elif what == "prep" and n_ == 0:
                        dve.wait_ge(A.free((un, "w2")), A.use((un, "w2")))
                        ts(b[:, 0, :], b[:, 0, :], 1.0, None, ALU.add).then_inc(vector_step, step.up())
                        dve.wait_ge(vector_step, step.n)
                        way = slice(None) if d == 0 else slice(None, None, -1)
                        dve.tensor_tensor_scan(b[:, 1, way], reset[:, :], b[:, 0, way], 0.0, ALU.mult, ALU.add)\
                            .then_inc(cum.sem, 1)
                    elif what == "prep" and n_ == 1:
                        dve.wait_ge(cum.sem, cum.at[un])
                        tt(b[:, 0, :], b[:, 1, :], b[:, 0, :], ALU.subtract).then_inc(dk.sem, 1)
                        dve.wait_ge(A.free((un, "a2")), A.use((un, "a2")))
                        ts(bk, ba, -0.5, -0.5, ALU.mult, ALU.add).then_inc(vector_step, step.up())
                        rate = step.n
                    elif what == "prep" and n_ == 2:
                        dve.wait_ge(vector_step, rate)
                        ts(ba, ba, DR("s1", j), DR("s2", j), ALU.mult, ALU.add).then_inc(vector_step, step.up())
                        tt(bk, bk, nkk[:, :], ALU.mult)
                        dve.wait_ge(vector_step, step.n)
                        tt(ba, ba, zt[:, 2 + j, :], ALU.mult).then_inc(vector_step, step.up())
                        rate = step.n
                    elif what == "prep" and n_ == 3:
                        dve.wait_ge(vector_step, rate)
                        dve.wait_ge(exps.sem, exps.at[un, 1])
                        if d == 0:
                            ts(kds[:, j, :], ba, 1.0, None, ALU.mult)
                        else:
                            tt(kds[:, j, :], kds[:, j, :], ba, ALU.add)
                        for part, s_ in HALF:
                            tt(BK[part, :, s_, :], chunks(bk[part]), chunks(b3[part, p, :]), ALU.mult)
                    elif what == "prep" and n_ == 4:
                        for part, s_ in HALF:
                            tt(BK[part, :, 1 - s_, :], chunks(ba[part]), chunks(b3[part, p, :]), ALU.mult)
                            tt(Q[part, p, 2 * s_ + 1, :], zt[part, j, :], b[part, 2, :], ALU.mult)
                    elif what == "prep" and n_ == 5:
                        ts(PC[:, p, :], chunks(b[:, 2, :])[:, :, C - 1 if d == 0 else 0], 1.0, None, ALU.mult)
                        dve.wait_ge(exps.sem, exps.at[un, 2])
                        for part, s_ in HALF:
                            k = tt(Q[part, p, 2 * s_, :], nkk[part, :], b[part, 0, :], ALU.mult)
                        k.then_inc(prep.sem, 1)
                    elif what == "v":
                        for w, (m0, m1) in enumerate(((0, 7), (7, 13))):
                            dve.wait_ge(v_tp.sem, v_tp.at[l, i, w])
                            src = A.slot((l, i, "v", w)).rearrange("p (m n) -> p m n", n=P)
                            e = min(m1, NC)
                            ts(SV[64:, m0:e, 0:HD], src[64:, 0:e - m0, 0:HD], 1.0, None, ALU.mult)
                            s_ = max(m0, 1)
                            ts(SV[0:64, s_ - 1:m1 - 1, HD:], src[0:64, s_ - m0:m1 - m0, HD:], 1.0, None, ALU.mult)\
                                .then_inc(A.free((l, i, "v", w)), 1)
                    elif what == "gram":
                        g = n_
                        if g == 0:
                            dve.wait_ge(prep.sem, prep.at[un])
                        dve.wait_ge(A.full((un, "gram", g)), A.use((un, "gram", g)))
                        src = A.slot((un, "gram", g)).rearrange("p (h c n) -> p h c n", h=2, n=P)
                        tt(M[:, p, :, 4 * g:4 * g + 4, :], src[:, :, :, C:],
                           bc(tri(1), [P, 1, C], 1).unsqueeze(1).to_broadcast([P, 2, 4, C]), ALU.mult)
                        for part, s_ in HALF:
                            other = HALF[1 - s_][0]
                            mask = lambda p_: tri(0)[p_].unsqueeze(1).to_broadcast([64, 4, C])
                            tt(chunks(Q[other, p, 2 * s_, :])[:, 4 * g:4 * g + 4, :], src[other, s_, :, 0:C], mask(other),
                               ALU.mult)
                            k = tt(LT[part, 4 * g:4 * g + 4, :], src[part, s_, :, 0:C], mask(part), ALU.mult)
                        k.then_inc(A.free((un, "gram", g)), 1)
                    elif what == "t" and n_ == 0:
                        dve.wait_ge(A.free((un, "gram", 2)), A.use((un, "gram", 2)))
                        tt(XT[:, p], LT[:, :, :], m3(up(0)), ALU.mult).then_inc(vector_step, step.up())
                        dve.wait_ge(vector_step, step.n)
                        tt(XT[:, p], XT[:, p], m3(K("istack", C)), ALU.add).then_inc(xt_one.sem, 1)
                        dve.wait_ge(A.full((un, "t", 0)), A.use((un, "t", 0)))
                        src = chunks(A.slot((un, "t", 0))[:, PSC:])
                        tt(X[:, :, :], src, m3(lo(0)), ALU.mult).then_inc(A.free((un, "t", 0)), 1)
                        dve.wait_ge(A.free((un, "t", 0)), A.use((un, "t", 0)))
                        tt(X[:, :, :], X[:, :, :], m3(K("istack", C)), ALU.add).then_inc(x_one.sem, 1)
                    elif what == "x":
                        dve.wait_ge(A.full((un, "x", n_)), A.use((un, "x", n_)))
                        src = chunks(A.slot((un, "x", n_))[:, PSC:])
                        masked_copy(X[:, :, :], lo(n_), src).then_inc(A.free((un, "x", n_)), 1)
                    elif what == "xt":
                        dve.wait_ge(A.full((un, "xt", n_)), A.use((un, "xt", n_)))
                        src = chunks(A.slot((un, "xt", n_))[:, PSC:])
                        masked_copy(XT[:, p], up(n_), src).then_inc(A.free((un, "xt", n_)), 1)
                    elif what == "w":
                        dve.wait_ge(scan_full.sem, scan_full.at[un, "w", n_])
                        ts(Wc[:, n_ % 2, :], scan_w, 1.0, None, ALU.mult).then_inc(scan_read.sem, 1)
                    elif what == "u":
                        dve.wait_ge(scan_full.sem, scan_full.at[un, "u", n_])
                        for part, s_ in HALF:
                            k = ts(UV[part, chunk_order(d)[n_], HD * s_:HD * (s_ + 1)], scan_u[part], 1.0, None, ALU.mult)
                        k.then_inc(scan_read.sem, 1)
                    elif what == "s" and n_ < NC - 1:
                        c, after = chunk_order(d)[n_:n_ + 2]
                        dve.wait_ge(scan_full.sem, scan_full.at[un, "s", n_])
                        dve.wait_ge(s_dec.sem, s_dec.at[un, n_])
                        for part, s_ in HALF:
                            k = stt(SV[part, after, HD * s_:HD * (s_ + 1)], scan_s[part], PC[part, p, c:c + 1],
                                    SP[part, :], ALU.mult, ALU.add)
                        k.then_inc(scan_read.sem, 1)
                    elif what == "s":
                        dve.wait_ge(y_full.sem, y_full.at[un])
                        src = psB[:, 0, PSC + c0:]
                        if d == 0:
                            if j:
                                dve.wait_ge(y_lo.sem, y_lo.at[l, 0])
                            ts(Y[:, c0:], src, 1.0, None, ALU.mult).then_inc(y_read.sem, 1)
                        else:
                            tt(Y[:, c0:], src, Y[:, c0:], ALU.add).then_inc(y_read.sem, 1)
                    elif what == "post":
                        stt(b[:, 1, c0:], zt[:, i, c0:], V(l, "rk", i), kds[:, i, c0:], ALU.mult, ALU.mult)\
                            .then_inc(bon.sem, 1)
                        dve.wait_ge(A.full((l, i, "bonus")), A.use((l, i, "bonus")))
                        src = A.slot((l, i, "bonus"))
                        tt(b3[:, 1, c0:], src[:, PSC + c0:], zv[:, i, C + c0:C + TOK], ALU.mult)\
                            .then_inc(A.free((l, i, "bonus")), 1)
                        dve.wait_ge(A.full((l, i, "mean")), A.use((l, i, "mean")))
                        src = A.slot((l, i, "mean"))
                        dve.wait_ge(y_read.sem, y_read.at[l, i, 1])
                        stt(Y[:, c0:], src[:, PSC + c0:], -1.0 / 64, Y[:, c0:], ALU.mult, ALU.add)\
                            .then_inc(A.free((l, i, "mean")), 1)
                        dve.wait_ge(rw_std.sem, rw_std.at[l, i])
                        dve.reciprocal(b[:, 2, c0:], b[:, 2, c0:]).then_inc(A.free((l, i, "var")), 1)
                        dve.wait_ge(A.free((l, i, "var")), A.use((l, i, "var")))
                        tt(Y[:, c0:], Y[:, c0:], b[:, 2, c0:], ALU.mult).then_inc(vector_step, step.up())
                        dve.wait_ge(vector_step, step.n)
                        ts(Y[:, c0:], Y[:, c0:], V(l, "lg", i), V(l, "lb", i), ALU.mult, ALU.add)\
                            .then_inc(vector_step, step.up())
                        dve.wait_ge(vector_step, step.n)
                        tt(Y[:, c0:], Y[:, c0:], b3[:, 1, c0:], ALU.add).then_inc(vector_step, step.up())
                        dve.wait_ge(vector_step, step.n)
                        dve.wait_ge(A.full((l, i, "gate")), A.use((l, i, "gate")))
                        src = A.slot((l, i, "gate"))
                        tt(Y[:, c0:], src[:, PSC + c0:], Y[:, c0:], ALU.mult).then_inc(A.free((l, i, "gate")), 1)
                dve.wait_ge(x_in, 16 * (l + 2))
                for m in range(KT):
                    key = (l, "out", m)
                    dve.wait_ge(A.full(key), A.use(key))
                    add_gated(l, A.slot(key), m, 2, c0, key)
                gains(l, "A2", 4, "n2")
                inverse((l, 2), c0)
                norm((l, 2), c0, "A2", 3)
                if l == 0:
                    dve.wait_ge(rows_in, 16)

                def group(g0, g):
                    i, t = mlp0[l] + LOOP[l] * g0, 0
                    for j in range(UPG):
                        i += 1
                        for _ in range(ada_after(l, j)):
                            modulate(1, i, rows2, psB, t + 12 * g, 16 * (LOOP[l] // RAW) * g, 12 * g)
                            i, t = i + 1, t + 1
                        key = (l, "mlp", g0, j)
                        dve.wait_ge(A.full(key), A.use(key) + 8 * g)
                        src = A.slot(key)
                        done = 8 * (l * GROUPS + g0) + j + 1
                        if j < 8:
                            dve.wait_ge(relu_ready, done + 8 * g)
                            stt(hsq[:, j % 2, c0:], src[:, PSC + c0:], 0.0, relu[:, j % 2, c0:], ALU.max, ALU.mult)\
                                .then_inc(A.free(key), 1)
                            dve.wait_ge(hid_hi_ready, done + 8 * g)
                            tt(hid_lo[:, j, c0:], hsq[:, j % 2, c0:], f32(hid_hi[:, j, c0:]), ALU.subtract)\
                                .then_inc(hid_ready, 1)
                        else:
                            add_gated(l, src, j - 8, 5, c0, key)

                if l == 0:
                    with dve.Fori(0, GROUPS) as g:
                        group(0, g)
                    modulations(1, 0, 48, 96)
                else:
                    with dve.Fori(0, GROUPS - 1) as g:
                        group(0, g)
                    group(GROUPS - 1, 0)
            key = (DEPTH, 0)
            inverse(key, CTX)
            for k in range(KT):
                stt(x[:, k, CTX:], x[:, k, CTX:], vec[:, V_FINAL + k:V_FINAL + k + 1], rinv[:, CTX:],
                                   ALU.mult, ALU.mult).then_inc(fin_ready.sem, 1)

        @block.gpsimd
        def _(pool):
            step = Steps()

            def split_lo(n, plus=0, i_plus=0):
                i = unit_of_split[n]
                pool.wait_ge(w_hi, n + 1 + plus)
                pool.tensor_tensor(wlo[:, n % SPL], raw[:, i % RAW], f32(whi[:, n % SPL]), ALU.subtract)\
                    .then_inc(w_lo, 1)

            def operand_lo(key, c0):
                for k in range(KT):
                    pool.wait_ge(act_hi.sem, act_hi.at[key, k])
                    pool.tensor_tensor(L(k)[:, c0:], hb[:, k % 2, c0:], f32(H(k))[:, c0:], ALU.subtract)\
                        .then_inc(act_lo.sem, 1)

            n = 0
            split_lo(0)
            split_lo(1)
            for l in ls:
                c0 = first(l)
                operand_lo((l, 1), 0)
                pool.wait_ge(act_lo.sem, act_lo.at[(l, 1), KT - 1])
                if l == 1:
                    pool.wait_ge(x_kept, 16)
                pool.memset(u_sb[:, :, :], 0.0)
                pool.memset(zv[:, :, :], 0.0)
                pool.memset(pp[:, :, :], 0.0).then_inc(pads.sem, 1)
                for i in range(N_IN):
                    split_lo(n + SPL)
                    n += 1
                pool.wait_ge(pads.sem, pads.at[(l,)])
                pool.wait_ge(mix_in, 48 * (l + 1))
                pool.wait_ge(ada_used, NT_MODS)
                for i in range(2):
                    pool.wait_ge(A.free((l, "pool", i)), A.use((l, "pool", i)))
                for i in range(2):
                    cur, buf = pp[:, i, :], ps[:, i, :]
                    pool.tensor_tensor(buf[:, 1:PWID], cur[:, 0:PWID - 1], cur[:, 1:PWID], ALU.add)\
                        .then_inc(pool_step, step.up())
                    widths = ((2, 4), (8, 16))[i]
                    w, src, dst = 2, buf, ptmp[:, :]
                    for part, want in ((slice(0, 64), widths[0]), (slice(64, P), widths[1])):
                        while w < want:
                            h = w // 2
                            pool.wait_ge(pool_step, step.n)
                            pool.tensor_tensor(dst[:, w:PWID - w], src[:, w - h:PWID - w - h], src[:, w + h:PWID - w + h],
                                                    ALU.add).then_inc(pool_step, step.up())
                            src, dst, w = dst, src, 2 * w
                        pool.wait_ge(pool_step, step.n)
                        for s_, t0, tn in segs(c0):
                            o = PL if s_ == 0 else 8
                            pool.tensor_tensor(rcnt[part, i, t0:t0 + tn], src[part, o:o + tn], rcnt[part, i, t0:t0 + tn],
                                                    ALU.mult).then_inc(pool_step, step.up())
                    pool.wait_ge(pool_step, step.n)
                    for s_, t0, tn in segs(c0):
                        o = PL if s_ == 0 else 8
                        k = pool.tensor_tensor(rcnt[:, i, t0:t0 + tn], rcnt[:, i, t0:t0 + tn], cur[:, o:o + tn], ALU.subtract)
                    k.then_inc(pool_d.sem, 1)
                    pool.wait_ge(pool_d.sem, pool_d.at[l, i])
                pool.wait_ge(kr_ready.sem, kr_ready.at[(l,)])
                for h in hs:
                    if h >= 2:
                        last = max(i for i, (hh_, _) in enumerate(au[l]) if hh_ == h - 2)
                        pool.wait_ge(A.full((l, "s", last)), A.use((l, "s", last)))
                    pool.tensor_copy(kT[rp, h % 2, :], krope[rp, :]).then_inc(k_full.sem, 1)
                pool.wait_ge(A.free((l, "poolp", 1)), A.use((l, "poolp", 1)))
                pool.wait_ge(k_full.sem, k_full.at[l, HEADS - 1])
                for p in range(2):
                    pool.memset(Q[64:, p, 1, :], 0.0)
                    k = pool.memset(Q[0:64, p, 3, :], 0.0)
                k.then_inc(rw_zero.sem, 1)
                for i in range(4):
                    un, order, p = (l, i // 2, i % 2), chunk_order(i % 2), i % 2
                    if i:
                        pool.wait_ge(y_full.sem, y_full.at[un] - 1)
                    pool.memset(SV[0:64, order[0], 0:HD], 0.0)
                    pool.memset(SV[64:, order[0], HD:], 0.0).then_inc(s_zero.sem, 1)
                    pool.wait_ge(prep.sem, prep.at[un])
                    pool.wait_ge(s_zero.sem, s_zero.at[un])
                    for n_, c in enumerate(order[:-1]):
                        if n_:
                            pool.wait_ge(scan_read.sem, scan_read.at[un, "s", n_ - 1])
                        for part, s_ in HALF:
                            k = pool.tensor_scalar(SP[part, :], SV[part, c, HD * s_:HD * (s_ + 1)], PC[part, p, c:c + 1],
                                                   0.0, ALU.mult, ALU.add)
                        k.then_inc(s_dec.sem, 1)
                    if i % 2:
                        pool.wait_ge(s_dec.sem, s_dec.at[un, NC - 2])
                        pool.wait_ge(y_hi.sem, y_hi.at[l, "rw", i // 2])
                        pool.tensor_tensor(L(2 + i // 2)[:, c0:], Y[:, c0:], f32(H(2 + i // 2))[:, c0:], ALU.subtract)\
                            .then_inc(y_lo.sem, 1)
                        pool.wait_ge(y_lo.sem, y_lo.at[l, i // 2])
                for m in range(KT):
                    split_lo(n + SPL)
                    n += 1
                operand_lo((l, 2), c0)

                def group(g0, g, end):
                    for j in range(UPG - (SPL if end else 0)):
                        split_lo(n + UPG * g0 + j + SPL, UPG * g)

                if l == 0:
                    with pool.Fori(0, GROUPS) as g:
                        group(0, g, False)
                else:
                    with pool.Fori(0, GROUPS - 1) as g:
                        group(0, g, False)
                    group(GROUPS - 1, 0, True)
                n += UPG * GROUPS

        @block.sync
        def _(sp):
            def load(i, plus_lo=0, plus_ada=0, at=None, plus=0):
                if i >= RAW:
                    before = i - RAW
                    if before in split_no:
                        sp.wait_ge(w_lo, split_no[before] + 1 + plus_lo)
                    else:
                        sp.wait_ge(ada_used, ada_no[before] + 1 + plus_ada)
                src = stream[i] if at is None else stream[bass.ds(at, 1)].rearrange("a p n -> (a p) n")
                sp.dma_start(raw[:, i % RAW], src.rearrange("p (k m) -> p k m", k=KT)).then_inc(w_in[i % RAW], 16)

            sp.dma_start(rows[:, :, :].rearrange("p s n -> p (s n)"), cond_in.to_broadcast([P, 2 * D])).then_inc(c_in, 16)
            sp.dma_start(cst[:, :], consts).then_inc(c_in, 16)
            sp.dma_start(vec[:, :], vecs).then_inc(c_in, 16)
            sp.dma_start(x[:, :, :], xT).then_inc(x_in, 16)
            for i in range(RAW):
                load(i)
            sp.wait_ge(cond_ready, 1)
            sp.dma_start(kept_rows, rows[0:1, :, :].rearrange("p s n -> p (s n)")).then_inc(rows_kept, 16)
            n = RAW
            for l in ls:
                first_in = 16 if l == 0 else mlp0[0] + LOOP[0] * GROUPS
                while n < first_in + RAW + 1:
                    load(n)
                    n += 1
                if l == 1:
                    sp.wait_ge(A.free((0, "mlp", 0, 15)), A.use((0, "mlp", 0, 15)) + 8 * (GROUPS - 1))
                    sp.wait_ge(A.free((0, "mlp", 0, 14)), A.use((0, "mlp", 0, 14)) + 8 * (GROUPS - 1))
                    sp.dma_start(kept, x[:, :, CTX:]).then_inc(x_kept, 16)
                sp.wait_ge(act_lo.sem, act_lo.at[(l, 1), KT - 1])
                if l == 1:
                    sp.wait_ge(x_kept, 16)
                sp.dma_start(cs[:, :, :], big[:, BIG["cos"]:BIG["cos"] + 2 * LAT].rearrange("p (a n) -> p a n", a=2))\
                    .then_inc(mix_in, 16)
                sp.dma_start(rcnt[:, :, :], big[:, BIG["rcnt"]:].rearrange("p (a n) -> p a n", a=2))\
                    .then_inc(mix_in, 16)
                sp.dma_start(sw_a[:, :], small_a[l]).then_inc(mix_in, 16)
                while n < mlp0[l] - 8 + RAW:
                    load(n)
                    n += 1
                sp.wait_ge(A.free((l, "poolp", 1)), A.use((l, "poolp", 1)))
                sp.dma_start(reset[:, :], big[:, 0:TOK]).then_inc(rw_in, 16)
                sp.dma_start(sw_r[:, :], small_r[l]).then_inc(rw_in, 16)
                sp.wait_ge(y_lo.sem, y_lo.at[l, 1])
                if l == 0:
                    sp.dma_start(x[:, :, :], xT).then_inc(x_in, 16)
                else:
                    sp.dma_start(x[:, :, CTX:], kept).then_inc(x_in, 16)
                while n < mlp0[l]:
                    load(n)
                    n += 1
                per = LOOP[l]
                with sp.Fori(0, GROUPS) as g:
                    for i in range(per):
                        load(mlp0[l] + i, UPG * g, 12 * g, mlp0[l] + i + per * g)
                n = mlp0[l] + per * GROUPS
            for k in range(KT):
                sp.wait_ge(fin_ready.sem, fin_ready.at[(k,)])
                sp.dma_start(out[:, k, :], x[:, k, CTX:]).then_inc(out_done, 16)
            sp.wait_ge(out_done, 16 * KT)


def _tables():
    c = np.zeros((P, CST["end"]), np.float32)
    r, q = np.arange(P)[:, None], np.arange(P)[None, :]
    c[:, CST["ident"]:][:, :P] = r == q
    c[:, CST["ones"]:][:, :P] = 1
    c[:, CST["bones"]:][:, :P] = r // 64 == q // 64
    r, q = r % 64, np.arange(64)[None, :]
    for i in range(6):
        h = 1 << i
        lo = (r // (2 * h) == q // (2 * h)) & (r // h % 2 == 1) & (q // h % 2 == 0)
        up = (r // (2 * h) == q // (2 * h)) & (r // h % 2 == 0) & (q // h % 2 == 1)
        c[:, CST["lo"] + 64 * i:][:, :64] = lo
        c[:, CST["up"] + 64 * i:][:, :64] = up
    for i, m in enumerate((r < q, r <= q, r > q, r >= q)):
        c[:, CST["tri"] + 64 * i:][:, :64] = m
    c[:, CST["istack"]:][:, :64] = r == q
    for a in (0, 16):
        for m in range(8):
            c[NOPE + a + 8 + m, CST["rot"] + a + m] = -1
            c[NOPE + a + m, CST["rot"] + a + 8 + m] = 1
    g = np.zeros((P, BIG["end"]), np.float32)
    t = np.arange(TOK)
    g[:, BIG["reset"]:][:, :TOK] = t % C != 0
    nf = ROPE // 4
    freq = (10000.0 ** (-np.arange(nf, dtype=np.float32) / nf)).astype(np.float32)
    for row in range(ROPE):
        pos = (np.arange(LAT) // 64 if row < 16 else np.arange(LAT) % 64).astype(np.float32)
        ang = pos * freq[row % 8]
        g[NOPE + row, BIG["cos"]:][:LAT] = np.cos(ang)
        g[NOPE + row, BIG["sin"]:][:LAT] = np.sin(ang)
    for i, w in enumerate((2, 4, 8, 16)):
        for t0, n in ((0, CTX), (CTX, LAT)):
            s = np.arange(n)
            cnt = np.clip(s + w - w // 2, 0, n) - np.clip(s - w // 2, 0, n)
            g[64 * (i % 2):64 * (i % 2) + 64, BIG["rcnt"] + TOK * (i // 2) + t0:][:, :n] = 1.0 / cnt.astype(np.float32)
    return c, g


def _layout(a):
    cols = lambda v: np.asarray(v).reshape(-1, P).T
    tile = lambda w: w.reshape(KT, P, P).transpose(1, 0, 2).reshape(P, KT * P)
    ada = lambda l, t: a["ada_w"][l][:, P * t:P * (t + 1)].T

    def projection(l, i):
        (name, _), c = IN_UNITS[i]
        if name != "rope":
            return tile(a["w_in"][l][:, c:c + P])
        w = np.zeros((D, P), a["w_in"].dtype)
        w[:, NOPE:QD] = a["w_in"][l][:, c:c + ROPE]
        return tile(w)

    def mlp(l, g, j):
        if j < 8:
            return tile(a["mlp_w1"][l][:, D * g + P * j:][:, :P])
        return tile(a["mlp_w2"][l][D * g:D * (g + 1), P * (j - 8):P * (j - 7)])

    units, t0, t1 = [ada(0, t) for t in range(16)], 16, 0
    for l in range(DEPTH):
        for i in range(N_IN):
            units.append(projection(l, i))
            for _ in range(IN_ADA[i] if l == 0 else 0):
                units.append(ada(0, t0))
                t0 += 1
        units += [tile(a["w_out"][l][:, P * m:P * (m + 1)]) for m in range(KT)]
        for g in range(GROUPS):
            for j in range(UPG):
                units.append(mlp(l, g, j))
                for _ in range(ADA_AFTER.get(j, 0) if l == 0 else 0):
                    units.append(ada(1, t1))
                    t1 += 1
    stream = np.stack(units)
    vecs = []
    for l in range(DEPTH):
        for name in ("ada_b", "norm1_g", "norm2_g", "conv_dw", "conv_db", "conv_gn_g", "conv_gn_b", "pool_scale",
                     "rw_mu_prev", "rw_mu_next", "rw_w0", "rw_a0", "rw_kk", "rw_ka", "rw_rk", "rw_lnx_g", "rw_lnx_b",
                     "mla_qn_g", "mla_kvn_g"):
            vecs.append(cols(a[name][l]))
    vecs.append(cols(a["final_g"]))
    vecs = np.concatenate(vecs, 1)
    cond = np.concatenate([a["c"][0], a["c_ctx"]])[None]
    rows = lambda w: w.reshape(-1, P, w.shape[-1]).transpose(1, 0, 2).reshape(P, -1)
    sa, sr = [], []
    for l in range(DEPTH):
        pw = np.zeros((P, 2, P), np.float32)
        for i in range(4):
            o = 64 * (i % 2)
            pw[o:o + 64, i // 2, o:o + 64] = a["pool_w"][l][i]
        sa.append(np.concatenate([rows(a["mla_wuq"][l]), a["mla_wukv"][l], rows(a["conv_pw"][l]), pw.reshape(P, -1)], 1))
        sr.append(np.concatenate([a["rw_w2"][l].reshape(P, GW), a["rw_a2"][l].reshape(P, GW), a["rw_g2"][l]], 1))
    xs = np.concatenate([a["ctx"][0], a["x"][0]], 0).T.reshape(KT, P, TOK).transpose(1, 0, 2)
    c, g = _tables()
    return {"xT": xs, "stream": stream, "vecs": vecs, "cond_in": cond, "consts": c, "big": g, "small_a": np.stack(sa),
            "small_r": np.stack(sr)}


def kernel(**inputs):
    import concourse.bacc as _bacc
    from concourse.bass_utils import run_bass_kernel_spmd as _run

    nc = _bacc.Bacc("TRN2", target_bir_lowering=False, num_devices=1)
    arrays = {k: np.ascontiguousarray(v) for k, v in _layout({k: np.asarray(v) for k, v in inputs.items()}).items()}
    args = {k: nc.dram_tensor(k, v.shape, mybir.dt.from_np(v.dtype), kind="ExternalInput").ap() for k, v in arrays.items()}
    kept = nc.dram_tensor("kept", (P, KT, LAT), F32, kind="Internal").ap()
    kept_rows = nc.dram_tensor("kept_rows", (1, 2 * D), F32, kind="Internal").ap()
    out = nc.dram_tensor("out_t", (P, KT, LAT), F32, kind="ExternalOutput").ap()
    trunk(nc, kept=kept, kept_rows=kept_rows, out=out, **args)
    r = _run(nc, [arrays], core_ids=[0])
    y = r.results[0]["out_t"]
    return y.transpose(2, 1, 0).reshape(1, LAT, D)
```

```python
from contextlib import ExitStack

import numpy as np
import concourse.bass as bass
from concourse import mybir

F32 = mybir.dt.float32
F32R = mybir.dt.float32r
U32 = mybir.dt.uint32
ALU = mybir.AluOpType
ACT = mybir.ActivationFunctionType
AX_X = mybir.AxisListType.X

P = 128
D = 1024
KT = D // P
CTX, LAT = 256, 512
TOK = CTX + LAT
DEPTH = 2
GW = 256
HD = 64
C = 64
NC = TOK // C
CCTX = CTX // C
TAPS = 31
HEADS = 4
NOPE, ROPE = 64, 32
QD = NOPE + ROPE
FF = 4 * D
GROUPS = 4
ADA_AFTER = {1: 2, **{j: 1 for j in range(2, 12)}}
IN_ADA = [3, 3, 3, 3] + [1] * 9 + [2, 2, 1, 1, 2, 3]
UPG = 16
NT_MODS = 48
RAW = 4
SPL = 2
NORM_EPS, GN_EPS, LNX_EPS = 1e-6, 1e-5, 64e-5
C1 = float(-0.5 * np.exp(-0.5))
SCALE = float(QD) ** -0.5
T = TOK * 4

OFF_POOL, OFF_Q, OFF_RW, OFF_KV = 512, 768, 1024, 2176

IN_UNITS = ([(("q", i), OFF_Q + P * i) for i in range(2)] + [(("kv", 0), OFF_KV), (("rope", 0), OFF_KV + P)]
            + [(("z", i), OFF_RW + P * i) for i in (7, 8, 2, 3, 0, 1, 4, 5, 6)]
            + [(("cg", i), GW + P * i) for i in range(2)] + [(("cv", i), P * i) for i in range(2)]
            + [(("pool", i), OFF_POOL + P * i) for i in range(2)])
LAT_ONLY = {"q", "cg", "cv", "pool"}
N_IN = len(IN_UNITS)


def columns(names):
    at, n = {}, 0
    for name, width in names:
        at[name] = n
        n += width
    at["end"] = n
    return at


VEC = [("ada_b", 48), ("n1", 8), ("n2", 8), ("dw", 2 * TAPS), ("db", 2), ("cgg", 2), ("cgb", 2), ("psc", 2),
       ("mup", 9), ("mun", 9), ("w0", 4), ("a0", 4), ("kk", 2), ("ka", 2), ("rk", 2), ("lg", 2), ("lb", 2),
       ("qn", 2), ("kvn", 1)]
VEC_L = columns(VEC)
V_FINAL = DEPTH * VEC_L["end"]
N_VEC = V_FINAL + KT

CST = columns([("ident", P), ("ones", P), ("bones", P), ("lo", 6 * C), ("up", 6 * C), ("tri", 4 * C), ("istack", C),
               ("rot", P)])
BIG = columns([("reset", TOK), ("cos", LAT), ("sin", LAT), ("rcnt", 2 * TOK)])
SW_A = columns([("wuq", 2 * HEADS * QD), ("wukv", 4 * P), ("pw", 2 * GW), ("poolw", 2 * P)])
SW_R = columns([("w2", GW), ("a2", GW), ("g2", GW)])

DER = columns([("A1", 16), ("A2", 16), ("c0", 9), ("hw0", 4), ("ha0", 4), ("nkk", 2), ("s1", 2), ("s2", 2),
               ("hg", 2), ("hb", 2)])


class Steps:

    def __init__(self):
        self.n = 0

    def up(self):
        self.n += 1
        return 1


class Signal:

    def __init__(self, sem, keys):
        self.sem, self.at = sem, {k: n + 1 for n, k in enumerate(keys)}


class Slots:

    def __init__(self, tensor, full, free):
        self.tensor, self.sem_full, self.sem_free, self.n, self.at = tensor, full, free, 0, {}

    def claim(self, key):
        self.at[key] = self.n
        self.n += 1
        return self.slot(key)

    def slot(self, key):
        return self.tensor[:, self.at[key] % 2, :]

    def reused(self, key):
        return self.at[key] >= 2

    def use(self, key):
        return self.at[key] // 2 + 1

    def full(self, key):
        return self.sem_full[self.at[key] % 2]

    def free(self, key):
        return self.sem_free[self.at[key] % 2]


def chunk_order(d):
    if d == 0:
        return list(range(NC))
    return list(range(CCTX - 1, -1, -1)) + list(range(NC - 1, CCTX - 1, -1))


def attention_units(l):
    return [(h, q) for h in range(HEADS) for q in range(0 if l == 0 else 2, TOK // P)]


def front(i):
    steps = [("decay", 0), ("kk", 0)] if i == 0 else []
    steps += [("lora", i)] + [("prep", i, n) for n in range(1, 6)] + [("gram", i, g) for g in range(3)] + [("bkt", i)]
    steps += [("kk", 2)] if i == 1 else []
    steps.append(("t", i, 0))
    for n in range(1, 6):
        steps += [("t", i, n)] + [("x", i, n)] * (n < 5) + [("xt", i, n)]
        steps += [("decay", i + 1)] if n == 2 and i < 3 else []
    return steps


def scan(i):
    return [(s, i, n) for n in range(NC) for s in ("w", "u", "s")]


def rwkv_schedule():
    order = front(0) + [("v", 0)]
    for i in range(4):
        chain, other = scan(i), front(i + 1) if i < 3 else []
        if i == 2:
            for n in range(4):
                other.insert(other.index(("xt", 3, n + 1)) + 1, ("post", 0, n))
        for n, step in enumerate(other):
            order.append(step)
            take = 2 if step[0] in ("bkt", "t") else 1
            order += chain[:take]
            chain = chain[take:]
        order += chain
        if i == 1:
            order.append(("v", 1))
    return order + [("post", 1, n) for n in range(4)]


def bc(ap, shape, axis):
    return ap.unsqueeze(axis).to_broadcast(shape)


def trunk(nc, xT, stream, vecs, cond_in, consts, big, small_a, small_r, kept, kept_rows, out):
    es = ExitStack()
    with es:
        sem = lambda name: es.enter_context(nc.semaphore(name))
        base = (nc.sbuf_base + 31) // 32 * 32

        class Region:

            def __init__(self, offset):
                self.o = offset

            def __call__(self, name, shape, dt=F32):
                size = (int(np.prod(shape[1:])) * 4 + 31) // 32 * 32
                assert self.o + size <= nc.sbuf_usable_end, (name, self.o + size)
                t = nc.alloc_sbuf_tensor_at(name, shape, dt, offset=self.o)
                self.o += size
                return t

        R = Region(base)
        actH, actL, act_at = [], [], []
        for g in range(4):
            act_at.append(R.o)
            actH.append(R(f"act_hi{g}", [P, 2, TOK], F32R))
            actL.append(R(f"act_lo{g}", [P, 2, TOK], F32R))
        raw = R("raw_weights", [P, RAW, KT, P])
        whi = R("weights_hi", [P, SPL, KT, P], F32R)
        wlo = R("weights_lo", [P, SPL, KT, P], F32R)
        cst = R("consts_sb", [P, CST["end"]])
        vec = R("vecs_sb", [P, N_VEC])
        mods = R("mods", [P, DEPTH, NT_MODS, 2])
        der = R("derived", [P, DER["end"]])
        sw_r = R("small_r_sb", [P, SW_R["end"]])
        stat_at = R.o
        stat = R("softmax_stats", [P, 4, HEADS * TOK // P])
        z_at = R.o
        zt = R("z_tiles", [P, 7, TOK])
        zv = R("z_v", [P, 2, TOK + 2 * C])
        free0 = R.o

        x = R("x_tiles", [P, KT, TOK])
        sq = R("squares", [P, 2, TOK])
        sq_sum = R("squares_sum", [P, TOK])
        rinv = R("rinv", [P, TOK])
        tb_at = R.o
        tb = R("normed", [P, 2, TOK])
        hb = R("modulated", [P, 2, TOK])
        hid_lo = R("hidden_lo", [P, 8, TOK], F32R)
        relu = R("relu", [P, 2, TOK])
        hsq = R("hidden_sq", [P, 2, TOK])
        hid_hi = Region(z_at)("hidden_hi", [P, 8, TOK], F32R)
        rows2 = Region(tb_at)("silu_rows2", [P, 2, D])

        R = Region(free0)
        wa = R("work_a", [P, 2, TOK])
        wb = R("work_b", [P, 2, TOK])
        q_sb = R("q_low_rank", [P, 2, TOK])
        ckv = R("kv_low_rank", [P, TOK])
        krope = R("k_rope", [P, TOK])
        ltmp = R("low_rank_tmp", [P, TOK])
        lrin = R("low_rank_rinv", [P, TOK])
        cs = R("cos_sin", [P, 2, LAT])
        sw_a = R("small_a_sb", [P, SW_A["end"]])
        UL = 15 + CTX + 15
        u_sb = R("conv_u", [P, 2, UL + LAT + 15])
        PL = 8 + CTX + 16
        PWID = PL + LAT + 8
        pp = R("pool_p", [P, 2, PWID])
        rows_at = R.o
        u_acc = R("conv_taps", [P, 2, CTX + 15 + LAT])
        ps = R("pool_sums", [P, 2, PWID])
        rcnt = R("pool_rcnt", [P, 2, TOK])
        qT = R("q_t", [P, 2, TOK])
        kT = R("k_t", [P, 2, TOK])
        rtmp = R("rope_tmp", [P, LAT])
        R = Region(rows_at)
        rows = R("silu_rows", [P, 2, D])
        rows_tmp = R("silu_rows_tmp", [P, 2, D])
        R = Region(act_at[1])
        v_tok = R("v_tok", [P, TOK // P, HEADS * HD])
        otok = R("o_tok", [P, TOK // P, HEADS * HD])
        R = Region(act_at[2])
        acc = R("conv_normed", [P, 2, TOK])
        ptmp = R("pool_tmp", [P, PWID])

        R = Region(free0)
        Q = R("rw_q", [P, 2, 4, TOK])
        BKt = R("rw_bk_tok", [P, 2, NC, P])
        XT_at = R.o
        XT = R("rw_xt", [P, 2, NC, C])
        M_at = R.o
        M = R("rw_m", [P, 2, 2, NC, C])
        BK_at = R.o
        BK = R("rw_bk", [P, NC, 2, C])
        UV = R("rw_uv", [P, NC, P])
        SV = R("rw_sv", [P, NC, P])
        b_at = R.o
        X = R("rw_x", [P, NC, C])
        Tc = R("rw_t", [P, NC, C])
        LT = R("rw_lt", [P, NC, C])
        Y = R("rw_y", [P, TOK])
        reset = R("rw_reset", [P, TOK])
        Wc = R("rw_w", [P, 2, C])
        R = Region(stat_at)
        SP = R("rw_s_decayed", [P, C])
        PC = R("rw_p_end", [P, 2, NC])
        R = Region(act_at[1] + T)
        nkk = R("rw_nkk", [P, TOK])
        kds = R("rw_kd_sum", [P, 2, TOK])
        b = Region(b_at)("rw_tmp", [P, 3, TOK])
        fin = Region(BK_at)("rw_tmp_end", [P, 2, TOK])
        wlog = Region(BK_at)("rw_decay_log", [P, 2, TOK])
        b3 = Region(XT_at)("rw_tmp3", [P, 2, TOK])
        b45 = Region(M_at)("rw_tmp45", [P, 2, 2, TOK])

        psA = es.enter_context(nc.psum_tensor("psA", [P, 2, 1024], F32))
        psB = es.enter_context(nc.psum_tensor("psB", [P, 2, 1024], F32))
        A = Slots(psA, [sem("a0_full"), sem("a1_full")], [sem("a0_free"), sem("a1_free")])
        B = Slots(psB, [sem("b0_full"), sem("b1_full")], [sem("b0_free"), sem("b1_free")])

        V = lambda l, name, i=0, n=1: vec[:, l * VEC_L["end"] + VEC_L[name] + i:][:, 0:n]
        DR = lambda name, i=0, n=1: der[:, DER[name] + i:DER[name] + i + n]
        K = lambda name, n, i=0: cst[:, CST[name] + i:CST[name] + i + n]
        ident, ones, bones = K("ident", P), K("ones", P), K("bones", P)
        H = lambda k: actH[k // 2][:, k % 2, :]
        L = lambda k: actL[k // 2][:, k % 2, :]
        f32 = lambda ap: ap.bitcast(F32)
        PSC = 256
        first = lambda l: 0 if l == 0 else CTX
        segs = lambda c0: [(0, CTX, LAT)] + ([(1, 0, CTX)] if c0 == 0 else [])

        units = [("ada", 0)] * 16
        for i in range(N_IN):
            units += [("split", IN_UNITS[i][0])] + [("ada", 0)] * IN_ADA[i]
        units += [("split", "out")] * 8
        mlp0 = {0: len(units)}
        LOOP = {0: 28, 1: 16}
        ada_after = lambda l, j: ADA_AFTER.get(j, 0) if l == 0 else 0
        for g in range(GROUPS):
            for j in range(UPG):
                units += [("split", "mlp")] + [("ada", 1)] * ada_after(0, j)
        units += [("split", u[0]) for u in IN_UNITS] + [("split", "out")] * 8
        mlp0[1] = len(units)
        units += [("split", "mlp")] * (UPG * GROUPS)
        split_no, unit_of_split, n = {}, [], 0
        for i, (kind, _) in enumerate(units):
            if kind == "split":
                split_no[i] = len(unit_of_split)
                unit_of_split.append(i)
        ada_no = {i: k for k, i in enumerate(i for i, u in enumerate(units) if u[0] == "ada")}
        SPL_L = len(unit_of_split) // DEPTH
        S_OUT, S_MLP = N_IN, N_IN + 8
        assert N_IN + 8 + UPG * GROUPS == SPL_L

        c_in = sem("constants_in")
        mix_in = sem("mixing_constants_in")
        rw_in = sem("rwkv_constants_in")
        x_in = sem("x_loaded")
        x_kept = sem("x_kept")
        out_done = sem("out_stored")
        w_in = [sem(f"raw_full{i}") for i in range(RAW)]
        w_hi, w_lo, ada_used = sem("w_hi"), sem("w_lo"), sem("ada_used")
        cond_th, cond_ready = sem("cond_tanh"), sem("cond_ready")
        rows_kept, rows_in = sem("silu_rows_kept"), sem("silu_rows_in")
        vector_step, pool_step = sem("vector_step"), sem("pool_step")
        relu_ready, hid_hi_ready, hid_ready = sem("relu_ready"), sem("hidden_hi_ready"), sem("hidden_ready")

        ls, hs = range(DEPTH), range(HEADS)
        norms = [(l, n) for l in ls for n in (1, 2)] + [(DEPTH, 0)]
        nk = [(n, k) for n in norms for k in range(KT)]
        li2 = [(l, i) for l in ls for i in range(2)]
        sq_ready = Signal(sem("squares_ready"), nk)
        sq_added = Signal(sem("squares_added"), [(n, k) for n in norms for k in range(1, KT)])
        rms = Signal(sem("rms_ready"), norms)
        mod_ready = Signal(sem("modulated"), nk[:-KT])
        act_hi = Signal(sem("act_hi_ready"), nk[:-KT])
        act_lo = Signal(sem("act_lo_ready"), nk[:-KT])
        fin_ready = Signal(sem("final_tile"), [(k,) for k in range(KT)])
        der_ready = Signal(sem("derived_ready"), [(l,) for l in ls])

        lr_sq = Signal(sem("low_rank_squared"), [(l, i) for l in ls for i in range(3)])
        lr_normed = Signal(sem("low_rank_normed"), li2)
        kr_ready = Signal(sem("k_rope_rotated"), [(l,) for l in ls])
        z_order = [u[0][1] for u in IN_UNITS if u[0][0] == "z"]
        z_mixed = Signal(sem("z_mixed"), [(l, i) for l in ls for i in z_order])
        pads = Signal(sem("pads_zeroed"), [(l,) for l in ls])
        lh = [(l, h) for l in ls for h in hs]
        q_rot = Signal(sem("q_rotated"), lh)
        k_full = Signal(sem("k_rope_copied"), lh)
        au = {l: attention_units(l) for l in ls}
        lau = [(l, i) for l in ls for i in range(len(au[l]))]
        rowmax = Signal(sem("row_max"), lau)
        y_hi = Signal(sem("y_hi_ready"), [(l, s, i) for l in ls for s in ("conv", "pool", "att", "rw") for i in range(2)])
        y_lo = Signal(sem("y_lo_ready"), li2)
        conv_sum = Signal(sem("conv_summed"), li2)
        conv_sq = Signal(sem("conv_squared"), li2)
        conv_std = Signal(sem("conv_std"), li2)
        conv_pre = Signal(sem("conv_scaled"), li2)
        conv_th = Signal(sem("conv_tanh"), li2)
        conv_act = Signal(sem("conv_silu"), li2)
        pool_d = Signal(sem("pool_diff"), li2)

        rw_zero = Signal(sem("rw_zeroed"), [(l,) for l in ls])
        l_lora = Signal(sem("decay_input"), [(l,) for l in ls])
        g_th = Signal(sem("gate_tanh"), [(l,) for l in ls])
        kk_sq = Signal(sem("kk_squared"), li2)
        kk_std = Signal(sem("kk_norm"), li2)
        ru = [(l, j, d) for l in ls for j in range(2) for d in range(2)]
        cum = Signal(sem("decay_summed"), ru)
        exps = Signal(sem("decay_exps"), [(u, i) for u in ru for i in range(3)])
        dk = Signal(sem("decay_before"), ru)
        rate_key = Signal(sem("rate_for_key"), ru)
        kd_ready = Signal(sem("kd_ready"), ru)
        pool_k = Signal(sem("k_hat_ready"), ru)
        prep = Signal(sem("chunk_operands"), ru)
        v_tp = Signal(sem("v_chunks"), [(l, j, w) for l in ls for j in range(2) for w in range(2)])
        x_one = Signal(sem("x_first"), ru)
        xt_one = Signal(sem("xt_first"), ru)
        scan_keys = [(u, s_, n) for u in ru for n in range(NC) for s_ in ("w", "u", "s") if s_ != "s" or n < NC - 1]
        scan_full = Signal(sem("scan_product"), scan_keys)
        scan_read = Signal(sem("scan_product_read"), scan_keys)
        y_full = Signal(sem("scan_y_summed"), ru)
        y_read = Signal(sem("scan_y_read"), ru)
        s_zero = Signal(sem("state_zeroed"), ru)
        s_dec = Signal(sem("state_decayed"), [(u, i) for u in ru for i in range(NC - 1)])
        rw_sq = Signal(sem("rw_squared"), li2)
        rw_std = Signal(sem("rw_std"), li2)
        bon = Signal(sem("bonus_product"), li2)

        block = es.enter_context(nc.Block())
        conv_step = lambda l, i: i - (len(au[l]) - 8)
        next_norm = {0: (1, 1), 1: (DEPTH, 0)}
        RW = rwkv_schedule()
        scan_w, scan_u, scan_s = psB[:, 1, 0:C], psB[:, 1, 512:512 + C], psB[:, 1, C:2 * C]
        HALF = ((slice(0, 64), 0), (slice(64, P), 1))
        rp = slice(NOPE, QD)
        ZI = {0: 0, 1: 1, 2: 2, 3: 3, 6: 4, 7: 5, 8: 6}
        z_of = lambda i: zv[:, i - 4, C:C + TOK] if i in (4, 5) else zt[:, ZI[i], :]
        chunks = lambda ap: ap.rearrange("p (c t) -> p c t", t=C)

        @block.tensor
        def _(pe):
            def span(dst, lhsT, rhs, start, stop, c0=0, part=slice(0, P)):
                if c0 == 0:
                    pe.matmul(dst[part, PSC:PSC + CTX], lhsT, rhs[:, 0:CTX], start=start, stop=stop)
                return pe.matmul(dst[part, PSC + CTX:], lhsT, rhs[:, CTX:TOK], start=start, stop=stop)

            def unit_products(dst, w, hi, lo, c0, each):
                for k in range(KT):
                    if each:
                        each(k)
                    span(dst, whi[:, w, k, :], lo(k), k == 0, False, c0)
                    span(dst, whi[:, w, k, :], hi(k), False, False, c0)
                    m = span(dst, wlo[:, w, k, :], hi(k), False, k == KT - 1, c0)
                return m

            def linear(n, key, c0, hi=H, lo=L, plus=0, slots=0, each=None):
                dst = A.claim(key)
                if A.reused(key):
                    pe.wait_ge(A.free(key), A.use(key) - 1 + slots)
                pe.wait_ge(w_lo, n + 1 + plus)
                unit_products(dst, n % SPL, hi, lo, c0, each).then_inc(A.full(key), 1)

            def small(pool, key, c0, pairs, part=slice(0, P)):
                dst = pool.claim(key)
                if pool.reused(key):
                    pe.wait_ge(pool.free(key), pool.use(key) - 1)
                for i, (lhsT, rhs) in enumerate(pairs):
                    m = span(dst, lhsT, rhs, i == 0, i == len(pairs) - 1, c0, part)
                m.then_inc(pool.full(key), 1)

            def norm_sum(key, c0):
                pe.wait_ge(sq_added.sem, sq_added.at[key, KT - 1])
                small(B, ("norm", key), c0, [(ones, sq_sum[:, :])])

            pe.wait_ge(c_in, 16 * 3)
            nsplit = 0
            for l in ls:
                c0 = first(l)
                if l == 0:
                    norm_sum((0, 1), 0)
                for i, (name, _) in enumerate(IN_UNITS):
                    normed = lambda k: pe.wait_ge(act_lo.sem, act_lo.at[(l, 1), k])
                    linear(nsplit, (l,) + name, c0 if name[0] in LAT_ONLY else 0, each=None if i else normed)
                    nsplit += 1
                    if i == 5:
                        pe.wait_ge(lr_sq.sem, lr_sq.at[l, 1])
                        small(A, (l, "qstat"), c0, [(ones, ltmp[:, :]), (ones, lrin[:, :])])
                    elif i == 7:
                        pe.wait_ge(lr_sq.sem, lr_sq.at[l, 2])
                        small(A, (l, "kvstat"), 0, [(ones, kT[:, 0, :])])

                if l == 0:
                    pe.wait_ge(ada_used, NT_MODS)
                pe.wait_ge(mix_in, 48 * (l + 1))
                pe.wait_ge(A.free((l, "rope", 0)), A.use((l, "rope", 0)))

                def rotate(key, src):
                    dst = B.claim(key)
                    if B.reused(key):
                        pe.wait_ge(B.free(key), B.use(key) - 1)
                    pe.matmul(dst[rp, PSC + CTX:], K("rot", ROPE)[rp, :], src[rp, CTX:], start=True,
                                       stop=True).then_inc(B.full(key), 1)

                rotate((l, "krot"), krope[:, :])
                pe.wait_ge(lr_normed.sem, lr_normed.at[l, 1])
                for w, blocks in enumerate(((0, 1, 2, 3), (4, 5))):
                    dst = A.claim((l, "v", w))
                    if A.reused((l, "v", w)):
                        pe.wait_ge(A.free((l, "v", w)), A.use((l, "v", w)) - 1)
                    vw = sw_a[:, SW_A["wukv"]:][:, 0:4 * P].rearrange("p (h n) -> p h n", h=HEADS)[:, :, NOPE:]
                    for b_ in blocks:
                        m = pe.matmul(dst[:, GW * (b_ % 4):GW * (b_ % 4 + 1)], ckv[:, P * b_:P * (b_ + 1)], vw,
                                      start=True, stop=True)
                    m.then_inc(A.full((l, "v", w)), 1)

                def head_operands(h):
                    wq = lambda k: sw_a[:, SW_A["wuq"] + k * HEADS * QD + h * QD:][:, 0:QD]
                    wk = sw_a[:, SW_A["wukv"] + h * P:][:, 0:NOPE]
                    small(A, (l, "qh", h), c0, [(wq(k), q_sb[:, k, :]) for k in range(2)], slice(0, QD))
                    small(A, (l, "kh", h), 0, [(wk, ckv[:, :])], slice(0, NOPE))
                    pe.wait_ge(A.free((l, "qh", h)), A.use((l, "qh", h)))
                    rotate((l, "qrot", h), qT[:, h % 2, :])

                def scores(i):
                    h, q = au[l][i]
                    dst = A.claim((l, "s", i))
                    if A.reused((l, "s", i)):
                        pe.wait_ge(A.free((l, "s", i)), A.use((l, "s", i)) - 1)
                    if i == 0 or au[l][i - 1][0] != h:
                        pe.wait_ge(q_rot.sem, q_rot.at[l, h])
                        pe.wait_ge(A.free((l, "kh", h)), A.use((l, "kh", h)))
                        pe.wait_ge(k_full.sem, k_full.at[l, h])
                    m = pe.matmul(dst[:, PSC:PSC + CTX], qT[0:QD, h % 2, P * q:P * (q + 1)], kT[0:QD, h % 2, 0:CTX],
                                  start=True, stop=True)
                    if q >= CTX // P:
                        m = pe.matmul(dst[:, PSC + CTX:], qT[0:QD, h % 2, P * q:P * (q + 1)], kT[0:QD, h % 2, CTX:],
                                      start=True, stop=True)
                    m.then_inc(A.full((l, "s", i)), 1)

                blocks_of = lambda q: (CTX if q < CTX // P else TOK) // P

                def turn(i):
                    dst = B.claim((l, "pt", i))
                    if B.reused((l, "pt", i)):
                        pe.wait_ge(B.free((l, "pt", i)), B.use((l, "pt", i)) - 1)
                    pe.wait_ge(A.free((l, "s", i)), A.use((l, "s", i)))
                    for b_ in range(blocks_of(au[l][i][1])):
                        m = pe.transpose(dst[:, PSC + P * b_:PSC + P * (b_ + 1)], wa[:, i % 2, P * b_:P * (b_ + 1)], ident)
                    m.then_inc(B.full((l, "pt", i)), 1)

                def mix_values(i):
                    h, q = au[l][i]
                    nb = blocks_of(q)
                    dst = B.claim((l, "o", i))
                    if B.reused((l, "o", i)):
                        pe.wait_ge(B.free((l, "o", i)), B.use((l, "o", i)) - 1)
                    if i == 0:
                        pe.wait_ge(A.free((l, "v", 0)), A.use((l, "v", 0)))
                        pe.wait_ge(A.free((l, "v", 1)), A.use((l, "v", 1)))
                    pe.wait_ge(B.free((l, "pt", i)), B.use((l, "pt", i)))
                    for b_ in range(nb):
                        m = pe.matmul(dst[:, 0:HD], wb[:, i % 2, P * b_:P * (b_ + 1)], v_tok[:, b_, HD * h:HD * (h + 1)],
                                      start=b_ == 0, stop=b_ == nb - 1)
                    m.then_inc(B.full((l, "o", i)), 1)

                def conv(step):
                    if step == 1:
                        for i in range(2):
                            pe.wait_ge(conv_sum.sem, conv_sum.at[l, i])
                            small(B, (l, "cmean", i), c0, [(bones, acc[:, i, :])])
                    elif step == 3:
                        for i in range(2):
                            pe.wait_ge(conv_sq.sem, conv_sq.at[l, i])
                            small(B, (l, "cvar", i), c0, [(bones, u_sb[:, i, 0:TOK])])
                    elif step == 5:
                        pe.wait_ge(conv_act.sem, conv_act.at[l, 1])
                        for i in range(2):
                            small(A, (l, "convp", i), c0,
                                  [(sw_a[:, SW_A["pw"] + k * GW + i * P:][:, 0:P], acc[:, k, :]) for k in range(2)])
                    elif step == 6:
                        for i in range(2):
                            pe.wait_ge(pool_d.sem, pool_d.at[l, i])
                            small(A, (l, "poolp", i), c0, [(sw_a[:, SW_A["poolw"] + i * P:][:, 0:P], rcnt[:, i, :])])

                head_operands(0)
                for i in range(len(au[l])):
                    h = au[l][i][0]
                    if (i == 0 or au[l][i - 1][0] != h) and h + 1 < HEADS:
                        head_operands(h + 1)
                    scores(i)
                    if i:
                        turn(i - 1)
                    if i > 1:
                        mix_values(i - 2)
                    conv(conv_step(l, i))
                turn(len(au[l]) - 1)
                mix_values(len(au[l]) - 2)
                mix_values(len(au[l]) - 1)
                for i in range(2):
                    dst = A.claim((l, "att", i))
                    if A.reused((l, "att", i)):
                        pe.wait_ge(A.free((l, "att", i)), A.use((l, "att", i)) - 1)
                    if i == 0:
                        pe.wait_ge(B.free((l, "o", len(au[l]) - 1)), B.use((l, "o", len(au[l]) - 1)))
                        pe.wait_ge(B.free((l, "o", len(au[l]) - 2)), B.use((l, "o", len(au[l]) - 2)))
                    for q in range(c0 // P, TOK // P):
                        m = pe.transpose(dst[:, PSC + P * q:PSC + P * (q + 1)], otok[:, q, P * i:P * (i + 1)], ident)
                    m.then_inc(A.full((l, "att", i)), 1)

                pe.wait_ge(rw_in, 32 * (l + 1))
                pe.wait_ge(l_lora.sem, l_lora.at[(l,)])
                pe.wait_ge(rw_zero.sem, rw_zero.at[(l,)])
                def by_chunk(key, lhsT, rhs):
                    dst = A.claim(key)
                    if A.reused(key):
                        pe.wait_ge(A.free(key), A.use(key) - 1)
                    for c in range(NC):
                        for part, _ in HALF:
                            m = pe.matmul(dst[part, PSC + C * c:][:, 0:C], lhsT[part, c, :], rhs(c)[part], start=True,
                                          stop=True)
                    m.then_inc(A.full(key), 1)

                for what, i, *rest in RW:
                    j, d, p = i // 2, i % 2, i % 2
                    un, n_ = (l, j, d), rest[0] if rest else 0
                    if what == "kk":
                        pe.wait_ge(kk_sq.sem, kk_sq.at[l, j])
                        small(A, (l, "kk", j), 0, [(bones, nkk[:, :])])
                    elif what == "decay":
                        dp = slice(64 * d, 64 * d + 64)
                        small(A, (un, "w2"), 0, [(sw_r[dp, SW_R["w2"] + P * j:][:, 0:P], zt[dp, 5, :])])
                    elif what == "lora":
                        dp = slice(64 * d, 64 * d + 64)
                        small(A, (un, "a2"), 0, [(sw_r[dp, SW_R["a2"] + P * j:][:, 0:P], zt[dp, 6, :])])
                    elif what == "v":
                        for w, ms in enumerate((range(0, 7), range(7, 13))):
                            key = (l, i, "v", w)
                            dst = A.claim(key)
                            if A.reused(key):
                                pe.wait_ge(A.free(key), A.use(key) - 1)
                            for m_ in ms:
                                o = m_ - ms[0]
                                m = pe.transpose(dst[:, P * o:P * (o + 1)], zv[:, i, C * m_:C * m_ + P], ident)
                            m.then_inc(A.full(key), 1)
                    elif what == "gram":
                        if n_ == 0:
                            pe.wait_ge(prep.sem, prep.at[un])
                            pe.wait_ge(pool_k.sem, pool_k.at[un])
                        key = (un, "gram", n_)
                        dst = A.claim(key)
                        if A.reused(key):
                            pe.wait_ge(A.free(key), A.use(key) - 1)
                        for c in range(4 * n_, 4 * n_ + 4):
                            for part, s_ in HALF:
                                m = pe.matmul(dst[:, 512 * s_ + P * (c % 4):][:, 0:P], BK[part, c, :, :],
                                              Q[part, p, 2 * s_:2 * s_ + 2, C * c:C * (c + 1)], start=True, stop=True)
                        m.then_inc(A.full(key), 1)
                    elif what == "bkt":
                        for w in range(2):
                            key = (un, "bkt", w)
                            dst = A.claim(key)
                            if A.reused(key):
                                pe.wait_ge(A.free(key), A.use(key) - 1)
                            for c in range(8 * w, min(8 * w + 8, NC)):
                                m = pe.transpose(dst[:, P * (c % 8):][:, 0:P], BK[:, c, :, :], ident)
                            m.then_inc(A.full(key), 1)
                    elif what == "t":
                        if n_ == 0:
                            pe.wait_ge(A.free((un, "gram", 2)), A.use((un, "gram", 2)))
                            by_chunk((un, "t", 0), LT, lambda c: K("istack", C))
                        else:
                            if n_ == 1:
                                pe.wait_ge(x_one.sem, x_one.at[un])
                            else:
                                pe.wait_ge(A.free((un, "x", n_ - 1)), A.use((un, "x", n_ - 1)))
                            by_chunk((un, "t", n_), LT, lambda c: X[:, c, :])
                    elif what == "x":
                        if n_ == 1:
                            pe.wait_ge(xt_one.sem, xt_one.at[un])
                        else:
                            pe.wait_ge(A.free((un, "xt", n_ - 1)), A.use((un, "xt", n_ - 1)))
                        pe.wait_ge(A.free((un, "t", n_)), A.use((un, "t", n_)))
                        by_chunk((un, "x", n_), XT[:, p], lambda c: Tc[:, c, :])
                    elif what == "xt":
                        if n_ == 5:
                            pe.wait_ge(A.free((un, "xt", 4)), A.use((un, "xt", 4)))
                            pe.wait_ge(A.free((un, "t", 5)), A.use((un, "t", 5)))
                        by_chunk((un, "xt", n_), Tc, lambda c: XT[:, p, c, :])
                    elif what == "w":
                        c = chunk_order(d)[n_]
                        if n_ == 0:
                            pe.wait_ge(A.free((un, "xt", 5)), A.use((un, "xt", 5)))
                            pe.wait_ge(A.free((un, "bkt", 1)), A.use((un, "bkt", 1)))
                            pe.wait_ge(A.free((l, j, "v", 1)), A.use((l, j, "v", 1)))
                            pe.wait_ge(s_zero.sem, s_zero.at[un])
                            if i:
                                pe.wait_ge(y_read.sem, y_read.at[un] - 1)
                            else:
                                pe.wait_ge(B.free((l, "cvar", 0)), B.use((l, "cvar", 0)))
                                pe.wait_ge(B.free((l, "cvar", 1)), B.use((l, "cvar", 1)))
                        else:
                            pe.wait_ge(scan_read.sem, scan_read.at[un, "s", n_ - 1])
                        for part, s_ in HALF:
                            m = pe.matmul(scan_w[part], Q[:, p, 2 * s_, C * c:C * (c + 1)],
                                          SV[:, c, HD * s_:HD * (s_ + 1)], start=True, stop=True)
                        m.then_inc(scan_full.sem, 1)
                    elif what == "u":
                        c = chunk_order(d)[n_]
                        pe.wait_ge(scan_read.sem, scan_read.at[un, "w", n_])
                        for part, _ in HALF:
                            m = pe.matmul(scan_u[part], XT[part, p, c, :], Wc[part, n_ % 2, :], start=True, stop=True)
                        m.then_inc(scan_full.sem, 1)
                    elif what == "s":
                        c = chunk_order(d)[n_]
                        pe.wait_ge(scan_read.sem, scan_read.at[un, "u", n_])
                        if n_ < NC - 1:
                            for part, s_ in HALF:
                                m = pe.matmul(scan_s[part], BKt[:, p, c, HD * s_:HD * (s_ + 1)],
                                              UV[:, c, HD * s_:HD * (s_ + 1)], start=True, stop=True)
                            m.then_inc(scan_full.sem, 1)
                        if c * C >= c0:
                            o = PSC + C * c
                            for part, s_ in HALF:
                                hv = slice(HD * s_, HD * (s_ + 1))
                                pe.matmul(psB[part, 0, o:o + C], SV[:, c, hv], Q[:, p, 2 * s_ + 1, C * c:C * (c + 1)],
                                          start=True, stop=False)
                                m = pe.matmul(psB[part, 0, o:o + C], UV[:, c, hv], M[:, p, s_, c, :], start=False,
                                              stop=True)
                        if n_ == NC - 1:
                            m.then_inc(y_full.sem, 1)
                    elif what == "post" and n_ == 0:
                        pe.wait_ge(y_read.sem, y_read.at[l, i, 1])
                        small(A, (l, i, "mean"), c0, [(bones, Y[:, :])])
                    elif what == "post" and n_ == 1:
                        pe.wait_ge(bon.sem, bon.at[l, i])
                        small(A, (l, i, "bonus"), c0, [(bones, fin[:, 0, :])])
                    elif what == "post" and n_ == 2:
                        pe.wait_ge(rw_sq.sem, rw_sq.at[l, i])
                        small(A, (l, i, "var"), c0, [(bones, fin[:, 1, :])])
                    elif what == "post":
                        small(A, (l, i, "gate"), c0, [(sw_r[:, SW_R["g2"] + P * i:][:, 0:P], zt[:, 4, :])])

                for key in ("att", "convp", "poolp"):
                    for i in range(2):
                        pe.wait_ge(A.free((l, key, i)), A.use((l, key, i)))
                pe.wait_ge(y_lo.sem, y_lo.at[l, 1])
                for m_ in range(KT):
                    linear(nsplit, (l, "out", m_), c0)
                    nsplit += 1
                norm_sum((l, 2), c0)

                hh, hl = (lambda k: hid_hi[:, k, :]), (lambda k: hid_lo[:, k, :])

                def group(g0, g):
                    normed = lambda k: pe.wait_ge(act_lo.sem, act_lo.at[(l, 2), k])
                    hidden = lambda k: pe.wait_ge(hid_ready, 8 * (l * GROUPS + g0) + k + 1 + 8 * g)
                    n = nsplit + UPG * g0
                    for j in range(UPG):
                        linear(n + j, (l, "mlp", g0, j), c0, *((H, L) if j < 8 else (hh, hl)), UPG * g, 8 * g,
                               {0: normed, 8: hidden}.get(j))

                with pe.Fori(0, GROUPS - 1) as g:
                    group(0, g)
                A.n += UPG * (GROUPS - 2)
                group(GROUPS - 1, 0)
                nsplit += UPG * GROUPS
                if l == 0:
                    pe.wait_ge(ada_used, 2 * NT_MODS)
                norm_sum(next_norm[l], 0 if l == 0 else CTX)

        @block.scalar
        def _(act):
            cp = lambda o, i, **k: act.activation(o, i, ACT.Copy, **k)

            def split_hi(n, i_plus=0):
                i = unit_of_split[n]
                act.wait_ge(w_in[i % RAW], 16 * (i // RAW + 1) + i_plus)
                act.activation(whi[:, n % SPL], raw[:, i % RAW], ACT.Copy).then_inc(w_hi, 1)

            def ahead(n, key):
                act.wait_ge(A.full(key), A.use(key))
                split_hi(n + SPL)
                return A.slot(key)

            def square(key, k, c0):
                if k >= 3:
                    act.wait_ge(sq_added.sem, sq_added.at[key, k - 2])
                act.activation(sq[:, k % 2, c0:] if k else sq_sum[:, c0:], x[:, k, c0:], ACT.Square)\
                    .then_inc(sq_ready.sem, 1)

            def norm_root(key, c0):
                act.wait_ge(B.full(("norm", key)), B.use(("norm", key)))
                src = B.slot(("norm", key))
                act.activation(rinv[:, c0:], src[:, PSC + c0:], ACT.Sqrt, scale=1.0 / D, bias=NORM_EPS)\
                    .then_inc(rms.sem, 1)

            def operand_hi(key, c0):
                for k in range(KT):
                    act.wait_ge(mod_ready.sem, mod_ready.at[key, k])
                    cp(H(k)[:, c0:], hb[:, k % 2, c0:]).then_inc(act_hi.sem, 1)

            act.wait_ge(c_in, 48)
            act.activation(rows_tmp[:, :, :], rows[:, :, :], ACT.Tanh, scale=0.5).then_inc(cond_th, 1)
            n = 0
            for l in ls:
                c0 = first(l)
                if l == 0:
                    act.wait_ge(x_in, 16)
                    for k in range(KT):
                        square((0, 1), k, 0)
                    norm_root((0, 1), 0)
                    split_hi(0)
                    split_hi(1)
                operand_hi((l, 1), 0)
                act.wait_ge(der_ready.sem, der_ready.at[(l,)])
                if l == 1:
                    act.wait_ge(x_kept, 16)
                nz = 0
                for name, i in (u[0] for u in IN_UNITS):
                    key = (l, name, i)
                    src = ahead(n, key)
                    n += 1
                    if name == "q":
                        cp(q_sb[:, i, c0:], src[:, PSC + c0:]).then_inc(A.free(key), 1)
                        act.wait_ge(A.free(key), A.use(key))
                        act.activation((ltmp, lrin)[i][:, c0:], q_sb[:, i, c0:], ACT.Square).then_inc(lr_sq.sem, 1)
                    elif name == "kv":
                        cp(ckv[:, :], src[:, PSC:]).then_inc(A.free(key), 1)
                        act.wait_ge(A.free(key), A.use(key))
                        act.activation(kT[:, 0, :], ckv[:, :], ACT.Square).then_inc(lr_sq.sem, 1)
                    elif name == "rope":
                        cp(krope[rp, :], src[rp, PSC:]).then_inc(A.free(key), 1)
                    elif name == "z":
                        if nz >= 2:
                            act.wait_ge(z_mixed.sem, z_mixed.at[l, z_order[nz - 2]])
                        cp(wa[:, nz % 2, :], src[:, PSC:])
                        act.activation(z_of(i), src[:, PSC:], ACT.Identity, scale=DR("c0", i)).then_inc(A.free(key), 1)
                        nz += 1
                    elif name == "cg":
                        act.activation(wb[:, i, c0:], src[:, PSC + c0:], ACT.Tanh, scale=0.5).then_inc(A.free(key), 1)
                    elif name == "pool":
                        if i == 0:
                            act.wait_ge(pads.sem, pads.at[(l,)])
                        if l == 0:
                            cp(pp[:, i, 8:8 + CTX], src[:, PSC:PSC + CTX])
                        cp(pp[:, i, PL:PL + LAT], src[:, PSC + CTX:]).then_inc(A.free(key), 1)
                    if (name, i) == IN_UNITS[5][0]:
                        key = (l, "qstat")
                        act.wait_ge(A.full(key), A.use(key))
                        act.activation(lrin[:, c0:], A.slot(key)[:, PSC + c0:], ACT.Sqrt, scale=1.0 / GW, bias=NORM_EPS)\
                            .then_inc(A.free(key), 1)
                    elif (name, i) == IN_UNITS[7][0]:
                        key = (l, "kvstat")
                        act.wait_ge(A.full(key), A.use(key))
                        act.activation(ltmp[:, :], A.slot(key)[:, PSC:], ACT.Sqrt, scale=1.0 / P, bias=NORM_EPS)\
                            .then_inc(A.free(key), 1)
                for w, nb in enumerate((4, 2)):
                    act.wait_ge(A.full((l, "v", w)), A.use((l, "v", w)))
                    src = A.slot((l, "v", w))
                    cp(v_tok[:, 4 * w:4 * w + nb, :], src[:, 0:GW * nb]).then_inc(A.free((l, "v", w)), 1)

                def head_operands(h):
                    act.wait_ge(A.full((l, "qh", h)), A.use((l, "qh", h)))
                    src = A.slot((l, "qh", h))
                    cp(qT[0:QD, h % 2, c0:], src[0:QD, PSC + c0:]).then_inc(A.free((l, "qh", h)), 1)
                    act.wait_ge(A.full((l, "kh", h)), A.use((l, "kh", h)))
                    src = A.slot((l, "kh", h))
                    cp(kT[0:NOPE, h % 2, :], src[0:NOPE, PSC:]).then_inc(A.free((l, "kh", h)), 1)

                def softmax(i):
                    e = PSC + (CTX if au[l][i][1] < CTX // P else TOK)
                    act.wait_ge(rowmax.sem, rowmax.at[l, i])
                    act.activation(wa[:, i % 2, 0:e - PSC], psA[:, A.at[(l, "s", i)] % 2, PSC:e], ACT.Exp,
                                           scale=SCALE, bias=stat[:, 1, i:i + 1], accum_out=stat[:, 2, i:i + 1])\
                                               .then_inc(A.free((l, "s", i)), 1)

                def turned(i):
                    e = PSC + (CTX if au[l][i][1] < CTX // P else TOK)
                    if i >= 2:
                        act.wait_ge(B.full((l, "o", i - 2)), B.use((l, "o", i - 2)))
                    act.wait_ge(B.full((l, "pt", i)), B.use((l, "pt", i)))
                    src = B.slot((l, "pt", i))
                    cp(wb[:, i % 2, 0:e - PSC], src[:, PSC:e]).then_inc(B.free((l, "pt", i)), 1)

                def conv(step):
                    for i in range(2):
                        if step == 2:
                            act.wait_ge(B.free((l, "cmean", i)), B.use((l, "cmean", i)))
                            act.activation(u_sb[:, i, c0:TOK], acc[:, i, c0:], ACT.Square).then_inc(conv_sq.sem, 1)
                        elif step == 3:
                            act.wait_ge(B.full((l, "cvar", i)), B.use((l, "cvar", i)))
                            src = B.slot((l, "cvar", i))
                            act.activation(q_sb[:, i, c0:], src[:, PSC + c0:], ACT.Sqrt, scale=1.0 / 64, bias=GN_EPS)\
                                .then_inc(conv_std.sem, 1)
                        elif step == 4:
                            act.wait_ge(conv_pre.sem, conv_pre.at[l, i])
                            act.activation(q_sb[:, i, c0:], acc[:, i, c0:], ACT.Tanh).then_inc(conv_th.sem, 1)
                        elif step == 5:
                            act.wait_ge(A.full((l, "convp", i)), A.use((l, "convp", i)))
                            src = A.slot((l, "convp", i))
                            cp(H(i)[:, c0:], src[:, PSC + c0:]).then_inc(y_hi.sem, 1)
                        elif step == 6:
                            act.wait_ge(A.full((l, "poolp", i)), A.use((l, "poolp", i)))
                            src = A.slot((l, "poolp", i))
                            act.activation(H(4 + i)[:, c0:], src[:, PSC + c0:], ACT.Identity, scale=V(l, "psc", i))\
                                .then_inc(y_hi.sem, 1)

                head_operands(0)
                for i in range(len(au[l])):
                    h = au[l][i][0]
                    if (i == 0 or au[l][i - 1][0] != h) and h + 1 < HEADS:
                        head_operands(h + 1)
                    softmax(i)
                    if i:
                        turned(i - 1)
                    conv(conv_step(l, i))
                turned(len(au[l]) - 1)
                for i in range(2):
                    act.wait_ge(A.full((l, "att", i)), A.use((l, "att", i)))
                    src = A.slot((l, "att", i))
                    cp(H(6 + i)[:, c0:], src[:, PSC + c0:]).then_inc(y_hi.sem, 1)
                act.wait_ge(A.free((l, "att", 1)), A.use((l, "att", 1)))
                act.wait_ge(z_mixed.sem, z_mixed.at[l, z_order[-1]])
                act.activation(zt[:, 5, :], zt[:, 5, :], ACT.Tanh).then_inc(l_lora.sem, 1)
                act.activation(zt[:, 4, c0:], zt[:, 4, c0:], ACT.Tanh, scale=0.5).then_inc(g_th.sem, 1)
                for what, i, *rest in RW:
                    j, d, p = i // 2, i % 2, i % 2
                    un, n_ = (l, j, d), rest[0] if rest else 0
                    if what == "kk":
                        if j:
                            act.wait_ge(prep.sem, prep.at[l, 0, 1])
                        act.activation(nkk[:, :], zt[:, 2 + j, :], ACT.Square, scale=V(l, "kk", j))\
                            .then_inc(kk_sq.sem, 1)
                        act.wait_ge(A.full((l, "kk", j)), A.use((l, "kk", j)))
                        src = A.slot((l, "kk", j))
                        act.activation(nkk[:, :], src[:, PSC:], ACT.Sqrt).then_inc(kk_std.sem, 1)
                    elif what == "decay":
                        act.wait_ge(A.full((un, "w2")), A.use((un, "w2")))
                        act.activation(wlog[:, 0, :], A.slot((un, "w2"))[:, PSC:], ACT.Tanh, scale=0.5,
                                       bias=DR("hw0", 2 * d + j)).then_inc(A.free((un, "w2")), 1)
                    elif what == "lora":
                        act.wait_ge(A.full((un, "a2")), A.use((un, "a2")))
                        act.activation(b45[:, p, 0, :], A.slot((un, "a2"))[:, PSC:], ACT.Tanh, scale=0.5,
                                       bias=DR("ha0", 2 * d + j)).then_inc(A.free((un, "a2")), 1)
                        act.wait_ge(A.free((un, "a2")), A.use((un, "a2")))
                        act.activation(b45[:, p, 1, :], b45[:, p, 0, :], ACT.Identity, scale=DR("s1", j),
                                       bias=DR("s2", j)).then_inc(rate_key.sem, 1)
                    elif what == "v":
                        for w, (m0, m1) in enumerate(((0, 7), (7, 13))):
                            act.wait_ge(A.full((l, i, "v", w)), A.use((l, i, "v", w)))
                            src = A.slot((l, i, "v", w)).rearrange("p (m n) -> p m n", n=P)
                            e = min(m1, NC)
                            cp(UV[64:, m0:e, 0:HD], src[64:, 0:e - m0, 0:HD])
                            s_ = max(m0, 1)
                            cp(UV[0:64, s_ - 1:m1 - 1, HD:], src[0:64, s_ - m0:m1 - m0, HD:]).then_inc(v_tp.sem, 1)
                    elif what == "prep" and n_ == 1:
                        act.wait_ge(cum.sem, cum.at[un])
                        act.activation(b3[:, p, :], wlog[:, 1, :], ACT.Exp, scale=-C1).then_inc(exps.sem, 1)
                        act.activation(b[:, 1, :], wlog[:, 1, :], ACT.Exp, scale=C1).then_inc(exps.sem, 1)
                        act.wait_ge(dk.sem, dk.at[un])
                        act.activation(b[:, 0, :], b[:, 0, :], ACT.Exp, scale=C1).then_inc(exps.sem, 1)
                    elif what == "bkt":
                        for w in range(2):
                            act.wait_ge(A.full((un, "bkt", w)), A.use((un, "bkt", w)))
                            k = min(8, NC - 8 * w)
                            cp(BKt[:, p, 8 * w:8 * w + k, :], A.slot((un, "bkt", w))[:, 0:P * k])\
                                .then_inc(A.free((un, "bkt", w)), 1)
                    elif what == "t" and n_:
                        act.wait_ge(A.full((un, "t", n_)), A.use((un, "t", n_)))
                        cp(Tc[:, :, :], chunks(A.slot((un, "t", n_))[:, PSC:])).then_inc(A.free((un, "t", n_)), 1)
                    elif what == "post" and n_ == 1:
                        act.wait_ge(A.free((l, i, "mean")), A.use((l, i, "mean")))
                        act.activation(fin[:, 1, c0:], Y[:, c0:], ACT.Square).then_inc(rw_sq.sem, 1)
                    elif what == "post" and n_ == 2:
                        act.wait_ge(A.full((l, i, "var")), A.use((l, i, "var")))
                        act.activation(fin[:, 1, c0:], A.slot((l, i, "var"))[:, PSC + c0:], ACT.Sqrt, scale=1.0 / 64,
                                       bias=LNX_EPS).then_inc(rw_std.sem, 1)
                    elif what == "post" and n_ == 3:
                        act.wait_ge(A.free((l, i, "gate")), A.use((l, i, "gate")))
                        cp(H(2 + i)[:, c0:], Y[:, c0:]).then_inc(y_hi.sem, 1)
                for m in range(KT):
                    ahead(n, (l, "out", m))
                    n += 1
                    if m:
                        act.wait_ge(A.free((l, "out", m - 1)), A.use((l, "out", m - 1)))
                        square((l, 2), m - 1, c0)
                act.wait_ge(A.free((l, "out", KT - 1)), A.use((l, "out", KT - 1)))
                square((l, 2), KT - 1, c0)
                norm_root((l, 2), c0)
                operand_hi((l, 2), c0)
                if l == 0:
                    act.wait_ge(act_lo.sem, act_lo.at[(0, 2), KT - 1])
                    act.wait_ge(rows_kept, 16)
                    act.dma_start(rows2[:, :, :].rearrange("p s n -> p (s n)"), kept_rows.to_broadcast([P, 2 * D]))\
                        .then_inc(rows_in, 16)

                def group(g0, g, end):
                    for j in range(UPG):
                        key, nj = (l, "mlp", g0, j), n + UPG * g0 + j
                        done = 8 * (l * GROUPS + g0) + j + 1
                        act.wait_ge(A.full(key), A.use(key) + 8 * g)
                        src = A.slot(key)
                        if j < 8:
                            if j >= 2:
                                act.wait_ge(A.free((l, "mlp", g0, j - 2)), A.use((l, "mlp", g0, j - 2)) + 8 * g)
                            act.activation(relu[:, j % 2, c0:], src[:, PSC + c0:], ACT.Relu).then_inc(relu_ready, 1)
                        if not (end and l and j >= UPG - SPL):
                            split_hi(nj + SPL, i_plus=16 * (LOOP[l] // RAW) * g)
                        if j < 8:
                            act.wait_ge(A.free(key), A.use(key) + 8 * g)
                            cp(hid_hi[:, j, c0:], hsq[:, j % 2, c0:]).then_inc(hid_hi_ready, 1)
                        if end and j > 8:
                            before = (l, "mlp", g0, j - 1)
                            act.wait_ge(A.free(before), A.use(before))
                            square(next_norm[l], j - 9, 0 if l == 0 else CTX)

                with act.Fori(0, GROUPS - 1) as g:
                    group(0, g, False)
                group(GROUPS - 1, 0, True)
                n += UPG * GROUPS
                last = (l, "mlp", GROUPS - 1, UPG - 1)
                act.wait_ge(A.free(last), A.use(last))
                square(next_norm[l], KT - 1, 0 if l == 0 else CTX)
                norm_root(next_norm[l], 0 if l == 0 else CTX)

        @block.vector
        def _(dve):
            step = Steps()
            tt, ts, stt = dve.tensor_tensor, dve.tensor_scalar, dve.scalar_tensor_tensor

            def derive(l):
                stt(DR("c0", 0, 9), V(l, "mup", 0, 9), -1.0, V(l, "mun", 0, 9), ALU.mult, ALU.subtract)
                ts(DR("hw0", 0, 4), V(l, "w0", 0, 4), 0.5, None, ALU.mult)
                ts(DR("ha0", 0, 4), V(l, "a0", 0, 4), 0.5, None, ALU.mult)
                ts(DR("nkk", 0, 2), V(l, "kk", 0, 2), -1.0, None, ALU.mult)
                ts(DR("s1", 0, 2), V(l, "ka", 0, 2), 0.5, None, ALU.mult)
                ts(DR("s2", 0, 2), V(l, "ka", 0, 2), -0.5, 1.0, ALU.mult, ALU.add)
                ts(DR("hg", 0, 2), V(l, "cgg", 0, 2), 0.5, None, ALU.mult)
                ts(DR("hb", 0, 2), V(l, "cgb", 0, 2), 0.5, None, ALU.mult).then_inc(vector_step, step.up())
                dve.wait_ge(vector_step, step.n)
                ts(DR("c0", 0, 9), DR("c0", 0, 9), 1.0, None, ALU.add).then_inc(der_ready.sem, 1)

            def modulate(l, i, silu, junk, t, plus=0, used=0):
                unit = raw[:, i % RAW].rearrange("p k m -> p (k m)")
                dve.wait_ge(w_in[i % RAW], 16 * (i // RAW + 1) + plus)
                if ada_no[i]:
                    dve.wait_ge(ada_used, ada_no[i] + used)
                for s_ in range(2):
                    feature = mods_flat[:, bass.ds(2 * NT_MODS * l + 2 * t + s_, 1)]
                    k = stt(junk[:, s_, :], unit, 0.5, silu[:, s_, :], ALU.mult, ALU.mult, accum_out=feature)
                k.then_inc(ada_used, 1)

            def modulations(l, t0, t1, used):
                dve.wait_ge(ada_used, used)
                tt(mods[:, l, t0:t1, :], mods[:, l, t0:t1, :], bc(V(l, "ada_b", t0, t1 - t0), [P, t1 - t0, 2], 2), ALU.add)\
                    .then_inc(vector_step, step.up())
                dve.wait_ge(vector_step, step.n)

            def gains(l, name, scale, g):
                o = DR(name, 0, 16).rearrange("p (t s) -> p t s", s=2)
                stt(o, mods[:, l, 8 * scale:8 * scale + 8, :], 1.0, bc(V(l, g, 0, 8), [P, 8, 2], 2), ALU.add, ALU.mult)\
                    .then_inc(vector_step, step.up())
                dve.wait_ge(vector_step, step.n)

            def inverse(key, c0):
                dve.wait_ge(rms.sem, rms.at[key])
                dve.reciprocal(rinv[:, c0:], rinv[:, c0:]).then_inc(B.free(("norm", key)), 1)
                dve.wait_ge(B.free(("norm", key)), B.use(("norm", key)))

            def norm(key, c0, name, shift):
                l = key[0]
                for k in range(KT):
                    if k >= 2:
                        dve.wait_ge(act_lo.sem, act_lo.at[key, k - 2])
                    tt(tb[:, k % 2, c0:], x[:, k, c0:], rinv[:, c0:], ALU.mult).then_inc(vector_step, step.up())
                    dve.wait_ge(vector_step, step.n)
                    for s_, t0, tn in reversed(segs(c0)):
                        i = ts(hb[:, k % 2, t0:t0 + tn], tb[:, k % 2, t0:t0 + tn], DR(name, 2 * k + s_),
                               mods[:, l, 8 * shift + k, s_:s_ + 1], ALU.mult, ALU.add)
                    i.then_inc(mod_ready.sem, 1)

            def add_gated(l, src, m, gate, c0, key):
                for s_, t0, tn in reversed(segs(c0)):
                    i = stt(x[:, m, t0:t0 + tn], src[:, PSC + t0:PSC + t0 + tn], mods[:, l, 8 * gate + m, s_:s_ + 1],
                            x[:, m, t0:t0 + tn], ALU.mult, ALU.add)
                i.then_inc(A.free(key), 1)

            def masked_copy(o, mask, src):
                return dve.copy_predicated(o, mask.bitcast(U32).unsqueeze(1).to_broadcast(list(o.shape)), src)

            turned = []
            mods_flat = mods[:, :, :, :].rearrange("p l t s -> p (l t s)")
            dve.wait_ge(c_in, 48)
            dve.wait_ge(cond_th, 1)
            stt(rows[:, :, :], rows_tmp[:, :, :], 1.0, rows[:, :, :], ALU.add, ALU.mult).then_inc(cond_ready, 1)
            dve.wait_ge(cond_ready, 1)
            for l in ls:
                c0 = first(l)
                derive(l)
                if l == 0:
                    for t in range(16):
                        modulate(0, t, rows, rows_tmp, t)
                        if t == 11:
                            inverse((0, 1), 0)
                    modulations(0, 0, 16, 16)
                gains(l, "A1", 1, "n1")
                if l:
                    inverse((l, 1), 0)
                norm((l, 1), 0, "A1", 0)
                if l == 1:
                    dve.wait_ge(x_kept, 16)
                nz, feature, at = 0, 16, 16
                for n_, (name, i) in enumerate(u[0] for u in IN_UNITS):
                    key = (l, name, i)
                    at += 1
                    for _ in range(IN_ADA[n_] if l == 0 else 0):
                        modulate(0, at, rows, psB, feature)
                        at, feature = at + 1, feature + 1
                    if name == "z":
                        dve.wait_ge(A.free(key), A.use(key))
                        z, p = z_of(i), wa[:, nz % 2, :]
                        for o, s_, t in ((1, 0, CTX - 1), (CTX + 1, CTX, LAT - 1)):
                            k = stt(z[:, o:o + t], p[:, s_:s_ + t], V(l, "mup", i), z[:, o:o + t], ALU.mult, ALU.add)
                        k.then_inc(vector_step, step.up())
                        nz += 1
                        dve.wait_ge(vector_step, step.n)
                        for o, s_, t in ((0, 1, CTX - 1), (CTX, CTX + 1, LAT - 1)):
                            k = stt(z[:, o:o + t], p[:, s_:s_ + t], V(l, "mun", i), z[:, o:o + t], ALU.mult, ALU.add)
                        k.then_inc(z_mixed.sem, 1)
                    elif name == "cg":
                        dve.wait_ge(A.free(key), A.use(key))
                        ts(wb[:, i, c0:], wb[:, i, c0:], 0.5, 0.5, ALU.mult, ALU.add).then_inc(vector_step, step.up())
                    elif name == "cv":
                        dve.wait_ge(A.full(key), A.use(key))
                        src = A.slot(key)
                        if i == 0:
                            dve.wait_ge(pads.sem, pads.at[(l,)])
                            dve.wait_ge(vector_step, step.n)
                        if l == 0:
                            tt(u_sb[:, i, 15:15 + CTX], src[:, PSC:PSC + CTX], wb[:, i, 0:CTX], ALU.mult)
                        tt(u_sb[:, i, UL:UL + LAT], src[:, PSC + CTX:], wb[:, i, CTX:], ALU.mult)\
                            .then_inc(A.free(key), 1)
                    if (name, i) == IN_UNITS[5][0]:
                        dve.wait_ge(A.free((l, "qstat")), A.use((l, "qstat")))
                        dve.reciprocal(lrin[:, c0:], lrin[:, c0:]).then_inc(vector_step, step.up())
                        dve.wait_ge(vector_step, step.n)
                        for i in range(2):
                            k = stt(q_sb[:, i, c0:], q_sb[:, i, c0:], V(l, "qn", i), lrin[:, c0:], ALU.mult, ALU.mult)
                        k.then_inc(lr_normed.sem, 1)
                    elif (name, i) == IN_UNITS[7][0]:
                        dve.wait_ge(A.free((l, "kvstat")), A.use((l, "kvstat")))
                        dve.reciprocal(ltmp[:, :], ltmp[:, :]).then_inc(vector_step, step.up())
                        dve.wait_ge(vector_step, step.n)
                        stt(ckv[:, :], ckv[:, :], V(l, "kvn"), ltmp[:, :], ALU.mult, ALU.mult)\
                            .then_inc(lr_normed.sem, 1)
                if l == 0:
                    modulations(0, 16, 48, 48)

                dve.wait_ge(mix_in, 48 * (l + 1))

                def rotate(key, o, signal, skey):
                    dve.wait_ge(B.full(key), B.use(key))
                    src = B.slot(key)
                    if turned:
                        dve.wait_ge(turned[-1][0].sem, turned[-1][0].at[turned[-1][1]])
                    turned.append((signal, skey))
                    tt(rtmp[rp, :], src[rp, PSC + CTX:], cs[rp, 1, :], ALU.mult).then_inc(B.free(key), 1)
                    tt(o, o, cs[rp, 0, :], ALU.mult).then_inc(vector_step, step.up())
                    dve.wait_ge(vector_step, step.n)
                    dve.wait_ge(B.free(key), B.use(key))
                    tt(o, o, rtmp[rp, :], ALU.add).then_inc(signal.sem, 1)

                rotate((l, "krot"), krope[rp, CTX:], kr_ready, (l,))

                span0, width = (0, CTX + 15 + LAT) if l == 0 else (UL - 15, LAT)
                ctap = u_acc
                taps = [(t, i) for t in range(TAPS) for i in range(2)]
                done_taps = [0]
                marks = {}

                def tap(count):
                    for _ in range(count):
                        if done_taps[0] >= len(taps):
                            return
                        t, i = taps[done_taps[0]]
                        done_taps[0] += 1
                        w = V(l, "dw", 2 * t + i)
                        u = u_sb[:, i, span0 + t:span0 + t + width]
                        o = ctap[:, i, 0:width]
                        if t == 0:
                            if i == 0:
                                dve.wait_ge(A.free((l, "cv", 0)), A.use((l, "cv", 0)))
                                dve.wait_ge(A.free((l, "cv", 1)), A.use((l, "cv", 1)))
                            k = ts(o, u, w, V(l, "db", i), ALU.mult, ALU.add)
                        else:
                            dve.wait_ge(vector_step, marks[i])
                            k = stt(o, u, w, o, ALU.mult, ALU.add)
                        k.then_inc(vector_step, step.up())
                        marks[i] = step.n

                def head_rotation(h):
                    dve.wait_ge(A.free((l, "qh", h)), A.use((l, "qh", h)))
                    rotate((l, "qrot", h), qT[rp, h % 2, CTX:], q_rot, (l, h))

                def maxima(i):
                    e = PSC + (CTX if au[l][i][1] < CTX // P else TOK)
                    dve.wait_ge(A.full((l, "s", i)), A.use((l, "s", i)))
                    src = A.slot((l, "s", i))
                    dve.tensor_reduce(stat[:, 0, i:i + 1], src[:, PSC:e], AX_X, ALU.max, negate=True)\
                        .then_inc(vector_step, step.up())
                    dve.wait_ge(vector_step, step.n)
                    ts(stat[:, 1, i:i + 1], stat[:, 0, i:i + 1], SCALE, None, ALU.mult).then_inc(rowmax.sem, 1)

                def mixed(i):
                    h, q = au[l][i]
                    dve.wait_ge(A.free((l, "s", i)), A.use((l, "s", i)))
                    dve.reciprocal(stat[:, 3, i:i + 1], stat[:, 2, i:i + 1]).then_inc(vector_step, step.up())
                    dve.wait_ge(vector_step, step.n)
                    dve.wait_ge(B.full((l, "o", i)), B.use((l, "o", i)))
                    src = B.slot((l, "o", i))
                    ts(otok[:, q, HD * h:HD * (h + 1)], src[:, 0:HD], stat[:, 3, i:i + 1], None, ALU.mult)\
                        .then_inc(B.free((l, "o", i)), 1)

                def low_part(k, key, ykey, scale=None):
                    dve.wait_ge(y_hi.sem, y_hi.at[ykey])
                    src = psA[:, A.at[key] % 2, PSC + c0:]
                    if scale is None:
                        i = tt(L(k)[:, c0:], src, f32(H(k))[:, c0:], ALU.subtract)
                    else:
                        i = stt(L(k)[:, c0:], src, scale, f32(H(k))[:, c0:], ALU.mult, ALU.subtract)
                    i.then_inc(A.free(key), 1)

                def conv(n):
                    if n == 0:
                        dve.wait_ge(vector_step, step.n)
                        assert done_taps[0] == len(taps)
                    for i in range(2):
                        if n == 0:
                            if l == 0:
                                ts(acc[:, i, 0:CTX], ctap[:, i, 0:CTX], 1.0, None, ALU.mult)
                            o = CTX + 15 if l == 0 else 0
                            ts(acc[:, i, CTX:], ctap[:, i, o:o + LAT], 1.0, None, ALU.mult).then_inc(conv_sum.sem, 1)
                        elif n == 1:
                            dve.wait_ge(B.full((l, "cmean", i)), B.use((l, "cmean", i)))
                            src = B.slot((l, "cmean", i))
                            dve.wait_ge(conv_sum.sem, conv_sum.at[l, i])
                            stt(acc[:, i, c0:], src[:, PSC + c0:], -1.0 / 64, acc[:, i, c0:], ALU.mult, ALU.add)\
                                .then_inc(B.free((l, "cmean", i)), 1)
                        elif n == 3:
                            dve.wait_ge(conv_std.sem, conv_std.at[l, i])
                            dve.reciprocal(q_sb[:, i, c0:], q_sb[:, i, c0:]).then_inc(B.free((l, "cvar", i)), 1)
                            dve.wait_ge(B.free((l, "cvar", i)), B.use((l, "cvar", i)))
                            tt(acc[:, i, c0:], acc[:, i, c0:], q_sb[:, i, c0:], ALU.mult)\
                                .then_inc(vector_step, step.up())
                            dve.wait_ge(vector_step, step.n)
                            ts(acc[:, i, c0:], acc[:, i, c0:], DR("hg", i), DR("hb", i), ALU.mult, ALU.add)\
                                .then_inc(conv_pre.sem, 1)
                        elif n == 4:
                            dve.wait_ge(conv_th.sem, conv_th.at[l, i])
                            stt(acc[:, i, c0:], q_sb[:, i, c0:], 1.0, acc[:, i, c0:], ALU.add, ALU.mult)\
                                .then_inc(conv_act.sem, 1)
                        elif n == 5:
                            low_part(i, (l, "convp", i), (l, "conv", i))
                        elif n == 6:
                            low_part(4 + i, (l, "poolp", i), (l, "pool", i), V(l, "psc", i))

                head_rotation(0)
                per = -(-len(taps) // (len(au[l]) - 7))
                for i in range(len(au[l])):
                    h = au[l][i][0]
                    if (i == 0 or au[l][i - 1][0] != h) and h + 1 < HEADS:
                        head_rotation(h + 1)
                    maxima(i)
                    tap(per)
                    if i > 1:
                        mixed(i - 2)
                    conv(conv_step(l, i))
                mixed(len(au[l]) - 2)
                mixed(len(au[l]) - 1)

                for i in range(2):
                    low_part(6 + i, (l, "att", i), (l, "att", i))

                dve.wait_ge(rw_in, 32 * (l + 1))
                dve.wait_ge(g_th.sem, g_th.at[(l,)])
                ts(zt[:, 4, c0:], zt[:, 4, c0:], 0.5, 0.5, ALU.mult, ALU.add).then_inc(vector_step, step.up())
                for what, i, *rest in RW:
                    j, d, p = i // 2, i % 2, i % 2
                    un, n_ = (l, j, d), rest[0] if rest else 0
                    ba, bk = b45[:, p, 0, :], b45[:, p, 1, :]
                    tri = lambda incl: K("tri", C, (2 * d + incl) * C)
                    lo = lambda i_: K("lo" if d == 0 else "up", C, i_ * C)
                    up = lambda i_: K("up" if d == 0 else "lo", C, i_ * C)
                    m3 = lambda m: m.unsqueeze(1).to_broadcast([P, NC, C])
                    if what == "kk":
                        dve.wait_ge(kk_std.sem, kk_std.at[l, j])
                        ts(nkk[:, :], nkk[:, :], 1e-12, None, ALU.max).then_inc(A.free((l, "kk", j)), 1)
                        dve.wait_ge(A.free((l, "kk", j)), A.use((l, "kk", j)))
                        dve.reciprocal(nkk[:, :], nkk[:, :]).then_inc(vector_step, step.up())
                        dve.wait_ge(vector_step, step.n)
                        stt(nkk[:, :], zt[:, 2 + j, :], DR("nkk", j), nkk[:, :], ALU.mult, ALU.mult)\
                            .then_inc(vector_step, step.up())
                        dve.wait_ge(vector_step, step.n)
                    elif what == "decay":
                        dve.wait_ge(A.free((un, "w2")), A.use((un, "w2")))
                        ts(wlog[:, 0, :], wlog[:, 0, :], 1.0, None, ALU.add).then_inc(vector_step, step.up())
                        dve.wait_ge(vector_step, step.n)
                        way = slice(None) if d == 0 else slice(None, None, -1)
                        dve.tensor_tensor_scan(wlog[:, 1, way], reset[:, :], wlog[:, 0, way], 0.0, ALU.mult, ALU.add)\
                            .then_inc(cum.sem, 1)
                    elif what == "prep" and n_ == 1:
                        dve.wait_ge(cum.sem, cum.at[un])
                        tt(b[:, 0, :], wlog[:, 1, :], wlog[:, 0, :], ALU.subtract).then_inc(dk.sem, 1)
                    elif what == "prep" and n_ == 2:
                        dve.wait_ge(rate_key.sem, rate_key.at[un])
                        tt(bk, bk, zt[:, 2 + j, :], ALU.mult).then_inc(kd_ready.sem, 1)
                        stt(ba, ba, 1.0, nkk[:, :], ALU.add, ALU.mult).then_inc(vector_step, step.up())
                        rate = step.n
                    elif what == "prep" and n_ == 3:
                        dve.wait_ge(vector_step, rate)
                        dve.wait_ge(exps.sem, exps.at[un, 1])
                        for part, s_ in HALF:
                            stt(BK[part, :, s_, :], chunks(ba[part]), -0.5, chunks(b3[part, p, :]), ALU.mult, ALU.mult)
                    elif what == "prep" and n_ == 4:
                        dve.wait_ge(kd_ready.sem, kd_ready.at[un])
                        if d == 0:
                            ts(kds[:, j, :], bk, 1.0, None, ALU.mult)
                        else:
                            tt(kds[:, j, :], kds[:, j, :], bk, ALU.add)
                        for part, s_ in HALF:
                            tt(Q[part, p, 2 * s_ + 1, :], zt[part, j, :], b[part, 1, :], ALU.mult)
                    elif what == "prep" and n_ == 5:
                        ts(PC[:, p, :], chunks(b[:, 1, :])[:, :, C - 1 if d == 0 else 0], 1.0, None, ALU.mult)
                        dve.wait_ge(exps.sem, exps.at[un, 2])
                        for part, s_ in HALF:
                            k = tt(Q[part, p, 2 * s_, :], nkk[part, :], b[part, 0, :], ALU.mult)
                        k.then_inc(prep.sem, 1)
                    elif what == "v":
                        for w, (m0, m1) in enumerate(((0, 7), (7, 13))):
                            dve.wait_ge(v_tp.sem, v_tp.at[l, i, w])
                            src = A.slot((l, i, "v", w)).rearrange("p (m n) -> p m n", n=P)
                            e = min(m1, NC)
                            ts(SV[64:, m0:e, 0:HD], src[64:, 0:e - m0, 0:HD], 1.0, None, ALU.mult)
                            s_ = max(m0, 1)
                            ts(SV[0:64, s_ - 1:m1 - 1, HD:], src[0:64, s_ - m0:m1 - m0, HD:], 1.0, None, ALU.mult)\
                                .then_inc(A.free((l, i, "v", w)), 1)
                    elif what == "gram":
                        g = n_
                        if g == 0:
                            dve.wait_ge(prep.sem, prep.at[un])
                        dve.wait_ge(A.full((un, "gram", g)), A.use((un, "gram", g)))
                        src = A.slot((un, "gram", g)).rearrange("p (h c n) -> p h c n", h=2, n=P)
                        tt(M[:, p, :, 4 * g:4 * g + 4, :], src[:, :, :, C:],
                           bc(tri(1), [P, 1, C], 1).unsqueeze(1).to_broadcast([P, 2, 4, C]), ALU.mult)
                        for part, s_ in HALF:
                            other = HALF[1 - s_][0]
                            mask = lambda p_: tri(0)[p_].unsqueeze(1).to_broadcast([64, 4, C])
                            tt(chunks(Q[other, p, 2 * s_, :])[:, 4 * g:4 * g + 4, :], src[other, s_, :, 0:C], mask(other),
                               ALU.mult)
                            k = tt(LT[part, 4 * g:4 * g + 4, :], src[part, s_, :, 0:C], mask(part), ALU.mult)
                        k.then_inc(A.free((un, "gram", g)), 1)
                    elif what == "t" and n_ == 0:
                        dve.wait_ge(A.free((un, "gram", 2)), A.use((un, "gram", 2)))
                        tt(XT[:, p], LT[:, :, :], m3(up(0)), ALU.mult).then_inc(vector_step, step.up())
                        dve.wait_ge(vector_step, step.n)
                        tt(XT[:, p], XT[:, p], m3(K("istack", C)), ALU.add).then_inc(xt_one.sem, 1)
                        dve.wait_ge(A.full((un, "t", 0)), A.use((un, "t", 0)))
                        src = chunks(A.slot((un, "t", 0))[:, PSC:])
                        tt(X[:, :, :], src, m3(lo(0)), ALU.mult).then_inc(A.free((un, "t", 0)), 1)
                        dve.wait_ge(A.free((un, "t", 0)), A.use((un, "t", 0)))
                        tt(X[:, :, :], X[:, :, :], m3(K("istack", C)), ALU.add).then_inc(x_one.sem, 1)
                    elif what == "x":
                        dve.wait_ge(A.full((un, "x", n_)), A.use((un, "x", n_)))
                        src = chunks(A.slot((un, "x", n_))[:, PSC:])
                        masked_copy(X[:, :, :], lo(n_), src).then_inc(A.free((un, "x", n_)), 1)
                    elif what == "xt":
                        dve.wait_ge(A.full((un, "xt", n_)), A.use((un, "xt", n_)))
                        src = chunks(A.slot((un, "xt", n_))[:, PSC:])
                        masked_copy(XT[:, p], up(n_), src).then_inc(A.free((un, "xt", n_)), 1)
                    elif what == "w":
                        dve.wait_ge(scan_full.sem, scan_full.at[un, "w", n_])
                        ts(Wc[:, n_ % 2, :], scan_w, 1.0, None, ALU.mult).then_inc(scan_read.sem, 1)
                    elif what == "u":
                        dve.wait_ge(scan_full.sem, scan_full.at[un, "u", n_])
                        for part, s_ in HALF:
                            k = ts(UV[part, chunk_order(d)[n_], HD * s_:HD * (s_ + 1)], scan_u[part], 1.0, None, ALU.mult)
                        k.then_inc(scan_read.sem, 1)
                    elif what == "s" and n_ < NC - 1:
                        c, after = chunk_order(d)[n_:n_ + 2]
                        dve.wait_ge(scan_full.sem, scan_full.at[un, "s", n_])
                        dve.wait_ge(s_dec.sem, s_dec.at[un, n_])
                        for part, s_ in HALF:
                            k = stt(SV[part, after, HD * s_:HD * (s_ + 1)], scan_s[part], PC[part, p, c:c + 1],
                                    SP[part, :], ALU.mult, ALU.add)
                        k.then_inc(scan_read.sem, 1)
                    elif what == "s":
                        dve.wait_ge(y_full.sem, y_full.at[un])
                        src = psB[:, 0, PSC + c0:]
                        if d == 0:
                            if j:
                                dve.wait_ge(y_lo.sem, y_lo.at[l, 0])
                            ts(Y[:, c0:], src, 1.0, None, ALU.mult).then_inc(y_read.sem, 1)
                        else:
                            tt(Y[:, c0:], src, Y[:, c0:], ALU.add).then_inc(y_read.sem, 1)
                    elif what == "post" and n_ == 0:
                        stt(fin[:, 0, c0:], zt[:, i, c0:], V(l, "rk", i), kds[:, i, c0:], ALU.mult, ALU.mult)\
                            .then_inc(bon.sem, 1)
                        dve.wait_ge(A.full((l, i, "mean")), A.use((l, i, "mean")))
                        src = A.slot((l, i, "mean"))
                        dve.wait_ge(y_read.sem, y_read.at[l, i, 1])
                        stt(Y[:, c0:], src[:, PSC + c0:], -1.0 / 64, Y[:, c0:], ALU.mult, ALU.add)\
                            .then_inc(A.free((l, i, "mean")), 1)
                    elif what == "post" and n_ == 1:
                        dve.wait_ge(A.full((l, i, "bonus")), A.use((l, i, "bonus")))
                        src = A.slot((l, i, "bonus"))
                        tt(fin[:, 0, c0:], src[:, PSC + c0:], zv[:, i, C + c0:C + TOK], ALU.mult)\
                            .then_inc(A.free((l, i, "bonus")), 1)
                    elif what == "post" and n_ == 2:
                        dve.wait_ge(rw_std.sem, rw_std.at[l, i])
                        dve.reciprocal(fin[:, 1, c0:], fin[:, 1, c0:]).then_inc(A.free((l, i, "var")), 1)
                    elif what == "post" and n_ == 3:
                        dve.wait_ge(A.free((l, i, "var")), A.use((l, i, "var")))
                        tt(Y[:, c0:], Y[:, c0:], fin[:, 1, c0:], ALU.mult).then_inc(vector_step, step.up())
                        dve.wait_ge(vector_step, step.n)
                        ts(Y[:, c0:], Y[:, c0:], V(l, "lg", i), V(l, "lb", i), ALU.mult, ALU.add)\
                            .then_inc(vector_step, step.up())
                        dve.wait_ge(vector_step, step.n)
                        tt(Y[:, c0:], Y[:, c0:], fin[:, 0, c0:], ALU.add).then_inc(vector_step, step.up())
                        dve.wait_ge(vector_step, step.n)
                        dve.wait_ge(A.full((l, i, "gate")), A.use((l, i, "gate")))
                        src = A.slot((l, i, "gate"))
                        tt(Y[:, c0:], src[:, PSC + c0:], Y[:, c0:], ALU.mult).then_inc(A.free((l, i, "gate")), 1)
                dve.wait_ge(x_in, 16 * (l + 2))
                for m in range(KT):
                    key = (l, "out", m)
                    dve.wait_ge(A.full(key), A.use(key))
                    add_gated(l, A.slot(key), m, 2, c0, key)
                gains(l, "A2", 4, "n2")
                inverse((l, 2), c0)
                norm((l, 2), c0, "A2", 3)
                if l == 0:
                    dve.wait_ge(rows_in, 16)

                def group(g0, g):
                    i, t = mlp0[l] + LOOP[l] * g0, 0
                    for j in range(UPG):
                        i += 1
                        for _ in range(ada_after(l, j)):
                            modulate(1, i, rows2, psB, t + 12 * g0 + 12 * g, 16 * (LOOP[l] // RAW) * g, 12 * g)
                            i, t = i + 1, t + 1
                        key = (l, "mlp", g0, j)
                        dve.wait_ge(A.full(key), A.use(key) + 8 * g)
                        src = A.slot(key)
                        done = 8 * (l * GROUPS + g0) + j + 1
                        if j < 8:
                            dve.wait_ge(relu_ready, done + 8 * g)
                            stt(hsq[:, j % 2, c0:], src[:, PSC + c0:], 0.0, relu[:, j % 2, c0:], ALU.max, ALU.mult)\
                                .then_inc(A.free(key), 1)
                            dve.wait_ge(hid_hi_ready, done + 8 * g)
                            tt(hid_lo[:, j, c0:], hsq[:, j % 2, c0:], f32(hid_hi[:, j, c0:]), ALU.subtract)\
                                .then_inc(hid_ready, 1)
                        else:
                            add_gated(l, src, j - 8, 5, c0, key)

                with dve.Fori(0, GROUPS - 1) as g:
                    group(0, g)
                group(GROUPS - 1, 0)
                if l == 0:
                    modulations(1, 0, NT_MODS, 2 * NT_MODS)
            key = (DEPTH, 0)
            inverse(key, CTX)
            for k in range(KT):
                stt(x[:, k, CTX:], x[:, k, CTX:], vec[:, V_FINAL + k:V_FINAL + k + 1], rinv[:, CTX:],
                                   ALU.mult, ALU.mult).then_inc(fin_ready.sem, 1)

        @block.gpsimd
        def _(pool):
            step = Steps()

            def split_lo(n, plus=0):
                i = unit_of_split[n]
                pool.wait_ge(w_hi, n + 1 + plus)
                pool.tensor_tensor(wlo[:, n % SPL], raw[:, i % RAW], f32(whi[:, n % SPL]), ALU.subtract)\
                    .then_inc(w_lo, 1)

            def operand_lo(key, c0):
                for k in range(KT):
                    pool.wait_ge(act_hi.sem, act_hi.at[key, k])
                    pool.tensor_tensor(L(k)[:, c0:], hb[:, k % 2, c0:], f32(H(k))[:, c0:], ALU.subtract)\
                        .then_inc(act_lo.sem, 1)

            def add_squares(key, k, c0):
                pool.wait_ge(sq_ready.sem, sq_ready.at[key, k])
                if k > 1:
                    pool.wait_ge(sq_added.sem, sq_added.at[key, k - 1])
                pool.tensor_tensor(sq_sum[:, c0:], sq_sum[:, c0:], sq[:, k % 2, c0:], ALU.add).then_inc(sq_added.sem, 1)

            n = 0
            for k in range(1, KT):
                add_squares((0, 1), k, 0)
            split_lo(0)
            split_lo(1)
            for l in ls:
                c0 = first(l)
                operand_lo((l, 1), 0)
                pool.wait_ge(act_lo.sem, act_lo.at[(l, 1), KT - 1])
                if l == 1:
                    pool.wait_ge(x_kept, 16)
                pool.memset(u_sb[:, :, :], 0.0)
                pool.memset(zv[:, :, :], 0.0)
                pool.memset(pp[:, :, :], 0.0).then_inc(pads.sem, 1)
                for i in range(N_IN):
                    split_lo(n + SPL)
                    n += 1
                def key_operand(h):
                    if h >= 2:
                        last = (l, "s", max(i for i, (h_, _) in enumerate(au[l]) if h_ == h - 2))
                        pool.wait_ge(A.full(last), A.use(last))
                    pool.tensor_copy(kT[rp, h % 2, :], krope[rp, :]).then_inc(k_full.sem, 1)

                pool.wait_ge(kr_ready.sem, kr_ready.at[(l,)])
                pool.wait_ge(w_lo, n + SPL)
                key_operand(0)
                key_operand(1)
                pool.wait_ge(k_full.sem, k_full.at[l, 1])
                pool.wait_ge(pads.sem, pads.at[(l,)])
                pool.wait_ge(mix_in, 48 * (l + 1))
                pool.wait_ge(ada_used, NT_MODS)
                for i in range(2):
                    pool.wait_ge(A.free((l, "pool", i)), A.use((l, "pool", i)))
                for i in range(2):
                    cur, buf = pp[:, i, :], ps[:, i, :]
                    pool.tensor_tensor(buf[:, 1:PWID], cur[:, 0:PWID - 1], cur[:, 1:PWID], ALU.add)\
                        .then_inc(pool_step, step.up())
                    widths = ((2, 4), (8, 16))[i]
                    w, src, dst = 2, buf, ptmp[:, :]
                    for part, want in ((slice(0, 64), widths[0]), (slice(64, P), widths[1])):
                        while w < want:
                            h = w // 2
                            pool.wait_ge(pool_step, step.n)
                            pool.tensor_tensor(dst[:, w:PWID - w], src[:, w - h:PWID - w - h], src[:, w + h:PWID - w + h],
                                                    ALU.add).then_inc(pool_step, step.up())
                            src, dst, w = dst, src, 2 * w
                        pool.wait_ge(pool_step, step.n)
                        for s_, t0, tn in segs(c0):
                            o = PL if s_ == 0 else 8
                            pool.tensor_tensor(rcnt[part, i, t0:t0 + tn], src[part, o:o + tn], rcnt[part, i, t0:t0 + tn],
                                                    ALU.mult).then_inc(pool_step, step.up())
                    pool.wait_ge(pool_step, step.n)
                    for s_, t0, tn in segs(c0):
                        o = PL if s_ == 0 else 8
                        k = pool.tensor_tensor(rcnt[:, i, t0:t0 + tn], rcnt[:, i, t0:t0 + tn], cur[:, o:o + tn], ALU.subtract)
                    k.then_inc(pool_d.sem, 1)
                    pool.wait_ge(pool_d.sem, pool_d.at[l, i])
                key_operand(2)
                key_operand(3)
                pool.wait_ge(A.free((l, "att", 1)), A.use((l, "att", 1)))
                pool.wait_ge(k_full.sem, k_full.at[l, HEADS - 1])
                for p in range(2):
                    pool.memset(Q[64:, p, 1, :], 0.0)
                    k = pool.memset(Q[0:64, p, 3, :], 0.0)
                k.then_inc(rw_zero.sem, 1)
                for what, i, *rest in RW:
                    j, d, p = i // 2, i % 2, i % 2
                    un, n_, order = (l, j, d), rest[0] if rest else 0, chunk_order(d)
                    if what == "prep" and n_ == 3:
                        pool.wait_ge(kd_ready.sem, kd_ready.at[un])
                        pool.wait_ge(exps.sem, exps.at[un, 1])
                        for part, s_ in HALF:
                            k = pool.tensor_tensor(BK[part, :, 1 - s_, :], chunks(b45[part, p, 1, :]),
                                                   chunks(b3[part, p, :]), ALU.mult)
                        k.then_inc(pool_k.sem, 1)
                    elif what == "w" and n_ < NC - 1:
                        if n_ == 0:
                            if i:
                                pool.wait_ge(y_full.sem, y_full.at[un] - 1)
                            else:
                                pool.wait_ge(rw_zero.sem, rw_zero.at[(l,)])
                            pool.memset(SV[0:64, order[0], 0:HD], 0.0)
                            pool.memset(SV[64:, order[0], HD:], 0.0).then_inc(s_zero.sem, 1)
                            pool.wait_ge(prep.sem, prep.at[un])
                            pool.wait_ge(s_zero.sem, s_zero.at[un])
                        else:
                            pool.wait_ge(scan_read.sem, scan_read.at[un, "s", n_ - 1])
                        for part, s_ in HALF:
                            k = pool.tensor_scalar(SP[part, :], SV[part, order[n_], HD * s_:HD * (s_ + 1)],
                                                   PC[part, p, order[n_]:order[n_] + 1], 0.0, ALU.mult, ALU.add)
                        k.then_inc(s_dec.sem, 1)
                        decayed = (un, n_)
                    elif what == "post" and n_ == 3:
                        pool.wait_ge(s_dec.sem, s_dec.at[decayed])
                        pool.wait_ge(y_hi.sem, y_hi.at[l, "rw", i])
                        pool.tensor_tensor(L(2 + i)[:, c0:], Y[:, c0:], f32(H(2 + i))[:, c0:], ALU.subtract)\
                            .then_inc(y_lo.sem, 1)
                        pool.wait_ge(y_lo.sem, y_lo.at[l, i])
                for m in range(KT):
                    split_lo(n + SPL)
                    n += 1
                    if m > 1:
                        add_squares((l, 2), m - 1, c0)
                add_squares((l, 2), KT - 1, c0)
                operand_lo((l, 2), c0)

                def group(g0, g, end=False):
                    for j in range(UPG):
                        if not (end and l and j >= UPG - SPL):
                            split_lo(n + UPG * g0 + j + SPL, UPG * g)
                        if end and j > 9:
                            add_squares(next_norm[l], j - 9, 0 if l == 0 else CTX)

                with pool.Fori(0, GROUPS - 1) as g:
                    group(0, g)
                group(GROUPS - 1, 0, True)
                add_squares(next_norm[l], KT - 1, 0 if l == 0 else CTX)
                n += UPG * GROUPS

        @block.sync
        def _(sp):
            def load(i, plus_lo=0, plus_ada=0, at=None):
                if i >= RAW:
                    before = i - RAW
                    if before in split_no:
                        sp.wait_ge(w_lo, split_no[before] + 1 + plus_lo)
                    else:
                        sp.wait_ge(ada_used, ada_no[before] + 1 + plus_ada)
                src = stream[i] if at is None else stream[bass.ds(at, 1)].rearrange("a p n -> (a p) n")
                sp.dma_start(raw[:, i % RAW], src.rearrange("p (k m) -> p k m", k=KT)).then_inc(w_in[i % RAW], 16)

            sp.dma_start(rows[:, :, :].rearrange("p s n -> p (s n)"), cond_in.to_broadcast([P, 2 * D]))\
                .then_inc(c_in, 16)
            sp.dma_start(cst[:, :], consts).then_inc(c_in, 16)
            sp.dma_start(vec[:, :], vecs).then_inc(c_in, 16)
            for i in range(RAW):
                load(i)
            sp.dma_start(x[:, :, :], xT).then_inc(x_in, 16)
            sp.wait_ge(cond_ready, 1)
            sp.dma_start(kept_rows, rows[0:1, :, :].rearrange("p s n -> p (s n)")).then_inc(rows_kept, 16)
            n = RAW
            for l in ls:
                first_in = 16 if l == 0 else mlp0[0] + LOOP[0] * GROUPS
                while n < first_in + RAW + 1:
                    load(n)
                    n += 1
                if l == 1:
                    for j in (14, 15):
                        key = (0, "mlp", GROUPS - 1, j)
                        sp.wait_ge(A.free(key), A.use(key))
                    sp.dma_start(kept, x[:, :, CTX:]).then_inc(x_kept, 16)
                sp.wait_ge(act_lo.sem, act_lo.at[(l, 1), KT - 1])
                if l == 1:
                    sp.wait_ge(x_kept, 16)
                sp.dma_start(cs[:, :, :], big[:, BIG["cos"]:BIG["cos"] + 2 * LAT].rearrange("p (a n) -> p a n", a=2))\
                    .then_inc(mix_in, 16)
                sp.dma_start(rcnt[:, :, :], big[:, BIG["rcnt"]:].rearrange("p (a n) -> p a n", a=2))\
                    .then_inc(mix_in, 16)
                sp.dma_start(sw_a[:, :], small_a[l]).then_inc(mix_in, 16)
                while n < mlp0[l] - 8 + RAW:
                    load(n)
                    n += 1
                sp.wait_ge(A.free((l, "att", 1)), A.use((l, "att", 1)))
                sp.dma_start(reset[:, :], big[:, 0:TOK]).then_inc(rw_in, 16)
                sp.dma_start(sw_r[:, :], small_r[l]).then_inc(rw_in, 16)
                sp.wait_ge(y_lo.sem, y_lo.at[l, 1])
                if l == 0:
                    sp.dma_start(x[:, :, :], xT).then_inc(x_in, 16)
                else:
                    sp.dma_start(x[:, :, CTX:], kept).then_inc(x_in, 16)
                while n < mlp0[l]:
                    load(n)
                    n += 1
                per = LOOP[l]
                with sp.Fori(0, GROUPS) as g:
                    for i in range(per):
                        load(mlp0[l] + i, UPG * g, 12 * g, mlp0[l] + i + per * g)
                n = mlp0[l] + per * GROUPS
            for k in range(KT):
                sp.wait_ge(fin_ready.sem, fin_ready.at[(k,)])
                sp.dma_start(out[:, k, :], x[:, k, CTX:]).then_inc(out_done, 16)
            sp.wait_ge(out_done, 16 * KT)


def _tables():
    c = np.zeros((P, CST["end"]), np.float32)
    r, q = np.arange(P)[:, None], np.arange(P)[None, :]
    c[:, CST["ident"]:][:, :P] = r == q
    c[:, CST["ones"]:][:, :P] = 1
    c[:, CST["bones"]:][:, :P] = r // 64 == q // 64
    r, q = r % 64, np.arange(64)[None, :]
    for i in range(6):
        h = 1 << i
        lo = (r // (2 * h) == q // (2 * h)) & (r // h % 2 == 1) & (q // h % 2 == 0)
        up = (r // (2 * h) == q // (2 * h)) & (r // h % 2 == 0) & (q // h % 2 == 1)
        c[:, CST["lo"] + 64 * i:][:, :64] = lo
        c[:, CST["up"] + 64 * i:][:, :64] = up
    for i, m in enumerate((r < q, r <= q, r > q, r >= q)):
        c[:, CST["tri"] + 64 * i:][:, :64] = m
    c[:, CST["istack"]:][:, :64] = r == q
    for a in (0, 16):
        for m in range(8):
            c[NOPE + a + 8 + m, CST["rot"] + a + m] = -1
            c[NOPE + a + m, CST["rot"] + a + 8 + m] = 1
    g = np.zeros((P, BIG["end"]), np.float32)
    t = np.arange(TOK)
    g[:, BIG["reset"]:][:, :TOK] = t % C != 0
    nf = ROPE // 4
    freq = (10000.0 ** (-np.arange(nf, dtype=np.float32) / nf)).astype(np.float32)
    for row in range(ROPE):
        pos = (np.arange(LAT) // 64 if row < 16 else np.arange(LAT) % 64).astype(np.float32)
        ang = pos * freq[row % 8]
        g[NOPE + row, BIG["cos"]:][:LAT] = np.cos(ang)
        g[NOPE + row, BIG["sin"]:][:LAT] = np.sin(ang)
    for i, w in enumerate((2, 4, 8, 16)):
        for t0, n in ((0, CTX), (CTX, LAT)):
            s = np.arange(n)
            cnt = np.clip(s + w - w // 2, 0, n) - np.clip(s - w // 2, 0, n)
            g[64 * (i % 2):64 * (i % 2) + 64, BIG["rcnt"] + TOK * (i // 2) + t0:][:, :n] = 1.0 / cnt.astype(np.float32)
    return c, g


def _layout(a):
    cols = lambda v: np.asarray(v).reshape(-1, P).T
    tile = lambda w: w.reshape(KT, P, P).transpose(1, 0, 2).reshape(P, KT * P)
    ada = lambda l, t: a["ada_w"][l][:, P * t:P * (t + 1)].T

    def projection(l, i):
        (name, _), c = IN_UNITS[i]
        if name != "rope":
            return tile(a["w_in"][l][:, c:c + P])
        w = np.zeros((D, P), a["w_in"].dtype)
        w[:, NOPE:QD] = a["w_in"][l][:, c:c + ROPE]
        return tile(w)

    def mlp(l, g, j):
        if j < 8:
            return tile(a["mlp_w1"][l][:, D * g + P * j:][:, :P])
        return tile(a["mlp_w2"][l][D * g:D * (g + 1), P * (j - 8):P * (j - 7)])

    units, t0, t1 = [ada(0, t) for t in range(16)], 16, 0
    for l in range(DEPTH):
        for i in range(N_IN):
            units.append(projection(l, i))
            for _ in range(IN_ADA[i] if l == 0 else 0):
                units.append(ada(0, t0))
                t0 += 1
        units += [tile(a["w_out"][l][:, P * m:P * (m + 1)]) for m in range(KT)]
        for g in range(GROUPS):
            for j in range(UPG):
                units.append(mlp(l, g, j))
                for _ in range(ADA_AFTER.get(j, 0) if l == 0 else 0):
                    units.append(ada(1, t1))
                    t1 += 1
    stream = np.stack(units)
    vecs = []
    for l in range(DEPTH):
        for name in ("ada_b", "norm1_g", "norm2_g", "conv_dw", "conv_db", "conv_gn_g", "conv_gn_b", "pool_scale",
                     "rw_mu_prev", "rw_mu_next", "rw_w0", "rw_a0", "rw_kk", "rw_ka", "rw_rk", "rw_lnx_g", "rw_lnx_b",
                     "mla_qn_g", "mla_kvn_g"):
            vecs.append(cols(a[name][l]))
    vecs.append(cols(a["final_g"]))
    vecs = np.concatenate(vecs, 1)
    cond = np.concatenate([a["c"][0], a["c_ctx"]])[None]
    rows = lambda w: w.reshape(-1, P, w.shape[-1]).transpose(1, 0, 2).reshape(P, -1)
    sa, sr = [], []
    for l in range(DEPTH):
        pw = np.zeros((P, 2, P), np.float32)
        for i in range(4):
            o = 64 * (i % 2)
            pw[o:o + 64, i // 2, o:o + 64] = a["pool_w"][l][i]
        sa.append(np.concatenate([rows(a["mla_wuq"][l]), a["mla_wukv"][l], rows(a["conv_pw"][l]), pw.reshape(P, -1)], 1))
        sr.append(np.concatenate([a["rw_w2"][l].reshape(P, GW), a["rw_a2"][l].reshape(P, GW), a["rw_g2"][l]], 1))
    xs = np.concatenate([a["ctx"][0], a["x"][0]], 0).T.reshape(KT, P, TOK).transpose(1, 0, 2)
    c, g = _tables()
    return {"xT": xs, "stream": stream, "vecs": vecs, "cond_in": cond, "consts": c, "big": g, "small_a": np.stack(sa),
            "small_r": np.stack(sr)}


def kernel(**inputs):
    import concourse.bacc as _bacc
    from concourse.bass_utils import run_bass_kernel_spmd as _run

    nc = _bacc.Bacc("TRN2", target_bir_lowering=False, num_devices=1)
    arrays = {k: np.ascontiguousarray(v) for k, v in _layout({k: np.asarray(v) for k, v in inputs.items()}).items()}
    args = {k: nc.dram_tensor(k, v.shape, mybir.dt.from_np(v.dtype), kind="ExternalInput").ap() for k, v in arrays.items()}
    kept = nc.dram_tensor("kept", (P, KT, LAT), F32, kind="Internal").ap()
    kept_rows = nc.dram_tensor("kept_rows", (1, 2 * D), F32, kind="Internal").ap()
    out = nc.dram_tensor("out_t", (P, KT, LAT), F32, kind="ExternalOutput").ap()
    trunk(nc, kept=kept, kept_rows=kept_rows, out=out, **args)
    r = _run(nc, [arrays], core_ids=[0])
    y = r.results[0]["out_t"]
    return y.transpose(2, 1, 0).reshape(1, LAT, D)
```
